# Optimizing a Trainium2 kernel written in Bass

```python
import math
import jax, jax.numpy as jnp
from jax import lax
import numpy as np

D_MODEL = 2048
BATCH = 1
SEQ = 256
DEPTH = 1

N_DIFF_HEADS = 8
DIFF_QK_DIM = 64
DIFF_V_DIM = 2 * DIFF_QK_DIM
N_DSA_HEADS = 8
DSA_HEAD_DIM = 128
N_IDX_HEADS = 16
IDX_DIM = 64
INDEX_TOPK = 256
D_FF = ((8 * D_MODEL // 3 + 255) // 256) * 256
ROPE_THETA = 500000.0
ROPE_FRACTION = 4
Q_BLOCK = 128
ADA_CHUNKS = 6
RMS_EPS = 1e-6

DIFF_Q = N_DIFF_HEADS * 2 * DIFF_QK_DIM
DIFF_K = N_DIFF_HEADS * 2 * DIFF_QK_DIM
DIFF_V = N_DIFF_HEADS * DIFF_V_DIM
DSA_Q = N_DSA_HEADS * DSA_HEAD_DIM
DSA_K = DSA_HEAD_DIM
DSA_V = DSA_HEAD_DIM
IDX_Q = N_IDX_HEADS * IDX_DIM
IDX_K = IDX_DIM
IDX_W = N_IDX_HEADS
PROJ_SIZES = (DIFF_Q, DIFF_K, DIFF_V, DSA_Q, DSA_K, DSA_V, IDX_Q, IDX_K, IDX_W)
PROJ_TOTAL = sum(PROJ_SIZES)
MIX_WIDTH = DIFF_V + N_DSA_HEADS * DSA_HEAD_DIM


def rms_norm(x, g):
    xf = x.astype(jnp.float32)
    y = xf * lax.rsqrt(jnp.mean(xf * xf, axis=-1, keepdims=True) + RMS_EPS)
    return (y * g.astype(jnp.float32)).astype(x.dtype)

def rope_tables(positions, rot_dim):
    inv_freq = ROPE_THETA ** (-(jnp.arange(0, rot_dim, 2, dtype=jnp.float32) / rot_dim))
    ang = positions.astype(jnp.float32)[..., None] * inv_freq
    return jnp.cos(ang), jnp.sin(ang)

def partial_rope(x, positions):
    d = x.shape[-1]
    rot = d // ROPE_FRACTION
    cos, sin = rope_tables(positions, rot)
    cos, sin = cos[:, :, None, :], sin[:, :, None, :]
    xr = x[..., :rot].astype(jnp.float32)
    x1, x2 = xr[..., : rot // 2], xr[..., rot // 2:]
    rotated = jnp.concatenate([x1 * cos - x2 * sin, x2 * cos + x1 * sin], axis=-1)
    return jnp.concatenate([rotated.astype(x.dtype), x[..., rot:]], axis=-1)

def differential_attention(q1, q2, k1, k2, v, lam):
    B, S, H, dq = q1.shape
    scale = dq ** -0.5
    key_pos = jnp.arange(S)

    def block(i):
        start = i * Q_BLOCK
        qb1 = lax.dynamic_slice_in_dim(q1, start, Q_BLOCK, axis=1)
        qb2 = lax.dynamic_slice_in_dim(q2, start, Q_BLOCK, axis=1)
        q_pos = start + jnp.arange(Q_BLOCK)
        mask = key_pos[None, :] <= q_pos[:, None]
        s1 = jnp.einsum('bqhd,bkhd->bhqk', qb1, k1).astype(jnp.float32) * scale
        s2 = jnp.einsum('bqhd,bkhd->bhqk', qb2, k2).astype(jnp.float32) * scale
        p1 = jax.nn.softmax(jnp.where(mask, s1, -jnp.inf), axis=-1)
        p2 = jax.nn.softmax(jnp.where(mask, s2, -jnp.inf), axis=-1)
        attn = p1 - lam * p2
        return jnp.einsum('bhqk,bkhd->bqhd', attn.astype(v.dtype), v)

    out = lax.map(block, jnp.arange(S // Q_BLOCK))
    return out.transpose(1, 0, 2, 3, 4).reshape(B, S, H, v.shape[-1])

def indexed_sparse_attention(q, k, v, iq, ik, iw, k_top):
    B, S, H, D = q.shape
    scale = D ** -0.5
    key_pos = jnp.arange(S)

    def block(i):
        start = i * Q_BLOCK
        qb = lax.dynamic_slice_in_dim(q, start, Q_BLOCK, axis=1)
        iqb = lax.dynamic_slice_in_dim(iq, start, Q_BLOCK, axis=1)
        iwb = lax.dynamic_slice_in_dim(iw, start, Q_BLOCK, axis=1)
        q_pos = start + jnp.arange(Q_BLOCK)
        mask = key_pos[None, :] <= q_pos[:, None]
        logits = jnp.einsum('bqhd,bkd->bqhk', iqb, ik).astype(jnp.float32)
        score = jnp.einsum('bqhk,bqh->bqk', jax.nn.relu(logits), iwb.astype(jnp.float32))
        score = jnp.where(mask[None], score, -jnp.inf)
        _, sel = lax.top_k(score, k_top)
        valid = sel <= q_pos[None, :, None]
        k_sel = jax.vmap(lambda kb, ib: kb[ib])(k, sel)
        v_sel = jax.vmap(lambda vb, ib: vb[ib])(v, sel)
        s = jnp.einsum('bqhd,bqkd->bhqk', qb, k_sel).astype(jnp.float32) * scale
        s = jnp.where(valid[:, None], s, -jnp.inf)
        p = jax.nn.softmax(s, axis=-1)
        return jnp.einsum('bhqk,bqkd->bqhd', p.astype(v.dtype), v_sel)

    out = lax.map(block, jnp.arange(S // Q_BLOCK))
    return out.transpose(1, 0, 2, 3, 4).reshape(B, S, H, D)

def first_inputs(seed: int = 0) -> dict:
    key = jax.random.key(seed)
    ks = jax.random.split(key, 20)
    f32 = jnp.float32

    def nrm(k, shape, scale):
        return jax.random.normal(k, shape, f32) * scale

    def gain(k, shape):
        return 1.0 + 0.05 * jax.random.normal(k, shape, f32)

    x = jax.random.normal(ks[0], (BATCH, SEQ, D_MODEL), f32)
    c = jax.random.normal(ks[1], (BATCH, D_MODEL), f32)
    offset = jax.random.randint(ks[2], (BATCH, 1), 0, 1024, dtype=jnp.int32)
    positions = (jnp.arange(SEQ, dtype=jnp.int32)[None, :] + offset).astype(jnp.int32)
    return {
        "x": x,
        "c": c,
        "positions": positions,
        "w_ada": nrm(ks[3], (DEPTH, D_MODEL, ADA_CHUNKS * D_MODEL), 0.5 * D_MODEL ** -0.5),
        "b_ada": nrm(ks[4], (DEPTH, ADA_CHUNKS * D_MODEL), 0.02),
        "g_attn_pre": gain(ks[5], (DEPTH, D_MODEL)),
        "g_attn_post": gain(ks[6], (DEPTH, D_MODEL)),
        "g_ffn_pre": gain(ks[7], (DEPTH, D_MODEL)),
        "g_ffn_post": gain(ks[8], (DEPTH, D_MODEL)),
        "w_in": nrm(ks[9], (DEPTH, D_MODEL, PROJ_TOTAL), D_MODEL ** -0.5),
        "lambda_q1": nrm(ks[10], (DEPTH, DIFF_QK_DIM), 0.1),
        "lambda_k1": nrm(ks[11], (DEPTH, DIFF_QK_DIM), 0.1),
        "lambda_q2": nrm(ks[12], (DEPTH, DIFF_QK_DIM), 0.1),
        "lambda_k2": nrm(ks[13], (DEPTH, DIFF_QK_DIM), 0.1),
        "g_diff_sub": gain(ks[14], (DEPTH, DIFF_V_DIM)),
        "w_o": nrm(ks[15], (DEPTH, MIX_WIDTH, D_MODEL), MIX_WIDTH ** -0.5),
        "w_gate": nrm(ks[16], (DEPTH, D_MODEL, D_FF), D_MODEL ** -0.5),
        "w_up": nrm(ks[17], (DEPTH, D_MODEL, D_FF), D_MODEL ** -0.5),
        "w_down": nrm(ks[18], (DEPTH, D_FF, D_MODEL), D_FF ** -0.5),
    }

def first_block(x, c, positions, w_ada, b_ada, g_attn_pre, g_attn_post, g_ffn_pre,
              g_ffn_post, w_in, lambda_q1, lambda_k1, lambda_q2, lambda_k2,
              g_diff_sub, w_o, w_gate, w_up, w_down):
    B, S, _ = x.shape
    k_top = min(INDEX_TOPK, S // 4)
    offsets = [0]
    for sz in PROJ_SIZES:
        offsets.append(offsets[-1] + sz)
    idx_w_scale = (N_IDX_HEADS ** -0.5) * (IDX_DIM ** -0.5)

    for l in range(DEPTH):
        mod = jax.nn.silu(c) @ w_ada[l] + b_ada[l]
        shift_a, scale_a, gate_a, shift_f, scale_f, gate_f = jnp.split(mod, ADA_CHUNKS, axis=-1)

        h = rms_norm(x, g_attn_pre[l]) * (1.0 + scale_a[:, None]) + shift_a[:, None]
        proj = h @ w_in[l]
        parts = [proj[..., offsets[i]:offsets[i + 1]] for i in range(len(PROJ_SIZES))]
        d_q, d_k, d_v, s_q, s_k, s_v, i_q, i_k, i_w = parts

        d_q = d_q.reshape(B, S, N_DIFF_HEADS, 2, DIFF_QK_DIM)
        d_k = d_k.reshape(B, S, N_DIFF_HEADS, 2, DIFF_QK_DIM)
        q1 = partial_rope(d_q[..., 0, :], positions)
        q2 = partial_rope(d_q[..., 1, :], positions)
        k1 = partial_rope(d_k[..., 0, :], positions)
        k2 = partial_rope(d_k[..., 1, :], positions)
        d_v = d_v.reshape(B, S, N_DIFF_HEADS, DIFF_V_DIM)
        lam_init = 0.8 - 0.6 * math.exp(-0.3 * l)
        lam = (jnp.exp(jnp.sum(lambda_q1[l].astype(jnp.float32) * lambda_k1[l].astype(jnp.float32)))
               - jnp.exp(jnp.sum(lambda_q2[l].astype(jnp.float32) * lambda_k2[l].astype(jnp.float32)))
               + lam_init)
        diff_out = differential_attention(q1, q2, k1, k2, d_v, lam)
        diff_out = rms_norm(diff_out, g_diff_sub[l]) * (1.0 - lam_init)
        diff_out = diff_out.reshape(B, S, DIFF_V)

        s_q = partial_rope(s_q.reshape(B, S, N_DSA_HEADS, DSA_HEAD_DIM), positions)
        s_k = partial_rope(s_k.reshape(B, S, 1, DSA_HEAD_DIM), positions)[:, :, 0]
        i_q = partial_rope(i_q.reshape(B, S, N_IDX_HEADS, IDX_DIM), positions)
        i_k = partial_rope(i_k.reshape(B, S, 1, IDX_DIM), positions)[:, :, 0]
        i_w = i_w * idx_w_scale
        dsa_out = indexed_sparse_attention(s_q, s_k, s_v, i_q, i_k, i_w, k_top)
        dsa_out = dsa_out.reshape(B, S, N_DSA_HEADS * DSA_HEAD_DIM)

        mixed = jnp.concatenate([diff_out, dsa_out], axis=-1) @ w_o[l]
        x = x + gate_a[:, None] * rms_norm(mixed, g_attn_post[l])

        h = rms_norm(x, g_ffn_pre[l]) * (1.0 + scale_f[:, None]) + shift_f[:, None]
        ff = (jax.nn.silu(h @ w_gate[l]) * (h @ w_up[l])) @ w_down[l]
        x = x + gate_f[:, None] * rms_norm(ff, g_ffn_post[l])

    return x


GRID_W = 64
N_META = 16
EPS = 1e-6
NEG_INF = -1e30
NA_HEADS = 8
NA_HEAD_DIM = 128
NA_WIN_ROWS = 8
NA_WIN_COLS = 16
NA_COL_BLOCK = 16
NA_KEY_COLS = NA_COL_BLOCK + NA_WIN_COLS
MLA_HEADS = 8
MLA_Q_RANK = 512
MLA_KV_RANK = 256
MLA_NOPE_DIM = 128
MLA_ROPE_DIM = 64
MLA_V_DIM = 128
MLA_QK_DIM = MLA_NOPE_DIM + MLA_ROPE_DIM
ROPE_THETA_2 = 10000.0
D_FF_2 = 5632
CONV_W = 3

NA_WIDTH = NA_HEADS * NA_HEAD_DIM
MLA_WIDTH = MLA_HEADS * MLA_V_DIM
D_MIX = NA_WIDTH + MLA_WIDTH
IN_COLS = 3 * NA_WIDTH + MLA_Q_RANK + MLA_KV_RANK + MLA_ROPE_DIM
IN_SPLITS = [NA_WIDTH, 2 * NA_WIDTH, 3 * NA_WIDTH, 3 * NA_WIDTH + MLA_Q_RANK, 3 * NA_WIDTH + MLA_Q_RANK + MLA_KV_RANK]


def rmsnorm(x, g):
    xf = x.astype(jnp.float32)
    y = xf * lax.rsqrt(jnp.mean(xf * xf, axis=-1, keepdims=True) + EPS)
    return (y * g.astype(jnp.float32)).astype(x.dtype)

def rope_tables_2(length, dtype):
    inv = ROPE_THETA_2 ** (-jnp.arange(0, MLA_ROPE_DIM, 2, dtype=jnp.float32) / MLA_ROPE_DIM)
    ang = jnp.arange(length, dtype=jnp.float32)[:, None] * inv[None, :]
    return jnp.cos(ang)[:, None, :].astype(dtype), jnp.sin(ang)[:, None, :].astype(dtype)

def apply_rope(x, cos, sin):
    half = x.shape[-1] // 2
    x1, x2 = x[..., :half], x[..., half:]
    return jnp.concatenate([x1 * cos - x2 * sin, x2 * cos + x1 * sin], axis=-1)

def neighbourhood_attention(q, k, v, rpb, meta_bias):
    B, L, H, D = q.shape
    T = L - N_META
    rows = T // GRID_W
    kh = min(NA_WIN_ROWS, rows)
    scale = D ** -0.5
    n_cb = GRID_W // NA_COL_BLOCK
    qm, km, vm = q[:, :N_META], k[:, :N_META], v[:, :N_META]

    s_mm = jnp.einsum('bqhd,bkhd->bhqk', qm, km).astype(jnp.float32) * scale + meta_bias.astype(jnp.float32)[None, :, None, :]
    p_mm = jax.nn.softmax(s_mm, axis=-1).astype(vm.dtype)
    meta_out = jnp.einsum('bhqk,bkhd->bqhd', p_mm, vm)

    qg = q[:, N_META:].reshape(B, rows, GRID_W, H, D)
    kg = k[:, N_META:].reshape(B, rows, GRID_W, H, D)
    vg = v[:, N_META:].reshape(B, rows, GRID_W, H, D)

    qcols = np.arange(GRID_W).reshape(n_cb, NA_COL_BLOCK)
    col_start = np.clip(qcols - NA_WIN_COLS // 2, 0, GRID_W - NA_WIN_COLS)
    kblk_start = np.clip(np.arange(n_cb) * NA_COL_BLOCK - NA_WIN_COLS // 2, 0, GRID_W - NA_KEY_COLS)
    key_cols = kblk_start[:, None] + np.arange(NA_KEY_COLS)[None, :]
    col_valid = (key_cols[:, None, :] >= col_start[:, :, None]) & (key_cols[:, None, :] < col_start[:, :, None] + NA_WIN_COLS)
    col_mask = jnp.asarray(np.where(col_valid, 0.0, NEG_INF), jnp.float32)
    dc_idx = np.clip(key_cols[:, None, :] - qcols[:, :, None] + NA_WIN_COLS - 1, 0, 2 * NA_WIN_COLS - 2)
    rpb32 = rpb.astype(jnp.float32)
    mbias = meta_bias.astype(jnp.float32)[None, None, None]

    def row_block(r):
        rs = jnp.clip(r - kh // 2, 0, rows - kh)
        kb = lax.dynamic_slice_in_dim(kg, rs, kh, axis=1)[:, :, key_cols]
        vb = lax.dynamic_slice_in_dim(vg, rs, kh, axis=1)[:, :, key_cols]
        qr = lax.dynamic_index_in_dim(qg, r, axis=1, keepdims=False).reshape(B, n_cb, NA_COL_BLOCK, H, D)
        s_win = jnp.einsum('bjqhd,bijkhd->bjqhik', qr, kb).astype(jnp.float32) * scale
        dr_idx = rs + jnp.arange(kh) - r + NA_WIN_ROWS - 1
        bias = rpb32[:, dr_idx][:, :, dc_idx].transpose(2, 3, 0, 1, 4)
        s_win = s_win + bias[None] + col_mask[None, :, :, None, None, :]
        s_met = jnp.einsum('bjqhd,bmhd->bjqhm', qr, km).astype(jnp.float32) * scale + mbias
        s = jnp.concatenate([s_met, s_win.reshape(B, n_cb, NA_COL_BLOCK, H, kh * NA_KEY_COLS)], axis=-1)
        p = jax.nn.softmax(s, axis=-1).astype(vb.dtype)
        p_win = p[..., N_META:].reshape(B, n_cb, NA_COL_BLOCK, H, kh, NA_KEY_COLS)
        out = jnp.einsum('bjqhm,bmhd->bjqhd', p[..., :N_META], vm) + jnp.einsum('bjqhik,bijkhd->bjqhd', p_win, vb)
        return out.reshape(B, GRID_W, H, D)

    real = lax.map(row_block, jnp.arange(rows))
    real = real.transpose(1, 0, 2, 3, 4).reshape(B, T, H, D)
    return jnp.concatenate([meta_out, real], axis=1)

def mla_attention(cq, ckv, k_pe, cq_g, ckv_g, w_q_up, w_kv_up, q_g, k_g, cos, sin):
    B, L, _ = cq.shape
    q = (rmsnorm(cq, cq_g) @ w_q_up).reshape(B, L, MLA_HEADS, MLA_QK_DIM)
    kv = (rmsnorm(ckv, ckv_g) @ w_kv_up).reshape(B, L, MLA_HEADS, MLA_NOPE_DIM + MLA_V_DIM)
    k_nope, v = kv[..., :MLA_NOPE_DIM], kv[..., MLA_NOPE_DIM:]
    k = jnp.concatenate([k_nope, jnp.broadcast_to(k_pe[:, :, None, :], (B, L, MLA_HEADS, MLA_ROPE_DIM))], axis=-1)
    q = rmsnorm(q, q_g)
    k = rmsnorm(k, k_g)
    q = jnp.concatenate([q[..., :MLA_NOPE_DIM], apply_rope(q[..., MLA_NOPE_DIM:], cos, sin)], axis=-1)
    k = jnp.concatenate([k[..., :MLA_NOPE_DIM], apply_rope(k[..., MLA_NOPE_DIM:], cos, sin)], axis=-1)
    scale = MLA_QK_DIM ** -0.5

    def attend(qb):
        s = jnp.einsum('bqhd,bkhd->bhqk', qb, k).astype(jnp.float32) * scale
        p = jax.nn.softmax(s, axis=-1).astype(v.dtype)
        return jnp.einsum('bhqk,bkhd->bqhd', p, v)

    out_meta = attend(q[:, :N_META])
    nb = (L - N_META) // Q_BLOCK
    qr = q[:, N_META:].reshape(B, nb, Q_BLOCK, MLA_HEADS, MLA_QK_DIM).transpose(1, 0, 2, 3, 4)
    out_real = lax.map(attend, qr).transpose(1, 0, 2, 3, 4).reshape(B, L - N_META, MLA_HEADS, MLA_V_DIM)
    return jnp.concatenate([out_meta, out_real], axis=1)

def conv_glu(x, w_gate, w_up, conv_w, conv_b, w_down):
    L = x.shape[1]
    g = x @ w_gate
    u = x @ w_up
    pad = CONV_W // 2
    gp = jnp.pad(g, ((0, 0), (pad, pad), (0, 0)))
    gc = conv_b
    for i in range(CONV_W):
        gc = gc + conv_w[i] * gp[:, i:i + L]
    return (jax.nn.silu(gc) * u) @ w_down

def second_inputs(seed: int = 0) -> dict:
    key = jax.random.key(seed)
    ks = jax.random.split(key, 24)
    f32 = jnp.float32

    def nrm(k, shape, s):
        return jax.random.normal(k, shape, f32) * s

    def gain(k, shape):
        return 1.0 + 0.05 * jax.random.normal(k, shape, f32)

    return {
        "x": nrm(ks[0], (BATCH, SEQ, D_MODEL), 1.0),
        "meta_tokens": nrm(ks[1], (N_META, D_MODEL), 1.0),
        "mix_norm_g": gain(ks[2], (DEPTH, D_MODEL)),
        "w_in": nrm(ks[3], (DEPTH, D_MODEL, IN_COLS), D_MODEL ** -0.5),
        "na_q_g": gain(ks[4], (DEPTH, NA_HEAD_DIM)),
        "na_k_g": gain(ks[5], (DEPTH, NA_HEAD_DIM)),
        "na_rpb": nrm(ks[6], (DEPTH, NA_HEADS, 2 * NA_WIN_ROWS - 1, 2 * NA_WIN_COLS - 1), 0.1),
        "na_meta_bias": nrm(ks[7], (DEPTH, NA_HEADS, N_META), 0.1),
        "mla_cq_g": gain(ks[8], (DEPTH, MLA_Q_RANK)),
        "mla_ckv_g": gain(ks[9], (DEPTH, MLA_KV_RANK)),
        "w_q_up": nrm(ks[10], (DEPTH, MLA_Q_RANK, MLA_HEADS * MLA_QK_DIM), MLA_Q_RANK ** -0.5),
        "w_kv_up": nrm(ks[11], (DEPTH, MLA_KV_RANK, MLA_HEADS * (MLA_NOPE_DIM + MLA_V_DIM)), MLA_KV_RANK ** -0.5),
        "mla_q_g": gain(ks[12], (DEPTH, MLA_QK_DIM)),
        "mla_k_g": gain(ks[13], (DEPTH, MLA_QK_DIM)),
        "na_out_g": gain(ks[14], (DEPTH, NA_WIDTH)),
        "mla_out_g": gain(ks[15], (DEPTH, MLA_WIDTH)),
        "w_out": nrm(ks[16], (DEPTH, D_MIX, D_MODEL), D_MIX ** -0.5),
        "ffn_norm_g": gain(ks[17], (DEPTH, D_MODEL)),
        "w_gate": nrm(ks[18], (DEPTH, D_MODEL, D_FF_2), D_MODEL ** -0.5),
        "w_up": nrm(ks[19], (DEPTH, D_MODEL, D_FF_2), D_MODEL ** -0.5),
        "conv_w": nrm(ks[20], (DEPTH, CONV_W, D_FF_2), CONV_W ** -0.5),
        "conv_b": nrm(ks[21], (DEPTH, D_FF_2), 0.01),
        "w_down": nrm(ks[22], (DEPTH, D_FF_2, D_MODEL), D_FF_2 ** -0.5),
    }

def second_block(x, meta_tokens, mix_norm_g, w_in, na_q_g, na_k_g, na_rpb, na_meta_bias, mla_cq_g, mla_ckv_g,
              w_q_up, w_kv_up, mla_q_g, mla_k_g, na_out_g, mla_out_g, w_out, ffn_norm_g, w_gate, w_up,
              conv_w, conv_b, w_down):
    B = x.shape[0]
    meta = jnp.broadcast_to(meta_tokens.astype(x.dtype)[None], (B, N_META, D_MODEL))
    h = jnp.concatenate([meta, x], axis=1)
    L = h.shape[1]
    cos, sin = rope_tables_2(L, x.dtype)
    for l in range(DEPTH):
        hn = rmsnorm(h, mix_norm_g[l])
        proj = hn @ w_in[l]
        q_a, k_a, v_a, cq, ckv, k_pe = jnp.split(proj, IN_SPLITS, axis=-1)
        q_a = rmsnorm(q_a.reshape(B, L, NA_HEADS, NA_HEAD_DIM), na_q_g[l])
        k_a = rmsnorm(k_a.reshape(B, L, NA_HEADS, NA_HEAD_DIM), na_k_g[l])
        v_a = v_a.reshape(B, L, NA_HEADS, NA_HEAD_DIM)
        out_a = neighbourhood_attention(q_a, k_a, v_a, na_rpb[l], na_meta_bias[l]).reshape(B, L, NA_WIDTH)
        out_b = mla_attention(cq, ckv, k_pe, mla_cq_g[l], mla_ckv_g[l], w_q_up[l], w_kv_up[l],
                              mla_q_g[l], mla_k_g[l], cos, sin).reshape(B, L, MLA_WIDTH)
        mix = jnp.concatenate([rmsnorm(out_a, na_out_g[l]), rmsnorm(out_b, mla_out_g[l])], axis=-1)
        h = h + mix @ w_out[l]
        h = h + conv_glu(rmsnorm(h, ffn_norm_g[l]), w_gate[l], w_up[l], conv_w[l], conv_b[l], w_down[l])
    return h[:, N_META:]


def setup_inputs(seed=0):
    out = dict(first_inputs(seed))
    for name, value in second_inputs(seed + 1).items():
        if name != "x":
            out[name + "_2"] = value
    return out


def reference(
    x, c, positions, w_ada, b_ada, g_attn_pre, g_attn_post, g_ffn_pre, g_ffn_post, w_in,
    lambda_q1, lambda_k1, lambda_q2, lambda_k2, g_diff_sub, w_o, w_gate, w_up, w_down,
    meta_tokens_2, mix_norm_g_2, w_in_2, na_q_g_2, na_k_g_2, na_rpb_2, na_meta_bias_2,
    mla_cq_g_2, mla_ckv_g_2, w_q_up_2, w_kv_up_2, mla_q_g_2, mla_k_g_2, na_out_g_2, mla_out_g_2,
    w_out_2, ffn_norm_g_2, w_gate_2, w_up_2, conv_w_2, conv_b_2, w_down_2,
):
    x = first_block(
        x, c, positions, w_ada, b_ada, g_attn_pre, g_attn_post, g_ffn_pre, g_ffn_post, w_in,
        lambda_q1, lambda_k1, lambda_q2, lambda_k2, g_diff_sub, w_o, w_gate, w_up, w_down,
    )
    return second_block(
        x, meta_tokens_2, mix_norm_g_2, w_in_2, na_q_g_2, na_k_g_2, na_rpb_2, na_meta_bias_2,
        mla_cq_g_2, mla_ckv_g_2, w_q_up_2, w_kv_up_2, mla_q_g_2, mla_k_g_2, na_out_g_2,
        mla_out_g_2, w_out_2, ffn_norm_g_2, w_gate_2, w_up_2, conv_w_2, conv_b_2, w_down_2,
    )


_drawn_inputs = setup_inputs


def setup_inputs(seed=0):
    import zlib

    import numpy as np

    out = dict(_drawn_inputs(seed))
    spreads = {}
    factors = {'g_ffn_post': 3.429,
     'lambda_q1': 8.0,
     'na_q_g_2': 3.783,
     'na_k_g_2': 3.006,
     'na_meta_bias_2': 11.905,
     'mla_cq_g_2': 4.405,
     'mla_q_g_2': 4.319,
     'mla_k_g_2': 4.763,
     'conv_b_2': 30.433,
     'na_rpb_2': 5.655,
     'na_out_g_2': 2.758,
     'mla_out_g_2': 2.79,
     'ffn_norm_g_2': 4.083}
    for name, (base, spread) in spreads.items():
        noise = np.random.default_rng([zlib.crc32(name.encode()), seed]).standard_normal(out[name].shape)
        drawn = base * np.exp(spread * noise) if base else spread * noise
        out[name] = __import__('jax').numpy.asarray(drawn.astype(out[name].dtype))
    for name, factor in factors.items():
        out[name] = (out[name] * factor).astype(out[name].dtype)
    return out
```

```python
from contextlib import ExitStack

import numpy as np

import concourse.bass as bass
from concourse import mybir

F32 = mybir.dt.float32
F32R = mybir.dt.float32r
I32 = mybir.dt.int32
ALU = mybir.AluOpType
ACT = mybir.ActivationFunctionType

P = 128
T = 256
TM = 272
TQ = 258
KC = 16
FC = 44
NEG = -1.0e30
USED = -3.0e38
BIG = 3.0e38
TILE = 1024

SHIFT_A, SCALE_A, GATE_A, SHIFT_F, SCALE_F, GATE_F = range(0, 96, 16)

W_IN_GROUPS = [
    [(4352, 4864)],
    [(4864, 5376)],
    [(5376, 5440), (5376, 5440), (4096, 4224), (4224, 4352), (5440, 5456)],
    [(3072, 3584)],
    [(3584, 4096)],
    [(1024, 1536)],
    [(2048, 2560)],
    [(0, 512)],
    [(1536, 2048)],
    [(2560, 3072)],
    [(512, 1024)],
]
G_COLS = [sum(b - a for a, b in g) for g in W_IN_GROUPS]
IQ0, IQ1, IKS, SQ0, SQ1, DK0, DV0, DQ0, DK1, DV1, DQ1 = range(11)
PASSES = [(0, 2), (2, 6), (6, 10), (10, 16)]

QA, KA, VA, CQ, CKV, KPE = 0, 8, 16, 24, 28, 30

KCHUNKS = {"o": 16, "gate": 16, "up": 16, "down": 44, "in2": 16, "qup": 4, "kvup": 2,
           "out2": 16, "gate2": 16, "up2": 16, "down2": 44}

VECS = [("b_ada", 96), ("g_attn_pre", 16), ("g_attn_post", 16), ("g_ffn_pre", 16), ("g_ffn_post", 16),
        ("mix_norm_g_2", 16), ("ffn_norm_g_2", 16), ("conv_w_2", 132), ("conv_b_2", 44),
        ("na_q_g_2", 1), ("na_k_g_2", 1), ("g_diff_sub", 1), ("mla_cq_g_2", 4), ("mla_ckv_g_2", 2),
        ("mq_n", 1), ("mq_r", 1), ("mk_n", 1), ("mk_r", 1), ("na_out_g_2", 8), ("mla_out_g_2", 8)]
VOFF = {}
for _name, _n in VECS:
    VOFF[_name] = sum(n for _, n in VECS[:len(VOFF)])
NVEC = sum(n for _, n in VECS)

CONSTS = [("ident", 128), ("swap", 128), ("causal", 256), ("namask", 64), ("freq", 16)]
COFF = {}
for _name, _n in CONSTS:
    COFF[_name] = sum(n for _, n in CONSTS[:len(COFF)])
NCONST = sum(n for _, n in CONSTS)
RPB_ROW = 160


def spread(main, extra, share=1.0):
    out, done = [], 0
    for i, m in enumerate(main):
        out.append(m)
        upto = min(len(extra), round((i + 1) * len(extra) / (len(main) * share)))
        out += extra[done:upto]
        done = max(done, upto)
    return out + extra[done:]


def blocks(mat, order):
    order = [(mat, kc, fb) for kc, fb in order] if isinstance(mat, str) else order
    assert len(order) % 8 == 0, (mat, len(order))
    return [("b", tuple(order[i:i + 8])) for i in range(0, len(order), 8)]


def tile_plan():
    def ada(c0, n):
        return [("a", 2 * c + h) for c in range(c0, c0 + n) for h in range(2)]

    def ada_pass(k0, k1):
        return ada(SHIFT_A + k0, k1 - k0) + ada(SCALE_A + k0, k1 - k0)

    plan = ada_pass(*PASSES[0])
    for i, (k0, k1) in enumerate(PASSES):
        tiles = [("x", g, kp) for g in range(11) for kp in range(k0 // 2, k1 // 2)]
        nxt = ada_pass(*PASSES[i + 1]) if i + 1 < len(PASSES) else ada(GATE_A, 16)
        plan += spread(tiles, nxt, 0.8)
    o = blocks("o", [(kc, fb) for fb in range(16) for kc in range(8, 16)])
    o += blocks("o", [(kc, fb) for fb in range(16) for kc in range(8)])
    plan += spread(o, ada(SHIFT_F, 16) + ada(SCALE_F, 16), 0.9)

    def glu(g, u):
        first = [(m, kc, fb) for kc in range(16) for m, fb in ((g, 0), (u, 0), (g, 1), (u, 1))]
        rest = [(m, kc, fb) for fb in range(2, FC) for m in (g, u) for kc in range(16)]
        return blocks(None, first + rest)

    plan += spread(glu("gate", "up"), ada(GATE_F, 16), 0.6)
    plan += blocks("down", [(kc, fb) for fb in range(16) for kc in range(FC)])
    in2 = [(kc, CQ + i) for kc in range(16) for i in range(4)]
    in2 += [(kc, fb) for fb in (CKV, CKV + 1, KPE) for kc in range(16)]
    plan += blocks("in2", in2)
    plan += blocks("qup", [(kc, fb) for fb in range(12) for kc in range(4)])
    plan += blocks("kvup", [(kc, fb) for fb in range(16) for kc in range(2)])
    plan += blocks("in2", [(kc, fb + h) for h in range(8) for fb in (QA, KA, VA) for kc in range(16)])
    plan += blocks("out2", [(kc, fb) for fb in range(16) for kc in range(8, 16)])
    plan += blocks("out2", [(kc, fb) for fb in range(16) for kc in range(8)])
    plan += glu("gate2", "up2")
    plan += blocks("down2", [(kc, fb) for fb in range(16) for kc in range(FC)])
    return plan


def flat(tokens):
    if tokens is None:
        return []
    if isinstance(tokens, tuple) and len(tokens) == 2 and isinstance(tokens[1], int):
        return [tokens]
    return [t for x in tokens for t in flat(x)]


class Engine:

    def __init__(self, sem):
        self.sem, self.n, self.queue, self.seen = sem, 0, [], {}

    def put(self, fn, after=(), signal=True):
        waits = {}
        for sem, value in flat(after):
            if value > self.seen.get(sem.num, 0):
                self.seen[sem.num] = value
                waits[sem.num] = (sem, value)
        if signal:
            self.n += 1
        self.queue.append((fn, list(waits.values()), signal))
        return (self.sem, self.n) if signal else None

    def emit(self, engine):
        for fn, waits, signal in self.queue:
            for sem, value in waits:
                engine.wait_ge(sem, value)
            ins = fn(engine)
            if signal:
                ins.then_inc(self.sem, 1)


class Ring:

    def __init__(self, items, free=None):
        self.items, self.i = items, 0
        self.free = free if free is not None else {k: [] for k in range(len(items))}

    def take(self):
        k = self.i
        self.i = (k + 1) % len(self.items)
        after = self.free[k]
        assert after is not None, "buffer still in use"
        self.free[k] = None
        return k, self.items[k], after

    def give(self, k, *tokens):
        self.free[k] = list(tokens)


def build(nc, wst, xT, metaT, vecs, consts, rope2, rev, cvec, positions, lambdas, rpb, mbias, out):
    ctx = ExitStack()
    with ctx:
        _build(nc, ctx, wst, xT, metaT, vecs, consts, rope2, rev, cvec, positions, lambdas, rpb, mbias, out)


def _build(nc, ctx, wst, xT, metaT, vecs, consts, rope2, rev, cvec, positions, lambdas, rpb, mbias, out):
    def sem(name):
        return ctx.enter_context(nc.semaphore(name))

    BASE = 16512
    LIMIT = 229344
    at = [BASE]
    seq = [0]

    def place(shape, dt, off, name="t"):
        seq[0] += 1
        size = 4
        for s in shape[1:]:
            size *= s
        assert off + size <= LIMIT, (name, off, size)
        return nc.alloc_sbuf_tensor_at(f"{name}_{seq[0]}", list(shape), dt, offset=off)

    def keep(shape, dt, name="t"):
        size = 4
        for s in shape[1:]:
            size *= s
        t = place(shape, dt, at[0], name)
        at[0] += (size + 31) // 32 * 32
        return t

    class Region:
        def __init__(self, start, stop=LIMIT):
            self.at, self.stop = start, stop

        def __call__(self, shape, dt=F32, name="r"):
            size = 4
            for s in shape[1:]:
                size *= s
            t = place(shape, dt, self.at, name)
            self.at += (size + 31) // 32 * 32
            assert self.at <= self.stop, (name, self.at, self.stop)
            return t

    V = Engine(sem("dve"))
    A = Engine(sem("act"))
    G = Engine(sem("pool"))
    PE = Engine(sem("pe"))
    SP = Engine(None)
    dma_sems = {}

    def f32(ap):
        return ap.bitcast(F32)

    def load(dst, src, name, engine=None, after=()):
        s = dma_sems[name] = sem(name)
        e = engine or SP
        e.put(lambda q: q.dma_start(dst, src).then_inc(s, 16), after, signal=False)
        return (s, 16)

    def act(o, i, fn, after=(), **kw):
        return A.put(lambda e: e.activation(o, i, fn, **kw), after)

    def tt(o, a, b, op, after=(), eng=None):
        return (eng or V).put(lambda e: e.tensor_tensor(o, a, b, op), after)

    def ts(o, a, s0, s1, op0, op1=None, after=(), eng=None, **kw):
        if op1 is None:
            return (eng or V).put(lambda e: e.tensor_scalar(o, a, s0, None, op0, **kw), after)
        return (eng or V).put(lambda e: e.tensor_scalar(o, a, s0, s1, op0, op1, **kw), after)

    def stt(o, a, s, b, op0, op1, after=()):
        return V.put(lambda e: e.scalar_tensor_tensor(out=o, in0=a, scalar=s, in1=b, op0=op0, op1=op1), after)

    def ttr(o, a, b, scale, init, op0, op1, acc, after=()):
        return V.put(lambda e: e.tensor_tensor_reduce(o, a, b, scale, init, op0, op1, acc), after)

    def mm(o, w, x, start, stop, after=(), signal=False):
        return PE.put(lambda e: e.matmul(o, w, x, start=start, stop=stop, skip_group_check=True), after, signal)

    def tr(o, i, after=(), signal=False):
        k = i.shape[0]
        return PE.put(lambda e: e.transpose(o, i, ident[0:k, 0:k]), after, signal)

    def memset(ap, v, after=(), eng=None):
        return (eng or G).put(lambda e: e.memset(ap, v), after)

    X = keep([P, KC, TM], F32, "x")
    RS, RW = 5, 4
    stage = keep([P, RS, TILE], F32, "stage")
    whi = keep([P, RW, TILE], F32R, "whi")
    wlo = keep([P, RW, TILE], F32R, "wlo")
    cst = keep([P, NCONST], F32, "cst")
    ones = keep([P, P], F32, "ones")
    vec = keep([P, NVEC], F32, "vec")
    adac = keep([P, 192], F32, "adac")
    mod = keep([P, 96], F32, "mod")
    mul = keep([P, 4, 16], F32, "mul")
    small = keep([P, 8], F32, "small")
    stat = keep([P, 64], F32, "stat")
    tc = keep([P, 8], F32, "tc")
    tc_free = {i: [] for i in range(8)}
    R0 = at[0]
    ident = cst[:, COFF["ident"]:COFF["ident"] + 128]
    swap = cst[:, COFF["swap"]:COFF["swap"] + 128]
    causal = cst[:, COFF["causal"]:COFF["causal"] + 256]
    namask = cst[:, COFF["namask"]:COFF["namask"] + 64]
    freq = cst[:, COFF["freq"]:COFF["freq"] + 16]
    eps = small[:, 0:1]
    nlam = small[:, 1:2]
    gdiff = small[:, 2:3]

    def v_(name, i=0, n=1):
        return vec[:, VOFF[name] + i:VOFF[name] + i + n]

    ps = [ctx.enter_context(nc.psum_tensor(f"ps{i}", [P, 512], F32)) for i in range(8)]
    bank_free = {i: [] for i in range(8)}

    class Banks:

        def __init__(self, ids):
            self.ids, self.i = ids, 0

        def take(self):
            b = self.ids[self.i % len(self.ids)]
            self.i += 1
            after = bank_free[b]
            assert after is not None, f"bank {b} in use"
            bank_free[b] = None
            return b, ps[b], after

    def give(b, *tokens):
        bank_free[b] = list(tokens)

    HID = R0 + 33024
    TMP = HID + 90112
    NTMP = LIMIT - TMP
    hidh = place([P, FC, T], F32R, HID, "hidh")
    hidl = place([P, FC, T], F32R, HID + 45056, "hidl")
    cb = place([P, 2048], F32, TMP - 8192, "cb")

    plan = tile_plan()
    stage_sem = [sem(f"stage{i}") for i in range(RS)]
    stage_free = [[] for _ in range(RS)]
    w_free = [[] for _ in range(RW)]
    st = {"dma": 0, "done": 0, "w": 0, "used": 0, "ready": []}
    ada_tok = {}
    cb_tok = []

    def stream_dma():
        while st["dma"] < len(plan) and st["dma"] - st["done"] < RS:
            t = st["dma"]
            s = t % RS
            SP.put(lambda q, t=t, s=s: q.dma_start(stage[:, s, :], wst[t]).then_inc(stage_sem[s], 16),
                   stage_free[s], signal=False)
            st["dma"] += 1

    def pump():
        stream_dma()
        while st["done"] < len(plan):
            t = st["done"]
            s = t % RS
            landed = (stage_sem[s], 16 * (t // RS + 1))
            kind = plan[t]
            if kind[0] == "a":
                j = kind[1]
                h = j % 2
                tok = ttr(stage[:, s, :], stage[:, s, :], cb[:, 1024 * h:1024 * (h + 1)], 1.0, 0.0,
                          ALU.mult, ALU.add, adac[:, j:j + 1], [landed, cb_tok])
                ada_tok[j] = tok
                stage_free[s] = [tok]
            else:
                if st["w"] - st["used"] >= RW:
                    break
                k = st["w"] % RW
                hi = act(whi[:, k, :], stage[:, s, :], ACT.Copy, [landed, w_free[k]])
                lo = tt(wlo[:, k, :], stage[:, s, :], f32(whi[:, k, :]), ALU.subtract, [landed, hi, w_free[k]])
                stage_free[s] = [lo]
                st["ready"].append((kind, k, hi, lo))
                st["w"] += 1
            st["done"] += 1
            stream_dma()

    def next_tile():
        pump()
        return st["ready"].pop(0)

    def tile_used(k, token):
        w_free[k] = [token]
        st["used"] += 1
        pump()

    pending = []

    def later(n, fn):
        pending.append([n, fn])

    def tick():
        due = []
        for p in pending:
            p[0] -= 1
            if p[0] <= 0:
                due.append(p)
        for p in due:
            pending.remove(p)
            p[1]()

    def drain():
        while pending:
            tick()

    def gemm(count, banks, moving, width, done):
        acc = {}
        for _ in range(count):
            (what, blks), k, hi_tok, lo_tok = next_tile()
            assert what == "b"
            last = None
            finished = []
            for i, (mat, kc, fb) in enumerate(blks):
                key = (mat, fb)
                first = key not in acc
                if first:
                    b, bank, free = banks.take()
                    acc[key] = [b, bank, 0, gemm_n(mat)]
                else:
                    free = []
                b, bank, n, total = acc[key]
                xh, xl, tok = moving(mat, kc)
                w = width(mat, fb)
                wh = whi[:, k, P * i:P * (i + 1)]
                wl = wlo[:, k, P * i:P * (i + 1)]
                acc[key][2] = n + 1
                end = n + 1 == total
                o = bank[:, 0:w]
                mm(o, wh, xh[:, 0:w], first, False, [hi_tok, tok, free])
                mm(o, wh, xl[:, 0:w], False, False)
                sig = end or i == len(blks) - 1
                last = mm(o, wl, xh[:, 0:w], False, end, [lo_tok], signal=sig) or last
                if end:
                    finished.append((mat, fb, b, bank, last))
                    del acc[key]
                    if i < len(blks) - 1:
                        mat_, fb_, b_, bank_, tok_ = finished.pop()
                        done(mat_, fb_, b_, bank_, tok_)
            tile_used(k, last)
            for f in finished:
                done(*f)
            tick()
            yield
        assert not acc

    halves = {}

    def gemm_n(mat):
        return halves.get(mat, KCHUNKS[mat])

    def run(main, sides=(), rate=1.0):
        live = list(sides)
        credit = 0.0
        for _ in main:
            credit += rate
            while credit >= 1.0:
                credit -= 1.0
                for s in list(live):
                    if next(s, "end") == "end":
                        live.remove(s)
        return live

    def finish(sides):
        live = list(sides)
        n = 0
        while live:
            for s in list(live):
                if next(s, "end") == "end":
                    live.remove(s)
            tick()
            n += 1
            assert n < 1000, "stuck"

    def rms(o, src, n, after, bias=None):
        a = act(o, src, ACT.Ln, after, scale=1.0 / n, bias=eps)
        b = act(o, o, ACT.Exp, [a], scale=-0.5)
        return a, b

    P1 = Region(TMP)
    P1b = Region(TMP - 16384, TMP - 8192)
    ering = Ring([P1([P, 2, 384], F32, "e") for _ in range(2)])
    ptring = Ring([P1([P, 384], F32, "pt") for _ in range(2)])
    R1 = P1([P, T], F32, "R1")
    rl = [P1b([P, 512], F32, "rl") for _ in range(2)]
    sc = P1b([P, 384], F32, "sc")
    wk = P1b([P, 384], F32, "wk")
    M1 = place([P, 384], F32, TMP - 16384, "M1")
    start_at = TMP - 16384 + 4096
    P1c = Region(TMP - 16384, TMP - 8192)
    oring = Ring([P1c([P, T], F32, "o") for _ in range(2)])
    sqring = Ring([P1c([P, T], F32, "sq") for _ in range(2)])
    rring = Ring([P1c([P, T], F32, "rr") for _ in range(2)])
    fring = Ring([P1c([P, T], F32, "mf") for _ in range(2)])
    rt = [P1([P, 128], F32, "rt") for _ in range(4)]
    cosT = P1([P, 2, 16], F32, "cosT")
    sinT = P1([P, 2, 16], F32, "sinT")
    iw = P1([P, 2, 16], F32, "iw")

    slot = [HID + 4096 * i for i in range(11)]
    extra = [HID + 45056 + 4096 * i for i in range(3)]
    part = [place([P, 2, 512], F32, slot[g], f"part{g}") for g in range(11)]
    xr = place([P, KC, T], F32, HID + 57344, "xr")
    mxh = place([P, 8, T], F32R, HID + 57344, "mxh")
    mxl = place([P, 8, T], F32R, HID + 57344 + 8192, "mxl")
    assert HID + 57344 + 16384 <= TMP - 16384
    hh = place([P, KC, T], F32R, R0, "hh")
    hl = place([P, KC, T], F32R, R0 + 16384, "hl")
    mdh = place([P, 8, T], F32R, R0, "mdh")
    mdl = place([P, 8, T], F32R, R0 + 8192, "mdl")

    cb_load = load(cb[:, :], bass.AP(cvec.tensor, 0, [[0, P], [1, 2048]]), "ld_c")
    vec_load = load(vec[:, :], vecs, "ld_vec")
    posi = place([P, 2], I32, start_at, "posi")
    posf = place([P, 2], F32, start_at + 32, "posf")
    ang = [place([P, 2, 16], F32, start_at + 64 + 128 * i, "ang") for i in range(4)]
    lam_in = place([P, 256], F32, start_at + 1024, "lam")
    lamt = place([P, 8], F32, start_at + 2048, "lamt")
    pos_load = load(posi[:, :], positions, "ld_pos", A)
    x_load = [load(X[:, 4 * i:4 * i + 4, 0:T], xT[:, 4 * i:4 * i + 4, :], f"ld_x{i}", A) for i in range(4)]
    cst_load = load(cst[:, :], consts, "ld_cst", A)
    lam_load = load(lam_in[:, :], bass.AP(lambdas.tensor, 0, [[0, P], [1, 256]]), "ld_lam", A)
    meta_load = load(X[:, :, T:TM], metaT, "ld_meta", A)
    stream_dma()

    ones_tok = memset(ones[:, :], 1.0)
    eps_tok = memset(eps, 1e-6)
    stat_tok = memset(stat[:, :], 0.0)
    cb_tok.append(act(cb[:, :], cb[:, :], ACT.Silu, [cb_load]))

    two_pi = 2.0 * np.pi
    C1 = 6.28125
    C2 = float(np.float32(np.floor((two_pi - C1) * 2.0 ** 22) / 2.0 ** 22))
    C3 = float(np.float32(two_pi - C1 - C2))
    H1 = float(np.float32(np.pi / 2))
    H2 = float(np.float32(np.pi / 2 - H1))
    MAGIC = 12582912.0
    PI = 3.1415925
    p0 = G.put(lambda e: e.tensor_copy(posf[:, :], posi[:, :]), [pos_load])
    a0, kk, rr, r2 = [a[:, :, :] for a in ang]
    pa = None
    for tb in range(2):
        pa = ts(ang[0][:, tb, :], freq, posf[:, tb:tb + 1], None, ALU.mult, None, [p0, cst_load], G)
    trig = []
    for dst, quarter in ((sinT, 0.0), (cosT, 0.25)):
        t = ts(kk, a0, float(1.0 / two_pi), quarter, ALU.mult, ALU.add, [pa, trig], G)
        t = ts(kk, kk, MAGIC, -MAGIC, ALU.add, ALU.add, [t], G)
        src = a0
        for c in (C1, C2, C3):
            t = ts(r2, kk, -c, None, ALU.mult, None, [t], G)
            t = tt(rr, src, r2, ALU.add, [t], G)
            src = rr
        if quarter:
            t = ts(rr, rr, H1, H2, ALU.add, ALU.add, [t], G)
        t = ts(rr, rr, PI, -PI, ALU.min, ALU.max, [t], G)
        trig = act(dst[:, :, :], rr, ACT.Sin, [t])
    trig_tok = trig

    xsq = [rl[i][:, 256 * j:256 * j + 256] for i in range(2) for j in range(2)]
    sq_free = [[] for _ in range(4)]
    b, bank, free = 0, ps[0], []
    for kc in range(KC):
        s = act(xsq[kc % 4], X[:, kc, 0:T], ACT.Square, [x_load[kc // 4], sq_free[kc % 4]])
        t = mm(bank[:, 0:T], ones[:, :], xsq[kc % 4], kc == 0, kc == KC - 1, [s, ones_tok], signal=True)
        sq_free[kc % 4] = [t]
    ra, rb = rms(R1[:, :], bank[:, 0:T], 2048, [t, eps_tok])
    bank_free[0] = [ra]
    xr_tok = []
    for kc in range(KC):
        eng = G if kc >= 4 else V
        xr_tok.append(tt(xr[:, kc, :], X[:, kc, 0:T], R1[:, :], ALU.mult, [rb, x_load[kc // 4]], eng))

    la = []
    for i in range(2):
        t = ttr(lam_in[:, 128 * i:128 * i + 64], lam_in[:, 128 * i:128 * i + 64], lam_in[:, 128 * i + 64:128 * i + 128],
                1.0, 0.0, ALU.mult, ALU.add, lamt[:, i:i + 1], [lam_load])
        la.append(t)
    le = act(lamt[:, 2:4], lamt[:, 0:2], ACT.Exp, la)
    l1 = tt(lamt[:, 4:5], lamt[:, 3:4], lamt[:, 2:3], ALU.subtract, [le], G)
    lam_tok = ts(nlam, lamt[:, 4:5], -0.2, None, ALU.add, None, [l1], G)
    gdiff_tok = ts(gdiff, v_("g_diff_sub"), 0.8, None, ALU.mult, None, [vec_load], G)

    def mod_chunks(c0, n):
        t = tt(mod[:, c0:c0 + n], adac[:, 2 * c0:2 * (c0 + n):2], adac[:, 2 * c0 + 1:2 * (c0 + n):2], ALU.add,
               [ada_tok[j] for j in range(2 * c0, 2 * (c0 + n))], G)
        return tt(mod[:, c0:c0 + n], mod[:, c0:c0 + n], v_("b_ada", c0, n), ALU.add, [t, vec_load], G)

    def gain(dst, c0, n, g, one):
        t = mod_chunks(c0, n)
        if one:
            t = ts(mod[:, c0:c0 + n], mod[:, c0:c0 + n], 1.0, None, ALU.add, None, [t], G)
        return tt(dst, mod[:, c0:c0 + n], g, ALU.mult, [t, vec_load], G)

    h_tok = {}

    def make_h(k0, k1):
        n = k1 - k0
        tsh = mod_chunks(SHIFT_A + k0, n)
        tsc = gain(mul[:, 0, k0:k1], SCALE_A + k0, n, v_("g_attn_pre", k0, n), True)
        for kc in range(k0, k1):
            a = ts(xr[:, kc, :], xr[:, kc, :], mul[:, 0, kc:kc + 1], mod[:, SHIFT_A + kc:SHIFT_A + kc + 1],
                   ALU.mult, ALU.add, [xr_tok[kc], tsh, tsc])
            h = act(hh[:, kc, :], xr[:, kc, :], ACT.Copy, [a])
            l = tt(hl[:, kc, :], xr[:, kc, :], f32(hh[:, kc, :]), ALU.subtract, [a, h])
            h_tok[kc] = [h, l]

    fin = {}
    part_tok = {}
    tmp2 = Ring(rl, {0: sq_free, 1: sq_free})
    gb = Banks([0, 1, 2])

    def project():
        pump()
        make_h(*PASSES[0])
        for pi, (k0, k1) in enumerate(PASSES):
            lastp = pi == len(PASSES) - 1
            for g in range(11):
                if g == 10 and not lastp:
                    make_h(*PASSES[pi + 1])
                n = G_COLS[g]
                bk = [gb.take() for _ in range(2)]
                last = None
                for kp in range(k0 // 2, k1 // 2):
                    (what, g_, kp_), k, hi_tok, lo_tok = next_tile()
                    assert (what, g_, kp_) == ("x", g, kp)
                    for i in range(2):
                        kc = 2 * kp + i
                        wh = whi[:, k, 512 * i:512 * i + n]
                        wl = wlo[:, k, 512 * i:512 * i + n]
                        for tb in range(2):
                            o = bk[tb][1][:, 0:n]
                            c = slice(P * tb, P * tb + P)
                            st_ = kc == k0
                            en = kc == k1 - 1
                            mm(o, hh[:, kc, c], wh, st_, False, [h_tok[kc], hi_tok, bk[tb][2]])
                            mm(o, hh[:, kc, c], wl, False, False, [lo_tok])
                            last = mm(o, hl[:, kc, c], wh, False, en, signal=(i == 1)) or last
                            if en and tb == 0:
                                tok0 = last
                    tile_used(k, last)
                    if kp < k1 // 2 - 1:
                        tick()
                        yield
                toks = [tok0, last]
                res = []
                for tb in range(2):
                    b, bank, _ = bk[tb]
                    dst = part[g][:, tb, 0:n]
                    if pi == 0:
                        t = act(dst, bank[:, 0:n], ACT.Copy, [toks[tb]])
                        give(b, t)
                    elif not lastp:
                        r, buf, fr = tmp2.take()
                        t = act(buf[:, 0:n], bank[:, 0:n], ACT.Copy, [toks[tb], fr])
                        give(b, t)
                        t = tt(dst, dst, buf[:, 0:n], ALU.add, [t, part_tok[g, tb]], G)
                        tmp2.give(r, t)
                    else:
                        t = tt(dst, bank[:, 0:n], dst, ALU.add, [toks[tb], part_tok[g, tb]])
                        give(b, t)
                    part_tok[g, tb] = t
                    res.append(t)
                if lastp:
                    fin[g] = res
                tick()
                yield

    ab = Banks([3, 4, 5, 6, 7])
    rot_free = [[]]

    def rotate(g, c0, heads, dim, half, after):
        v = part[g][:, :, c0:c0 + heads * dim].rearrange("p t (h d) -> p t h d", h=heads)
        step = 16 // half
        cosb = cosT[:, :, 0:16:step].unsqueeze(2).to_broadcast([P, 2, heads, half])
        sinb = sinT[:, :, 0:16:step].unsqueeze(2).to_broadcast([P, 2, heads, half])
        x1 = v[:, :, :, 0:half]
        x2 = v[:, :, :, half:2 * half]
        n = heads * half
        r = [q[:, 0:2 * n].rearrange("p (t h d) -> p t h d", t=2, h=heads) for q in rt]
        a = [after, rot_free[0], trig_tok]
        t1 = tt(r[0], x1, cosb, ALU.mult, a, G)
        t2 = tt(r[1], x2, sinb, ALU.mult, a, G)
        t3 = tt(r[2], x2, cosb, ALU.mult, a, G)
        t4 = tt(r[3], x1, sinb, ALU.mult, a, G)
        t5 = tt(x1, r[0], r[1], ALU.subtract, [t1, t2, t3, t4], G)
        t6 = tt(x2, r[2], r[3], ALU.add, [t3, t4], G)
        rot_free[0] = [t5, t6]
        return [t5, t6]

    def turn(g, cols, evac, after):
        b, bank, free = ab.take()
        for i, c in enumerate(cols):
            for tb in range(2):
                t = tr(bank[:, 256 * i + P * tb:256 * i + P * tb + P], part[g][:, tb, c:c + P], [after, free, cst_load],
                       signal=(i == len(cols) - 1 and tb == 1))
        give(b, *evac(bank, t))
        return t

    iqT = [place([P, 4, T], F32, extra[0], "iqT0"), place([P, 4, T], F32, slot[0], "iqT1")]
    ikz = place([P, 2, T], F32, slot[1], "ikz")
    skT = place([P, T], F32, slot[1] + 2048, "skT")
    sqT = [place([P, 4, T], F32, extra[1], "sqT0"), place([P, 4, T], F32, slot[3], "sqT1")]
    kz = [place([P, 2, 2, T], F32, o, f"kz{i}") for i, o in enumerate((slot[4], extra[2], slot[7], extra[0]))]
    dqT = [place([P, 4, T], F32, slot[5], "dqT0"), place([P, 4, T], F32, slot[8], "dqT1")]
    m1 = place([P, KC, T], F32, slot[0], "m1")
    T_ = {}
    turned = {}

    def prep():
        def plain(g, dst, key, free, dim, half):
            r = rotate(g, 0, 512 // dim, dim, half, fin[g])
            yield
            toks = []
            for j in range(2):
                def ev(bank, t, j=j):
                    e = act(dst[:, 2 * j:2 * j + 2, :], bank[:, :].rearrange("p (b t) -> p b t", b=2), ACT.Copy, [t, free])
                    T_.setdefault(key, []).append(e)
                    return [e]
                toks.append(turn(g, [256 * j, 256 * j + 128], ev, [fin[g], r]))
                yield
            turned[g] = toks[-1]

        def keys(g, hp, free):
            r = rotate(g, 0, 8, 64, 8, fin[g])
            zero = [memset(kz[hp + j][:, :, :, :], 0.0, free[j]) for j in range(2)]
            yield
            for j in range(2):
                z = kz[hp + j]

                def ev(bank, t, z=z, j=j):
                    v = bank[:, :].rearrange("p (b t) -> p b t", b=2)
                    e0 = act(z[0:64, :, 0, :], v[0:64], ACT.Copy, [t, zero[j]])
                    e1 = act(z[64:128, :, 1, :], v[64:128], ACT.Copy, [t, zero[j]])
                    for i in range(2):
                        T_[("kz", 2 * (hp + j) + i)] = [e0, e1]
                    return [e0, e1]
                tok = turn(g, [256 * j, 256 * j + 128], ev, [fin[g], r])
                yield
            turned[g] = tok

        def until(f):
            while not f():
                yield

        yield from until(lambda: IQ0 in fin)
        yield from plain(IQ0, iqT[0], "iq0", [], 64, 8)
        yield from until(lambda: IQ1 in fin)
        yield from plain(IQ1, iqT[1], "iq1", [turned[IQ0]], 64, 8)
        yield from until(lambda: IKS in fin)
        r = rotate(IKS, 0, 2, 64, 8, fin[IKS])
        r2_ = rotate(IKS, 128, 1, 128, 16, fin[IKS])
        zero = memset(ikz[:, :, :], 0.0, [turned[IQ1]])
        w = ts(iw[:, :, :], part[IKS][:, :, 384:400], 1.0 / 32, None, ALU.mult, None, fin[IKS], G)
        T_["iw"] = [w]
        yield

        def ev(bank, t):
            v = bank[:, :].rearrange("p (b t) -> p b t", b=2)
            e0 = act(ikz[0:64, 0, :], v[0:64, 0, :], ACT.Copy, [t, zero])
            e1 = act(ikz[64:128, 1, :], v[64:128, 0, :], ACT.Copy, [t, zero])
            e2 = act(skT[:, :], v[:, 1, :], ACT.Copy, [t, turned[IQ1]])
            T_["ik"] = [e0, e1]
            T_["sk"] = [e2]
            return [e0, e1, e2]
        turned[IKS] = turn(IKS, [0, 128], ev, [fin[IKS], r, r2_])
        yield
        yield from until(lambda: SQ0 in fin)
        yield from plain(SQ0, sqT[0], "sq0", [], 128, 16)
        yield from until(lambda: SQ1 in fin)
        yield from plain(SQ1, sqT[1], "sq1", [turned_tok(SQ0)], 128, 16)
        yield from until(lambda: DK0 in fin)
        yield from keys(DK0, 0, [[turned[SQ1]], []])
        yield from until(lambda: DQ0 in fin)
        yield from plain(DQ0, dqT[0], "dq0", [turned[DK0]], 64, 8)
        yield from until(lambda: DK1 in fin and "indexed" in T_)
        yield from keys(DK1, 2, [[turned[DQ0]], T_["indexed"]])
        yield from until(lambda: DQ1 in fin)
        yield from plain(DQ1, dqT[1], "dq1", [turned[DK1]], 64, 8)

    def turned_tok(g):
        return turned[g]

    def lock(pipe, n):
        for t in range(n + len(pipe) - 1):
            for s in range(len(pipe) - 1, -1, -1):
                i = t - s
                if 0 <= i < n:
                    r = pipe[s](i)
                    if r is not None:
                        yield from r
            yield

    def indexer():
        while not ("ik" in T_ and len(T_.get("iq1", [])) == 2):
            yield
        last = {}
        for p in range(8):
            q = iqT[p // 4][:, p % 4, :]
            qt = [T_["iq0"] if p < 4 else T_["iq1"], T_["ik"]]
            work = []
            r, buf3, fr = ering.take()
            flatbuf = buf3[:, :, :].rearrange("p a b -> p (a b)")
            for qb in (1, 0):
                n = 256 if qb else 128
                b, bank, free = ab.take()
                t = mm(bank[:, 0:2 * n].rearrange("p (h k) -> p h k", h=2), q[:, P * qb:P * qb + P], ikz[:, :, 0:n], True, True,
                       [free, qt], signal=True)
                buf = flatbuf[:, 0:512] if qb else flatbuf[:, 512:768]
                e = act(buf, bank[:, 0:2 * n], ACT.Relu, [t, fr])
                give(b, e)
                work.append((qb, n, buf, e))
            T_["idx_pe"] = t
            used = {0: [], 1: []}
            for h in range(2):
                for qb, n, buf, e in work:
                    dst = sc[:, 128 * qb:128 * qb + n]
                    w = iw[:, qb, 2 * p + h:2 * p + h + 1]
                    src = buf[:, n * h:n * h + n]
                    if p == 0 and h == 0:
                        t = ts(dst, src, w, None, ALU.mult, None, [e, T_["iw"]])
                    else:
                        t = stt(dst, src, w, dst, ALU.mult, ALU.add, [e, last[qb]])
                    last[qb] = t
                    used[qb].append(t)
            ering.give(r, used[0], used[1])
            yield
        T_["indexed"] = [T_["idx_pe"]]
        seg = {0: slice(0, 128), 1: slice(128, 384)}
        mask = {0: causal[:, 128:256], 1: causal[:, :]}
        t = {}
        for qb in (1, 0):
            t[qb] = tt(sc[:, seg[qb]], sc[:, seg[qb]], mask[qb], ALU.add, [last[qb], cst_load])
        src = {qb: sc[:, seg[qb]] for qb in (0, 1)}
        m8 = {qb: stat[:, 8 * qb:8 * qb + 8] for qb in (0, 1)}
        for r in range(8):
            for qb in (1, 0):
                t[qb] = V.put(lambda e, qb=qb, s=src[qb]: e.max(m8[qb], s), [t[qb], stat_tok])
            for qb in (1, 0):
                t[qb] = V.put(lambda e, qb=qb, s=src[qb]: e.match_replace(wk[:, seg[qb]], m8[qb], s, USED), [t[qb]])
                src[qb] = wk[:, seg[qb]]
            yield
        toks = []
        for qb in (1, 0):
            t[qb] = tt(wk[:, seg[qb]], wk[:, seg[qb]], sc[:, seg[qb]], ALU.is_equal, [t[qb]])
        for qb in (1, 0):
            toks.append(stt(M1[:, seg[qb]], wk[:, seg[qb]], NEG, mask[qb], ALU.mult, ALU.add, [t[qb], list(tmp2.free.values())]))
        T_["M"] = toks
        yield

    seg = {0: slice(0, 128), 1: slice(128, 384)}

    def transposed_p(E, after, key):
        b, bank, free = ab.take()
        for i in range(3):
            t = tr(bank[:, P * i:P * i + P], E[:, (0, 128, 256)[i]:(0, 128, 256)[i] + P], [after, free], signal=(i == 2))
        r, buf, fr = ptring.take()
        e = act(buf[:, :], bank[:, 0:384], ACT.Copy, [t, fr])
        give(b, e)
        return t, r, buf, e

    def weighted_v(v0, v1, buf, after):
        b, bank, free = ab.take()
        mm(bank[:, 0:256], v0, buf[:, 0:256], True, False, [after, free])
        t = mm(bank[:, 128:256], v1, buf[:, 256:384], False, True, signal=True)
        return b, bank, t

    dsa = {}
    mix_tok = {}
    SD = float(128 ** -0.5)

    def dsa_steps():
        while not ("M" in T_ and len(T_.get("sq1", [])) == 2):
            yield

        def s0(h):
            b, bank, free = ab.take()
            q = sqT[h // 4][:, h % 4, :]
            qt = [T_["sq0"] if h < 4 else T_["sq1"], T_["sk"]]
            t0 = mm(bank[:, 0:128], q[:, 0:128], skT[:, 0:128], True, True, [free, qt], signal=True)
            t1 = mm(bank[:, 128:384], q[:, 128:256], skT[:, :], False, True, signal=True)
            T_["dsa_pe"] = t1
            r, E, fr = ering.take()
            c = 16 + 4 * (h % 4)
            vs, es = [], []
            for qb, t in ((0, t1), (1, t1)):
                vs.append(ttr(E[:, 0, seg[qb]], bank[:, seg[qb]], M1[:, seg[qb]], -SD, BIG, ALU.add, ALU.min,
                              stat[:, c + qb:c + qb + 1], [t, fr, T_["M"]]))
            give(b, vs)
            for qb in range(2):
                es.append(act(E[:, 0, seg[qb]], E[:, 0, seg[qb]], ACT.Exp, [vs[qb]], scale=-1.0,
                              bias=stat[:, c + qb:c + qb + 1], accum_out=stat[:, c + 2 + qb:c + 3 + qb]))
            dsa[h] = dict(r=r, E=E, es=es, c=c)

        def s1(h):
            d = dsa[h]
            E, c = d["E"], d["c"]
            t = V.put(lambda e: e.reciprocal(stat[:, c:c + 2], stat[:, c + 2:c + 4]), [d["es"]])
            ns = []
            for qb in range(2):
                ns.append(ts(E[:, 0, seg[qb]], E[:, 0, seg[qb]], stat[:, c + qb:c + qb + 1], None, ALU.mult, None, [t]))
            t, r, buf, e = transposed_p(E[:, 0, :], ns, h)
            ering.give(d["r"], t)
            d.update(pr=r, buf=buf, e=e)

        def s2(h):
            d = dsa[h]
            b, bank, t = weighted_v(part[IKS][:, 0, 256:384], part[IKS][:, 1, 256:384], d["buf"], [d["e"], fin[IKS]])
            ptring.give(d["pr"], t)
            T_["dsa_pv"] = t
            a = act(mxh[:, h, :], bank[:, 0:256], ACT.Copy, [t, h_tok[15], xr_done()])
            l = tt(mxl[:, h, :], bank[:, 0:256], f32(mxh[:, h, :]), ALU.subtract, [a])
            give(b, l)
            mix_tok[8 + h] = [a, l]

        yield from lock([s0, s1, s2], 8)

    def xr_done():
        return [h_tok[k] for k in range(KC)]

    diff = {}

    def diff_steps():
        while not (len(T_.get("dq0", [])) == 2 and ("kz", 3) in T_ and 15 in mix_tok and PROJECTED):
            yield
        now = [(V.sem, V.n), (A.sem, A.n), (PE.sem, PE.n), (G.sem, G.n)]
        for ring in (oring, sqring, rring, fring):
            for k in ring.free:
                ring.free[k] = list(now)

        def s0(h):
            q = dqT[h // 4][:, h % 4, :]
            z = kz[h // 2][:, h % 2, :, :]
            qt = [T_["dq0"] if h < 4 else T_["dq1"], T_[("kz", h)]]
            bk = []
            for qb in range(2):
                n = 256 if qb else 128
                b, bank, free = ab.take()
                t = mm(bank[:, 0:2 * n].rearrange("p (c k) -> p c k", c=2), q[:, P * qb:P * qb + P], z[:, :, 0:n], True, True,
                       [free, qt], signal=True)
                bk.append((b, bank, t, n))
            r, E, fr = ering.take()
            c = 32 + 8 * (h % 4)
            vs = {}
            for qb, (b, bank, t, n) in enumerate(bk):
                for i in range(2):
                    vs[qb, i] = ttr(E[:, i, seg[qb]], bank[:, n * i:n * i + n], causal[:, 256 - n:256], -0.125, BIG,
                                    ALU.add, ALU.min, stat[:, c + 2 * qb + i:c + 2 * qb + i + 1], [t, fr, cst_load])
                give(b, vs[qb, 0], vs[qb, 1])
            es = []
            for qb in range(2):
                for i in range(2):
                    k = 2 * qb + i
                    es.append(act(E[:, i, seg[qb]], E[:, i, seg[qb]], ACT.Exp, [vs[qb, i]], scale=-1.0,
                                  bias=stat[:, c + k:c + k + 1], accum_out=stat[:, c + 4 + k:c + 5 + k]))
            diff[h] = dict(r=r, E=E, es=es, c=c)

        def s1(h):
            d = diff[h]
            E, c = d["E"], d["c"]
            t = V.put(lambda e: e.reciprocal(stat[:, c:c + 4], stat[:, c + 4:c + 8]), [d["es"]])
            u = ts(stat[:, c + 1:c + 4:2], stat[:, c + 1:c + 4:2], nlam, None, ALU.mult, None, [t, lam_tok])
            ns = []
            for qb in range(2):
                ns.append(ts(E[:, 0, seg[qb]], E[:, 0, seg[qb]], stat[:, c + 2 * qb:c + 2 * qb + 1], None, ALU.mult, None, [t]))
            for qb in range(2):
                ns[qb] = stt(E[:, 0, seg[qb]], E[:, 1, seg[qb]], stat[:, c + 2 * qb + 1:c + 2 * qb + 2], E[:, 0, seg[qb]],
                             ALU.mult, ALU.add, [u, ns[qb]])
            t, r, buf, e = transposed_p(E[:, 0, :], ns, h)
            ering.give(d["r"], t)
            d.update(pr=r, buf=buf, e=e)

        def s2(h):
            d = diff[h]
            g = DV0 if h < 4 else DV1
            c0 = 128 * (h % 4)
            b, bank, t = weighted_v(part[g][:, 0, c0:c0 + 128], part[g][:, 1, c0:c0 + 128], d["buf"], [d["e"], fin[g]])
            ptring.give(d["pr"], t)
            r1_, o, fr1 = oring.take()
            r2_, s, fr2 = sqring.take()
            a = act(s[:, :], bank[:, 0:256], ACT.Square, [t, fr2])
            a2 = act(o[:, :], bank[:, 0:256], ACT.Copy, [t, fr1])
            give(b, a, a2)
            d.update(o=o, s=s, ro=r1_, rs=r2_, a=a, a2=a2)

        def s3(h):
            d = diff[h]
            b, bank, free = ab.take()
            t = mm(bank[:, 0:256], ones[:, :], d["s"][:, :], True, True, [free, d["a"]], signal=True)
            sqring.give(d["rs"], t)
            rk, R, fr = rring.take()
            a, e = rms(R[:, :], bank[:, 0:256], 128, [t, fr])
            give(b, a)
            fk, f, fr = fring.take()
            t = stt(f[:, :], d["o"][:, :], gdiff, R[:, :], ALU.mult, ALU.mult, [e, d["a2"], fr, gdiff_tok])
            oring.give(d["ro"], t)
            rring.give(rk, t)
            a = act(mdh[:, h, :], f[:, :], ACT.Copy, [t, PROJECTED])
            l = tt(mdl[:, h, :], f[:, :], f32(mdh[:, h, :]), ALU.subtract, [t, a, PROJECTED])
            fring.give(fk, l)
            mix_tok[h] = [a, l]

        yield from lock([s0, s1, s2, s3], 8)

    PROJECTED = []

    sides = [prep(), indexer(), dsa_steps(), diff_steps()]
    sides = run(project(), sides, 1.0)
    PROJECTED.append((PE.sem, PE.n))
    n = 0
    while 15 not in mix_tok:
        for s in list(sides):
            if next(s, "end") == "end":
                sides.remove(s)
        tick()
        n += 1
        assert n < 500

    R2 = place([P, TM], F32, LIMIT - 1088, "R2")
    halves["o"] = 8
    m_tok = {}
    phase = {"half": 0}

    def o_moving(mat, kc):
        return (mxh[:, kc - 8, :], mxl[:, kc - 8, :], mix_tok[kc]) if kc >= 8 else (mdh[:, kc, :], mdl[:, kc, :], mix_tok[kc])

    o_free = [T_["dsa_pv"], T_["dsa_pe"], turned[SQ1]]

    def o_first(mat, fb, b, bank, tok):
        t = act(m1[:, fb, :], bank[:, 0:T], ACT.Copy, [tok, o_free])
        give(b, t)
        m_tok[fb] = t

    sides = run(gemm(16, gb, o_moving, lambda m, f: T, o_first), sides, 1.5)
    finish(sides)

    F = Region(TMP, LIMIT - 1088)
    sqf = Ring([F([P, TM], F32, "sqf") for _ in range(2)])
    ssum = F([P, TM], F32, "ssum")
    zr = Ring([F([P, TQ], F32, "z") for _ in range(2)])
    ur = Ring([F([P, T], F32, "u") for _ in range(2)])
    hr = Ring([F([P, T], F32, "hf") for _ in range(2)])
    cr = Ring([F([P, T], F32, "c") for _ in range(1)])
    Rm = zr.items[0]
    guard1 = [(V.sem, V.n), (A.sem, A.n), (PE.sem, PE.n), (G.sem, G.n)]
    for ring in (sqf, zr, ur, hr, cr):
        for k in ring.free:
            ring.free[k] = list(guard1)
    acc_tok = [[]]

    def square_in(src, n, after, first):
        if first:
            t = act(ssum[:, 0:n], src, ACT.Square, [after, acc_tok[0]])
            acc_tok[0] = [t]
            return t
        k, buf, fr = sqf.take()
        s = act(buf[:, 0:n], src, ACT.Square, [after, fr])
        t = tt(ssum[:, 0:n], ssum[:, 0:n], buf[:, 0:n], ALU.add, [s, acc_tok[0]], G)
        sqf.give(k, t)
        acc_tok[0] = [t]
        return s

    def rms_of_sum(o, n, after, div=2048):
        b, bank, free = ab.take()
        t = mm(bank[:, 0:n], ones[:, :], ssum[:, 0:n], True, True, [free, acc_tok[0]], signal=True)
        acc_tok[0] = [acc_tok[0], t]
        a, e = rms(o[:, 0:n], bank[:, 0:n], div, [t, after])
        give(b, a)
        return e

    acc_tok[0] = list(guard1)

    def o_second(mat, fb, b, bank, tok):
        t = tt(m1[:, fb, :], bank[:, 0:T], m1[:, fb, :], ALU.add, [tok, m_tok[fb]])
        give(b, t)
        m_tok[fb] = [t, square_in(m1[:, fb, :], T, [t], fb == 0)]

    for _ in gemm(16, gb, o_moving, lambda m, f: T, o_second):
        pass
    halves.clear()
    drain()

    yh = place([P, KC, TQ], F32R, R0, "yh")
    yl = place([P, KC, TQ], F32R, R0 + 16512, "yl")
    x_tok = {kc: [x_load[kc // 4], meta_load] for kc in range(KC)}
    y_tok = {}

    def add_residual(m, kc, s, R, Rtok, after):
        k, buf, fr = hr.take()
        t = stt(buf[:, 0:T], m[:, kc, :], s, R[:, 0:T], ALU.mult, ALU.mult, [Rtok, after, fr])
        t = tt(X[:, kc, 0:T], X[:, kc, 0:T], buf[:, 0:T], ALU.add, [t, x_tok[kc]])
        hr.give(k, t)
        x_tok[kc] = [t]
        return t

    def operand(yh, yl, kc, n, s, after):
        a = act(yh[:, kc, 0:n], X[:, kc, 0:n], ACT.Copy, [x_tok[kc], after], scale=s)
        l = stt(yl[:, kc, 0:n], X[:, kc, 0:n], s, f32(yh[:, kc, 0:n]), ALU.mult, ALU.subtract, [x_tok[kc], after, a])
        y_tok[kc] = [a, l]

    gate_tok = gain(mul[:, 1, :], GATE_A, 16, v_("g_attn_post", 0, 16), False)
    rm_tok = rms_of_sum(Rm, T, [])
    tsh = mod_chunks(SHIFT_F, 16)
    tsc = gain(mul[:, 2, :], SCALE_F, 16, v_("g_ffn_pre", 0, 16), True)
    y_guard = [(PE.sem, PE.n)]
    th, tl = [], []
    for c in range(T, TQ):
        th.append(act(yh[:, :, c], mod[:, SHIFT_F:SHIFT_F + 16], ACT.Copy, [tsh, y_guard]))
        tl.append(tt(yl[:, :, c], mod[:, SHIFT_F:SHIFT_F + 16], f32(yh[:, :, c]), ALU.subtract, [tsh, th, y_guard]))
    for kc in range(KC):
        add_residual(m1, kc, mul[:, 1, kc:kc + 1], Rm, [rm_tok, gate_tok], m_tok[kc])
        operand(yh, yl, kc, T, mul[:, 2, kc:kc + 1], [tsc, y_guard])
        y_tok[kc] += [th, tl]
        square_in(X[:, kc, 0:T], T, x_tok[kc], kc == 0)
    zr.free[0] = [x_tok[15]]
    r2_tok = rms_of_sum(R2, T, guard1)

    gb4 = Banks([0, 1, 2, 3])
    ab = Banks([4, 5, 6, 7])
    hid_tok = {}
    hid_free = [m_tok[k] for k in range(KC)] + [x_tok[15]]

    def glu_done(conv):
        gate_done = {}

        def done(mat, fb, b, bank, tok):
            if mat in ("gate", "gate2"):
                k, z, fr = zr.take()
                if not conv:
                    t = tt(z[:, 0:T], bank[:, 0:T], R2[:, 0:T], ALU.mult, [tok, r2_tok, fr])
                    c = tc[:, fb % 4:fb % 4 + 1]
                    t2 = V.put(lambda e: e.tensor_copy(c, bank[:, T:T + 1]), [tok, tc_free[fb % 4]])
                    s = act(z[:, 0:T], z[:, 0:T], ACT.Silu, [t, t2], bias=c)
                    tc_free[fb % 4] = [s]
                    give(b, t, t2)
                else:
                    t = tt(z[:, 1:T + 1], bank[:, 0:T], R2[:, 0:T], ALU.mult, [tok, r2_tok, fr])
                    t2 = tt(z[:, 0:1], bank[:, T:T + 1], R2[:, T:T + 1], ALU.mult, [tok, r2_tok, fr])
                    give(b, t, t2)
                    ck, c, cf = cr.take()
                    w = [v_("conv_w_2", FC * i + fb) for i in range(3)]
                    u = ts(c[:, :], z[:, 1:T + 1], w[1], v_("conv_b_2", fb), ALU.mult, ALU.add, [t, cf])
                    u = stt(c[:, :], z[:, 0:T], w[0], c[:, :], ALU.mult, ALU.add, [u, t2])
                    u = stt(c[:, :], z[:, 2:T + 2], w[2], c[:, :], ALU.mult, ALU.add, [u])
                    s = act(z[:, 1:T + 1], c[:, :], ACT.Silu, [u])
                    cr.give(ck, s)
                gate_done[fb] = (k, z, s)
                return
            k, z, s = gate_done.pop(fb)
            uk, u, uf = ur.take()
            c = tc[:, 4 + fb % 4:5 + fb % 4]
            t2 = [] if conv else V.put(lambda e: e.tensor_copy(c, bank[:, T:T + 1]), [tok, tc_free[4 + fb % 4]])
            t = tt(u[:, :], bank[:, 0:T], R2[:, 0:T], ALU.mult, [tok, r2_tok, uf])
            give(b, t, t2)
            hk, h, hf = hr.take()
            if not conv:
                t = stt(h[:, :], u[:, :], c, z[:, 0:T], ALU.add, ALU.mult, [t, t2, s, hf])
                tc_free[4 + fb % 4] = [t]
            else:
                t = tt(h[:, :], u[:, :], z[:, 1:T + 1], ALU.mult, [t, s, hf])
            zr.give(k, t)
            ur.give(uk, t)
            a = act(hidh[:, fb, :], h[:, :], ACT.Copy, [t, hid_free])

            def rest():
                l = tt(hidl[:, fb, :], h[:, :], f32(hidh[:, fb, :]), ALU.subtract, [a, hid_free])
                hr.give(hk, l)
                hid_tok[fb] = [a, l]
            later(1, rest)
        return done

    def y_moving(mat, kc):
        return yh[:, kc, :], yl[:, kc, :], y_tok[kc]

    def hid_moving(mat, kc):
        return hidh[:, kc, :], hidl[:, kc, :], hid_tok[kc]

    for _ in gemm(176, gb4, y_moving, lambda m, f: TQ, glu_done(False)):
        pass
    drain()

    m2 = place([P, KC, T], F32, R0, "m2")
    y_free = [(PE.sem, PE.n)]

    def down_done(mat, fb, b, bank, tok):
        s = square_in(bank[:, 0:T], T, [tok], fb == 0)
        t = act(m2[:, fb, :], bank[:, 0:T], ACT.Copy, [tok, y_free])
        give(b, s, t)
        m_tok[fb] = [t]

    gate_tok = gain(mul[:, 3, :], GATE_F, 16, v_("g_ffn_post", 0, 16), False)
    for _ in gemm(88, gb, hid_moving, lambda m, f: T, down_done):
        pass
    drain()
    rm_tok = rms_of_sum(Rm, T, [zr.free[0]])
    rm_users = []

    B2 = Region(R0)
    B2.at = R0 + 16384
    gh = place([P, KC, TM], F32R, HID, "gh")
    gl = place([P, KC, TM], F32R, HID + 17408, "gl")
    hid_used = [(PE.sem, PE.n)]
    for kc in range(KC):
        add_residual(m2, kc, mul[:, 3, kc:kc + 1], Rm, [rm_tok, gate_tok], m_tok[kc])
        operand(gh, gl, kc, TM, v_("mix_norm_g_2", kc), [hid_used, vec_load, meta_load])
        square_in(X[:, kc, :], TM, [x_tok[kc], meta_load], kc == 0)
    zr.free[0] = [x_tok[15]]
    r2_tok = rms_of_sum(R2, TM, [hid_tok[FC - 1]])

    TD = TM - T
    guard2 = [(V.sem, V.n), (A.sem, A.n), (PE.sem, PE.n), (G.sem, G.n)]
    RA = Region(R0, R0 + 33024)
    kn = RA([P, 8, TM], F32, "kn")
    qn = RA([P, 8, TQ], F32, "qn")
    vm = RA([P, 3, 1024], F32, "vm")
    cs2 = RA([P, 2, TM], F32, "cs2")
    kpr = RA([P, TM], F32, "kpr")
    mb2 = RA([P, 8, TD], F32, "mb2")
    outa = place([P, 8, TQ], F32, R0, "outa")
    RB = Region(HID + 34816, TMP)
    krz = RB([P, 8, TM], F32, "krz")
    qr = RB([P, 4, TQ], F32, "qr")
    b_at = RB.at
    cq = RB([P, 4, TQ], F32, "cq")
    ckv = RB([P, 2, TM], F32, "ckv")
    cqh = RB([P, 4, TQ], F32R, "cqh")
    cql = RB([P, 4, TQ], F32R, "cql")
    ckh = RB([P, 2, TM], F32R, "ckh")
    ckl = RB([P, 2, TM], F32R, "ckl")
    mbh = place([P, 8, TQ], F32R, b_at, "mbh")
    mbl = place([P, 8, TQ], F32R, b_at + 8256, "mbl")
    naq = [RB([P, TQ], F32, "naq") for _ in range(3)]
    nak = [RB([P, TM], F32, "nak") for _ in range(3)]
    nav = [RB([P, 3, P], F32, "nav") for _ in range(3)]
    bt = Ring([RB([P, 2, TM], F32, "bt")])
    kpsq = place([P, TM], F32, RB.at, "kpsq")
    tz = Ring([RB([P, 6, 64], F32, "tz")])
    revt = RB([P, P], F32, "revt")
    er2 = Ring([RB([P, 2, TM], F32, "er2") for _ in range(2)])
    em = Ring([RB([P, TM], F32, "em")])
    tmpr = Ring([RB([P, TM], F32, "tmp") for _ in range(2)])
    RC = Region(TMP + 3 * 1088, LIMIT - 1088)
    pt2 = Ring([RC([P, 3, TQ], F32, "pt2") for _ in range(2)])
    rhr = Ring([RC([P, TM], F32, "rh") for _ in range(2)])
    mah = place([P, 8, TQ], F32R, HID, "mah")
    mal = place([P, 8, TQ], F32R, HID + 8256, "mal")
    for ring in (bt, tz, er2, em, tmpr, pt2, rhr):
        for k in ring.free:
            ring.free[k] = list(guard2)
    nar = Ring([0, 1, 2], {k: list(guard2) for k in range(3)})

    zero2 = [memset(krz[:, :, :], 0.0, guard2), memset(vm[:, 2, :], 0.0, guard2)]
    zero2 += [memset(b[:, :, :], 0.0, guard2) for b in pt2.items]
    zero2 += [memset(b[:, 2, :], 0.0, guard2) for b in nav]
    cs_load = load(cs2[:, :, :], rope2, "ld_rope2", after=guard2)
    rev_load = load(revt[:, :], rev, "ld_rev", after=guard2)
    mb_load = load(mb2[:, :, :], bass.AP(mbias.tensor, 0, [[0, P], [1, 8 * TD]]), "ld_mb", after=guard2)
    naq_gain = small[:, 3:4]
    ng_tok = ts(naq_gain, v_("na_q_g_2"), float(128 ** -0.5), None, ALU.mult, None, [vec_load], G)
    SM = float(192 ** -0.5)

    tz_sem = [sem(f"tz{i}") for i in range(2)]

    def bias_load(h):
        k, Z, fr = tz.take()
        toks = []
        for a in range(2):
            src = bass.AP(rpb.tensor, (h * 15 + 4 + a) * RPB_ROW + 16, [[1, 64], [RPB_ROW, 6], [1, 64]])
            SP.put(lambda q, a=a, src=src: q.dma_start(Z[64 * a:64 * a + 64, :, :], src).then_inc(tz_sem[a], 16), fr, signal=False)
            toks.append((tz_sem[a], 16 * (h + 1)))
        return k, Z, toks

    def bias_tile(h):
        zk, Z, ztok = B_["tz", h]
        b, bank, free = ab.take()
        p = mm(bank[:, 0:384], revt[:, :], Z[:, :, :].rearrange("p j c -> p (j c)"), True, True, [free, ztok, rev_load], signal=True)
        tz.give(zk, p)
        if h + 1 < 8:
            B_["tz", h + 1] = bias_load(h + 1)
        k, B, fr = bt.take()
        mask = namask.unsqueeze(1).to_broadcast([P, 4, 64])
        toks = []
        for qb in range(2):
            src = bank[:, 128 - 128 * qb:384 - 128 * qb].rearrange("p (j c) -> p j c", j=4)
            toks.append(tt(B[:, qb, 0:T].rearrange("p (j c) -> p j c", j=4), src, mask, ALU.add, [p, fr]))
        give(b, toks)
        toks.append(G.put(lambda e: e.tensor_copy(B[:, :, T:TM], mb2[:, h, :].unsqueeze(1).to_broadcast([P, 2, TD])), [mb_load, fr]))
        return k, B, toks

    def head_rms(sq, n, after, div):
        b, bank, free = ab.take()
        t = mm(bank[:, 0:n], ones[:, :], sq[:, 0:n], True, True, [free, after], signal=True)
        k, R, fr = rhr.take()
        a, e = rms(R[:, 0:n], bank[:, 0:n], div, [t, fr])
        give(b, a)
        return k, R, t, e

    def rotate2(dst, n, after):
        k, a, fr = tmpr.take()
        t = tt(a[:, 0:n], dst, cs2[:, 1, 0:n], ALU.mult, [after, fr, cs_load], G)
        u = tt(dst, dst, cs2[:, 0, 0:n], ALU.mult, [after, t, cs_load], G)
        b, bank, free = ab.take()
        p = mm(bank[:, 0:n], swap, a[:, 0:n], True, True, [free, t], signal=True)
        tmpr.give(k, p)
        r = tt(dst, bank[:, 0:n], dst, ALU.add, [p, u])
        give(b, r)
        return r

    B_ = {}
    gains = {"mixed": [vec_load]}

    def cq_done(mat, fb, b, bank, tok):
        if fb < CKV:
            i = fb - CQ
            t = tt(cq[:, i, :], bank[:, 0:TQ], R2[:, 0:TQ], ALU.mult, [tok, r2_tok, guard2])
            give(b, t)
            square_in(cq[:, i, :], TQ, [t], i == 0)
            B_["cq", i] = t
            if i == 3:
                def f():
                    k, R, fr = rhr.take()
                    e = rms_of_sum(R, TQ, [fr], 512)
                    last = []
                    for i in range(4):
                        t = stt(cq[:, i, :], cq[:, i, :], v_("mla_cq_g_2", i), R[:, 0:TQ], ALU.mult, ALU.mult, [e, B_["cq", i]])
                        a = act(cqh[:, i, :], cq[:, i, :], ACT.Copy, [t, guard2])
                        l = tt(cql[:, i, :], cq[:, i, :], f32(cqh[:, i, :]), ALU.subtract, [t, a])
                        B_["cqn", i] = [a, l]
                        last.append(t)
                    rhr.give(k, last)
                later(2, f)
        elif fb < KPE:
            i = fb - CKV
            t = tt(ckv[:, i, :], bank[:, 0:TM], R2[:, :], ALU.mult, [tok, r2_tok, guard2])
            give(b, t)
            square_in(ckv[:, i, :], TM, [t], i == 0)
            B_["ckv", i] = t
            if i == 1:
                def f():
                    k, R, fr = rhr.take()
                    e = rms_of_sum(R, TM, [fr], 256)
                    last = []
                    for i in range(2):
                        t = stt(ckv[:, i, :], ckv[:, i, :], v_("mla_ckv_g_2", i), R[:, :], ALU.mult, ALU.mult, [e, B_["ckv", i]])
                        a = act(ckh[:, i, :], ckv[:, i, :], ACT.Copy, [t, guard2])
                        l = tt(ckl[:, i, :], ckv[:, i, :], f32(ckh[:, i, :]), ALU.subtract, [t, a])
                        B_["ckn", i] = [a, l]
                        last.append(t)
                    rhr.give(k, last)
                later(1, f)
        else:
            t = tt(kpr[:, :], bank[:, 0:TM], R2[:, :], ALU.mult, [tok, r2_tok, guard2])
            give(b, t)
            s = act(kpsq[:, :], kpr[:, :], ACT.Square, [t, guard2])
            s = ts(kpsq[:, :], kpsq[:, :], 0.5, None, ALU.mult, None, [s], G)
            B_["kpsq"] = s
            t = ts(kpr[:, :], kpr[:, :], v_("mk_r"), None, ALU.mult, None, [t, s])

            def f():
                B_["kpr"] = rotate2(kpr[:, :], TM, [t])
            later(1, f)

    def g_moving(mat, kc):
        return gh[:, kc, :], gl[:, kc, :], y_tok[kc]

    def in2_width(mat, fb):
        return TQ if fb < KA or CQ <= fb < CKV else TM

    def chain(mat, fb, b, bank, tok):
        cq_done(mat, fb, b, bank, tok)

    def first_then(n):
        for x in gemm(8, gb4, g_moving, in2_width, chain):
            yield x

    for _ in first_then(8):
        pass
    ab = Banks([3, 4, 5, 6, 7])
    for _ in gemm(6, gb, g_moving, in2_width, chain):
        pass

    def q_done(mat, fb, b, bank, tok):
        p, r = divmod(fb, 3)
        if r == 0:
            t = ts(qr[:, p, :], bank[:, 0:TQ], v_("mq_r"), None, ALU.mult, None, [tok, guard2])
            k, s, fr = tmpr.take()
            a = act(s[:, 0:TQ], bank[:, 0:TQ], ACT.Square, [t, fr])
            give(b, a)
            B_["sqr", p] = (k, s, a)

            def f():
                B_["qr", p] = rotate2(qr[:, p, :], TQ, [t])
            later(1, f)
            return
        h = 2 * p + r - 1
        t = V.put(lambda e: e.tensor_copy(qn[:, h, :], bank[:, 0:TQ]), [tok, guard2])
        give(b, t)
        k, sq, fr = sqf.take()
        a = act(sq[:, 0:TQ], qn[:, h, :], ACT.Square, [t, fr])
        half = slice(64 * (h % 2), 64 * (h % 2) + 64)
        rk, rs, ra = B_["sqr", p]
        t2 = tt(sq[half, 0:TQ], sq[half, 0:TQ], rs[half, 0:TQ], ALU.add, [a, ra])
        if r == 2:
            tmpr.give(rk, t2, B_["rs0"])
        B_["rs0"] = t2

        def f():
            k2, R, t3, e = head_rms(sq, TQ, [t2], 192)
            sqf.give(k, t3)
            u = stt(qn[:, h, :], qn[:, h, :], v_("mq_n"), R[:, 0:TQ], ALU.mult, ALU.mult, [e])
            w = tt(qr[half, p, :], qr[half, p, :], R[half, 0:TQ], ALU.mult, [e, B_["qr", p]])
            rhr.give(k2, u, w)
            B_["q", h] = [u, w]
        later(1, f)

    def k_done(mat, fb, b, bank, tok):
        h, r = divmod(fb, 2)
        if r == 0:
            t = V.put(lambda e: e.tensor_copy(kn[:, h, :], bank[:, 0:TM]), [tok, guard2])
            give(b, t)
            k, sq, fr = sqf.take()
            a = act(sq[:, :], kn[:, h, :], ACT.Square, [t, fr])
            t2 = tt(sq[:, :], sq[:, :], kpsq[:, :], ALU.add, [a, B_["kpsq"]], G)
            half = slice(64 * (h % 2), 64 * (h % 2) + 64)
            B_["kpsq_used"] = t2

            def f():
                k2, R, t3, e = head_rms(sq, TM, [t2], 192)
                sqf.give(k, t3)
                u = stt(kn[:, h, :], kn[:, h, :], v_("mk_n"), R[:, :], ALU.mult, ALU.mult, [e])
                w = tt(krz[half, h, :], kpr[half, :], R[half, :], ALU.mult, [e, B_["kpr"], zero2])
                rhr.give(k2, u, w)
                B_["k", h] = [u, w]
            later(1, f)
            return
        k, v, fr = tmpr.take()
        t = act(v[:, :], bank[:, 0:TM], ACT.Copy, [tok, fr])
        give(b, t)

        def f():
            c = slice(P * h, P * h + P)
            p, e = values(v, t, vm[:, 0:2, c], vm[0:16, 2, c])
            tmpr.give(k, p)
            B_["v", h] = e
        later(1, f)

    def values(v, after, dst, dst_meta):
        b, bank, free = ab.take()
        tr(bank[:, 0:P], v[:, 0:P], [free, after])
        tr(bank[:, P:2 * P], v[:, P:2 * P])
        p = tr(bank[0:TD, 2 * P:3 * P], v[:, T:TM], signal=True)
        e0 = act(dst, bank[:, 0:2 * P].rearrange("p (k d) -> p k d", k=2), ACT.Copy, [p, guard2])
        e1 = act(dst_meta, bank[0:TD, 2 * P:3 * P], ACT.Copy, [p, zero2])
        give(b, e0, e1)
        return p, [e0, e1]

    def cq_moving(mat, kc):
        return cqh[:, kc, :], cql[:, kc, :], B_["cqn", kc]

    def ck_moving(mat, kc):
        return ckh[:, kc, :], ckl[:, kc, :], B_["ckn", kc]

    for _ in gemm(6, gb, cq_moving, lambda m, f: TQ, q_done):
        pass
    for _ in gemm(4, gb, ck_moving, lambda m, f: TM, k_done):
        pass
    kv_done_pe = [(PE.sem, PE.n)]

    def softmax_rest(h, d):
        E, M, c, mk = d["E"], d["M"], d["c"], d["mk"]
        t = V.put(lambda e: e.reciprocal(stat[:, c:c + 2], stat[:, c + 3:c + 5]), [d["es"][0:2]])
        t2 = V.put(lambda e: e.reciprocal(stat[0:1, c + 2:c + 3], stat[0:1, c + 5:c + 6]), [d["es"][2]])
        ns = [ts(E[:, qb, :], E[:, qb, :], stat[:, c + qb:c + qb + 1], None, ALU.mult, None, [t]) for qb in range(2)]
        ns.append(ts(M[0:1, mk], M[0:1, mk], stat[0:1, c + 2:c + 3], None, ALU.mult, None, [t2]))
        b, bank, free = ab.take()
        for kc in range(2):
            for qb in range(2):
                p = tr(bank[:, T * kc + P * qb:T * kc + P * qb + P], E[:, qb, P * kc:P * kc + P], [free, ns[qb]],
                       signal=(kc == 1 and qb == 1))
        b2, bank2, free2 = ab.take()
        for qb in range(2):
            tr(bank2[0:TD, P * qb:P * qb + P], E[:, qb, T:TM], [free2])
        full = mk.stop > TD
        if full:
            for kc in range(2):
                tr(bank2[:, T + kc:T + kc + 1], M[0:1, P * kc:P * kc + P], [ns[2]])
            p2 = tr(bank2[0:TD, T + 2:T + 3], M[0:1, T:TM], signal=True)
        else:
            p2 = tr(bank2[0:TD, T + 2:T + 3], M[0:1, 0:TD], [ns[2]], signal=True)
        er2.give(d["er"], p2)
        em.give(d["emk"], p2)
        r, buf, fr = pt2.take()
        es = [act(buf[:, 0:2, 0:T], bank[:, :].rearrange("p (k q) -> p k q", k=2), ACT.Copy, [p, fr, zero2])]
        give(b, es[0])
        es.append(act(buf[0:TD, 2, 0:T], bank2[0:TD, 0:T], ACT.Copy, [p2, fr, zero2]))
        es.append(act(buf[0:TD, 2, T:T + 1], bank2[0:TD, T + 2:T + 3], ACT.Copy, [p2]))
        if full:
            es.append(act(buf[:, 0:2, T:T + 1], bank2[:, T:T + 2].unsqueeze(2), ACT.Copy, [p2]))
        give(b2, es[1:])
        d.update(pr=r, buf=buf, ps=es)

    def out_of(d, dst, after, first):
        b, bank, p = d["ob"]
        s = square_in(bank[:, 0:TQ], TQ, [p], first)
        a = act(dst, bank[:, 0:TQ], ACT.Copy, [p, after])
        give(b, s, a)
        return a

    mla, na = {}, {}

    def exps(d):
        E, M, c, mk, vs = d["E"], d["M"], d["c"], d["mk"], d["vs"]
        es = [act(E[:, qb, :], E[:, qb, :], ACT.Exp, [vs[qb]], scale=-1.0, bias=stat[:, c + qb:c + qb + 1],
                  accum_out=stat[:, c + 3 + qb:c + 4 + qb]) for qb in range(2)]
        es.append(act(M[0:1, mk], M[0:1, mk], ACT.Exp, [vs[2]], scale=-1.0, bias=stat[0:1, c + 2:c + 3],
                      accum_out=stat[0:1, c + 5:c + 6]))
        d["es"] = es

    def mla_steps():
        def s0(h):
            while not all((k, h) in B_ for k in ("q", "k", "v")):
                yield
            er, E, fr = er2.take()
            emk, M, fr2 = em.take()
            c = 8 * (h % 4)
            vs = []
            for i, q in enumerate((slice(0, P), slice(P, T), slice(T, T + 1))):
                b, bank, free = ab.take()
                m = 1 if i == 2 else P
                mm(bank[0:m, 0:TM], qn[:, h, q], kn[:, h, :], True, False, [free, B_["q", h], B_["k", h]])
                p = mm(bank[0:m, 0:TM], qr[:, h // 2, q], krz[:, h, :], False, True, signal=True)
                dst = M[0:1, :] if i == 2 else E[:, i, :]
                f2 = fr2 if i == 2 else fr
                v = ts(dst, bank[0:m, 0:TM], -SM, None, ALU.mult, ALU.min, [p, f2], accum_out=stat[0:m, c + i:c + i + 1])
                give(b, v)
                vs.append(v)
            d = mla[h] = dict(E=E, M=M, c=c, mk=slice(0, TM), vs=vs, er=er, emk=emk)
            exps(d)

        def s1(h):
            softmax_rest(h, mla[h])

        def s2(h):
            d = mla[h]
            b, bank, free = ab.take()
            for kc in range(3):
                p = mm(bank[:, 0:TQ], vm[:, kc, P * h:P * h + P], d["buf"][:, kc, :], kc == 0, kc == 2,
                       [free, d["ps"], B_["v", h]], signal=(kc == 2))
            pt2.give(d["pr"], p)
            d["ob"] = (b, bank, p)
            B_["outb", h] = out_of(d, qn[:, h, :], [p], h == 0)

        yield from lock([s0, s1, s2], 8)
        yield
        k, R, fr = rhr.take()
        e = rms_of_sum(R, TQ, [fr], 1024)
        yield
        for h in range(8):
            t = stt(qn[:, h, :], qn[:, h, :], v_("mla_out_g_2", h), R[:, 0:TQ], ALU.mult, ALU.mult, [e, B_["outb", h]])
            a = act(mbh[:, h, :], qn[:, h, :], ACT.Copy, [t, kv_done_pe])
            l = tt(mbl[:, h, :], qn[:, h, :], f32(mbh[:, h, :]), ALU.subtract, [t, a, kv_done_pe])
            B_["mix", 8 + h] = [a, l]
            if h % 2:
                yield
        rhr.give(k, t)
        B_["mla"] = True

    def na_done(mat, fb, b, bank, tok):
        kind, h = divmod(fb, 8)
        if kind == 0:
            force(lambda: nar.free[nar.i] is not None)
            k, _, fr = nar.take()
            B_["na", h] = (k, fr)
        k, fr = B_["na", h]
        n = TQ if kind == 0 else TM
        if kind < 2:
            dst = (naq, nak)[kind][k]
            t = tt(dst[:, :], bank[:, 0:n], R2[:, 0:n], ALU.mult, [tok, r2_tok, fr])
            give(b, t)
            sk, sq, sf = sqf.take()
            a = act(sq[:, 0:n], dst[:, :], ACT.Square, [t, sf])

            def f():
                k2, R, t3, e = head_rms(sq, n, [a], 128)
                sqf.give(sk, t3)
                g = naq_gain if kind == 0 else v_("na_k_g_2")
                u = stt(dst[:, :], dst[:, :], g, R[:, 0:n], ALU.mult, ALU.mult, [e, ng_tok])
                rhr.give(k2, u)
                B_["naqk"[0:2] + str(kind), h] = u
            later(1, f)
            return
        tk, v, tf = tmpr.take()
        t = tt(v[:, :], bank[:, 0:TM], R2[:, :], ALU.mult, [tok, r2_tok, tf])
        give(b, t)
        B_["r2_used"] = t

        def f():
            p, e = values(v, [t, fr], nav[k][:, 0:2, :], nav[k][0:TD, 2, :])
            tmpr.give(tk, p)
            B_["nav", h] = e
        later(1, f)

    def na_steps():
        def s0(h):
            while not (("nav", h) in B_ and "mla" in B_):
                yield
            k, fr = B_["na", h]
            bk, B, btok = bias_tile(h)
            er, E, fr = er2.take()
            emk, M, fr2 = em.take()
            c = 8 * (h % 4)
            vs = []
            for i, q in enumerate((slice(0, P), slice(P, T), slice(T, T + 1))):
                b, bank, free = ab.take()
                toks = [free, B_["na0", h], B_["na1", h]]
                if i < 2:
                    p = mm(bank[:, 0:TM], naq[k][:, q], nak[k][:, :], True, True, toks, signal=True)
                    v = ttr(E[:, i, :], bank[:, 0:TM], B[:, i, :], -1.0, BIG, ALU.add, ALU.min, stat[:, c + i:c + i + 1],
                            [p, btok, fr])
                else:
                    p = mm(bank[0:1, 0:TD], naq[k][:, q], nak[k][:, T:TM], True, True, toks, signal=True)
                    v = ttr(M[0:1, 0:TD], bank[0:1, 0:TD], B[0:1, 0, T:TM], -1.0, BIG, ALU.add, ALU.min,
                            stat[0:1, c + i:c + i + 1], [p, btok, fr2])
                give(b, v)
                vs.append(v)
            bt.give(bk, vs)
            d = na[h] = dict(E=E, M=M, c=c, mk=slice(0, TD), vs=vs, er=er, emk=emk)
            exps(d)

        def s1(h):
            softmax_rest(h, na[h])

        def s2(h):
            d = na[h]
            k, _ = B_["na", h]
            b, bank, free = ab.take()
            mm(bank[:, 0:TQ], nav[k][:, 2, :], d["buf"][:, 2, :], True, False, [free, d["ps"], B_["nav", h]])
            for kc in range(2):
                p = mm(bank[:, 0:T], nav[k][:, kc, :], d["buf"][:, kc, 0:T], False, kc == 1, signal=(kc == 1))
            pt2.give(d["pr"], p)
            nar.give(k, p)
            d["ob"] = (b, bank, p)
            B_["outa", h] = out_of(d, outa[:, h, :], [B_["outb", 7]], h == 0)

        yield from lock([s0, s1, s2], 8)
        yield
        k, R, fr = rhr.take()
        e = rms_of_sum(R, TQ, [fr], 1024)
        yield
        for h in range(8):
            t = stt(outa[:, h, :], outa[:, h, :], v_("na_out_g_2", h), R[:, 0:TQ], ALU.mult, ALU.mult, [e, B_["outa", h]])
            a = act(mah[:, h, :], outa[:, h, :], ACT.Copy, [t, in2_pe])
            l = tt(mal[:, h, :], outa[:, h, :], f32(mah[:, h, :]), ALU.subtract, [t, a, in2_pe])
            B_["mix", h] = [a, l]
            if h % 2:
                yield
        rhr.give(k, t)

    sides = []

    def step_sides():
        for s in list(sides):
            if next(s, "end") == "end":
                sides.remove(s)

    def force(cond):
        n = 0
        while not cond():
            step_sides()
            n += 1
            assert n < 200, "stuck"

    def run_with(main, rate):
        credit = 0.0
        for _ in main:
            credit += rate
            while credit >= 1.0:
                credit -= 1.0
                step_sides()

    in2_pe = []
    sides += [mla_steps(), na_steps()]
    tz.free[0] = [guard2, B_["kpsq_used"]]
    B_["tz", 0] = bias_load(0)
    run_with(gemm(48, gb, g_moving, in2_width, na_done), 0.8)
    in2_pe.append((PE.sem, PE.n))
    drain()
    force(lambda: "mla" in B_)

    halves["out2"] = 8

    def mix_moving(mat, kc):
        return (mbh[:, kc - 8, :], mbl[:, kc - 8, :], B_["mix", kc]) if kc >= 8 else (mah[:, kc, :], mal[:, kc, :], B_["mix", kc])

    def out_first(mat, fb, b, bank, tok):
        t = tt(X[:, fb, 0:TQ], bank[:, 0:TQ], X[:, fb, 0:TQ], ALU.add, [tok, x_tok[fb]])
        give(b, t)
        x_tok[fb] = [t]

    run_with(gemm(16, gb, mix_moving, lambda m, f: TQ, out_first), 1.0)
    n = 0
    while sides:
        step_sides()
        tick()
        n += 1
        assert n < 500
    guard3 = [(V.sem, V.n), (A.sem, A.n), (PE.sem, PE.n), (G.sem, G.n)]
    for ring in (zr, ur, hr, cr):
        for k in ring.free:
            ring.free[k] = list(guard3)

    def out_second(mat, fb, b, bank, tok):
        t = tt(X[:, fb, 0:TQ], bank[:, 0:TQ], X[:, fb, 0:TQ], ALU.add, [tok, x_tok[fb]])
        give(b, t)
        x_tok[fb] = [t]
        operand(yh, yl, fb, TQ, v_("ffn_norm_g_2", fb), [guard3])
        square_in(X[:, fb, 0:TQ], TQ, [t], fb == 0)

    run_with(gemm(16, gb, mix_moving, lambda m, f: TQ, out_second), 1.0)
    halves.clear()
    r2_tok = rms_of_sum(R2, TQ, [B_["r2_used"]])
    for i in range(2):
        zt = memset(zr.items[i][:, TQ - 1:TQ], 0.0, guard3)
        zr.free[i] = [guard3, zt]

    ab = Banks([4, 5, 6, 7])
    hid_free = [(PE.sem, PE.n), (A.sem, A.n)]
    for _ in gemm(176, gb4, y_moving, lambda m, f: TQ if m == "gate2" else T, glu_done(True)):
        pass
    drain()

    oring2 = [ur.items[0], ur.items[1], hr.items[0], hr.items[1]]
    ofree = [ur.free[0], ur.free[1], hr.free[0], hr.free[1]]
    osem = [sem(f"out{i}") for i in range(4)]
    ocount = [0] * 4

    def last_done(mat, fb, b, bank, tok):
        k = fb % 4
        o, s = oring2[k], osem[k]
        t = tt(o[:, :], bank[:, 0:T], X[:, fb, 0:T], ALU.add, [tok, x_tok[fb], ofree[k]])
        give(b, t)
        SP.put(lambda q: q.dma_start(out[:, fb, :], o[:, :]).then_inc(s, 16), [t], signal=False)
        ocount[k] += 16
        ofree[k] = [(s, ocount[k])]

    for _ in gemm(88, gb, hid_moving, lambda m, f: T, last_done):
        pass
    assert not st["ready"] and st["done"] == len(plan)
    out_sems = [(osem[k], ocount[k]) for k in range(4)]

    with nc.Block() as block:
        @block.sync
        def _(e):
            SP.emit(e)
            for s, v in out_sems:
                e.wait_ge(s, v)

        @block.tensor
        def _(e):
            PE.emit(e)

        @block.vector
        def _(e):
            V.emit(e)

        @block.scalar
        def _(e):
            A.emit(e)

        @block.gpsimd
        def _(e):
            G.emit(e)


def layout(inputs):
    g = {k: np.asarray(v) for k, v in inputs.items()}

    def part(name, n=None):
        return np.asarray(g[name]).reshape(-1, P).T

    def rows(a):
        return a.T.reshape(KC, P, -1).transpose(1, 0, 2)

    n, r = 128, 64
    conv = g["conv_w_2"][0].reshape(3, FC, P).transpose(2, 0, 1).reshape(P, 3 * FC)
    mq, mk = g["mla_q_g_2"][0], g["mla_k_g_2"][0]
    vec = {"conv_w_2": conv, "mq_n": mq[:n, None], "mk_n": mk[:n, None],
           "mq_r": np.concatenate([mq[n:], mq[n:]])[:, None], "mk_r": np.concatenate([mk[n:], mk[n:]])[:, None]}
    vecs = np.concatenate([vec[k] if k in vec else part(k) for k, _ in VECS], axis=1)
    assert vecs.shape == (P, NVEC)

    w_in = g["w_in"][0]
    w_ada = g["w_ada"][0]
    w_in2 = g["w_in_2"][0]
    kpe = w_in2[:, 3840:3904]
    qup = g["w_q_up_2"][0].reshape(512, 8, 192)
    qcols = []
    for p in range(4):
        a, b = qup[:, 2 * p], qup[:, 2 * p + 1]
        qcols += [a[:, n:], b[:, n:], a[:, :n], b[:, :n]]
    mats = {"o": g["w_o"][0], "gate": g["w_gate"][0], "up": g["w_up"][0], "down": g["w_down"][0],
            "in2": np.concatenate([w_in2, kpe], axis=1), "qup": np.concatenate(qcols, axis=1), "kvup": g["w_kv_up_2"][0],
            "out2": g["w_out_2"][0], "gate2": g["w_gate_2"][0], "up2": g["w_up_2"][0], "down2": g["w_down_2"][0]}
    plan = tile_plan()
    wst = np.zeros((len(plan), P, TILE), np.float32)
    for t, what in enumerate(plan):
        if what[0] == "a":
            c, h = divmod(what[1], 2)
            wst[t] = w_ada[1024 * h:1024 * (h + 1), P * c:P * (c + 1)].T
        elif what[0] == "x":
            _, grp, kp = what
            d = wst[t].reshape(P, 2, 512)
            for i in range(2):
                at = 0
                for a, b in W_IN_GROUPS[grp]:
                    d[:, i, at:at + b - a] = w_in[(2 * kp + i) * P:(2 * kp + i + 1) * P, a:b]
                    at += b - a
        else:
            for i, (m, kc, fb) in enumerate(what[1]):
                wst[t, :, P * i:P * (i + 1)] = mats[m][kc * P:(kc + 1) * P, fb * P:(fb + 1) * P]

    meta = np.concatenate([g["meta_tokens_2"][15:], g["meta_tokens_2"][:15]])
    rpb = np.zeros((8, 15, RPB_ROW), np.float32)
    rpb[:, :, 64:95] = g["na_rpb_2"][0]
    mb = g["na_meta_bias_2"][0]
    mbias = np.concatenate([mb[:, 15:], mb[:, :15]], axis=1)

    ident = np.eye(P, dtype=np.float32)
    swap = np.zeros((P, P), np.float32)
    for hd in (0, 64):
        for j in range(32):
            swap[hd + 32 + j, hd + j] = -1.0
            swap[hd + j, hd + 32 + j] = 1.0
    q, k = np.arange(P)[:, None], np.arange(P)[None, :]
    causal = np.concatenate([np.zeros((P, P)), np.where(k <= q, 0.0, NEG)], axis=1)
    c = np.arange(P) % 64
    start = np.clip(c - 8, 0, 48)[:, None]
    kk = np.arange(64)[None, :]
    namask = np.where((kk >= start) & (kk < start + 16), 0.0, NEG)
    inv = np.power(np.float32(500000.0), -(np.arange(0, 32, 2, dtype=np.float32) / np.float32(32)))
    freq = np.broadcast_to(inv, (P, 16))
    consts = np.concatenate([ident, swap, causal, namask, freq], axis=1).astype(np.float32)
    inv2 = np.power(np.float32(10000.0), -np.arange(0, 64, 2, dtype=np.float32) / np.float32(64)).astype(np.float32)
    posn = np.concatenate([np.arange(16, 272), [15], np.arange(15)]).astype(np.float32)
    angle = (posn[None, :] * inv2[np.arange(P) % 32][:, None]).astype(np.float32)
    rope2 = np.stack([np.cos(angle), np.sin(angle)], axis=1).astype(np.float32)

    return {"wst": wst, "xT": rows(g["x"][0]), "metaT": rows(meta), "vecs": vecs, "consts": consts, "rope2": rope2, "rev": ident[::-1],
            "cvec": g["c"], "positions": g["positions"][0].reshape(2, P).T,
            "lambdas": np.concatenate([g["lambda_q1"], g["lambda_k1"], g["lambda_q2"], g["lambda_k2"]]),
            "rpb": rpb, "mbias": mbias}


def kernel(**inputs):
    import concourse.bacc as bacc
    from concourse.bass_utils import run_bass_kernel_spmd

    nc = bacc.Bacc("TRN2", target_bir_lowering=False, num_devices=1)
    arrays = {f"in_{k}": np.ascontiguousarray(a) for k, a in layout(inputs).items()}
    args = [nc.dram_tensor(k, a.shape, mybir.dt.from_np(a.dtype), kind="ExternalInput").ap() for k, a in arrays.items()]
    args.append(nc.dram_tensor("out_0", (P, KC, T), F32, kind="ExternalOutput").ap())
    build(nc, *args)
    r = run_bass_kernel_spmd(nc, [arrays], core_ids=[0])
    got = r.results[0]["out_0"]
    return np.ascontiguousarray(got.transpose(2, 1, 0).reshape(1, T, KC * P))
```

```python
from contextlib import ExitStack

import numpy as np

import concourse.bass as bass
from concourse import mybir

F32 = mybir.dt.float32
F32R = mybir.dt.float32r
I32 = mybir.dt.int32
ALU = mybir.AluOpType
ACT = mybir.ActivationFunctionType

P = 128
T = 256
TM = 272
TQ = 258
KC = 16
FC = 44
FP = 36
NEG = -1.0e30
USED = -3.0e38
BIG = 3.0e38
TILE = 1024

SHIFT_A, SCALE_A, GATE_A, SHIFT_F, SCALE_F, GATE_F = range(0, 96, 16)

W_IN_GROUPS = [
    [(4352, 4864)],
    [(4864, 5376)],
    [(5376, 5440), (5376, 5440), (4096, 4224), (4224, 4352), (5440, 5456)],
    [(1024, 1536)],
    [(2048, 2560)],
    [(0, 512)],
    [(1536, 2048)],
    [(2560, 3072)],
    [(512, 1024)],
    [(3072, 3584)],
    [(3584, 4096)],
]
G_COLS = [sum(b - a for a, b in g) for g in W_IN_GROUPS]
IQ0, IQ1, IKS, DK0, DV0, DQ0, DK1, DV1, DQ1, SQ0, SQ1 = range(11)
PASSES = [(0, 2), (2, 6), (6, 10), (10, 16)]

QA, KA, VA, CQ, CKV, KPE = 0, 8, 16, 24, 28, 30

KCHUNKS = {"o": 16, "gate": 16, "up": 16, "down": 44, "in2": 16, "qup": 4, "kvup": 2,
           "out2": 16, "gate2": 16, "up2": 16, "down2": 44}

VECS = [("b_ada", 96), ("g_attn_pre", 16), ("g_attn_post", 16), ("g_ffn_pre", 16), ("g_ffn_post", 16),
        ("mix_norm_g_2", 16), ("ffn_norm_g_2", 16), ("conv_w_2", 132), ("conv_b_2", 44),
        ("na_q_g_2", 1), ("na_k_g_2", 1), ("g_diff_sub", 1), ("mla_cq_g_2", 4), ("mla_ckv_g_2", 2),
        ("mq_n", 1), ("mq_r", 1), ("mk_n", 1), ("mk_r", 1), ("na_out_g_2", 8), ("mla_out_g_2", 8)]
VOFF = {}
for _name, _n in VECS:
    VOFF[_name] = sum(n for _, n in VECS[:len(VOFF)])
NVEC = sum(n for _, n in VECS)

CONSTS = [("ident", 128), ("swap", 128), ("causal", 256), ("namask", 64), ("freq", 16)]
COFF = {}
for _name, _n in CONSTS:
    COFF[_name] = sum(n for _, n in CONSTS[:len(COFF)])
NCONST = sum(n for _, n in CONSTS)
RPB_ROW = 160


def spread(main, extra, share=1.0):
    out, done = [], 0
    for i, m in enumerate(main):
        out.append(m)
        upto = min(len(extra), round((i + 1) * len(extra) / (len(main) * share)))
        out += extra[done:upto]
        done = max(done, upto)
    return out + extra[done:]


def blocks(mat, order):
    order = [(mat, kc, fb) for kc, fb in order] if isinstance(mat, str) else order
    assert len(order) % 8 == 0, (mat, len(order))
    return [("b", tuple(order[i:i + 8])) for i in range(0, len(order), 8)]


def tile_plan():
    def ada(c0, n):
        return [("a", 2 * c + h) for c in range(c0, c0 + n) for h in range(2)]

    def ada_pass(k0, k1):
        return ada(SHIFT_A + k0, k1 - k0) + ada(SCALE_A + k0, k1 - k0)

    plan = ada_pass(*PASSES[0])
    for i, (k0, k1) in enumerate(PASSES):
        tiles = [("x", g, kp) for g in range(11) for kp in range(k0 // 2, k1 // 2)]
        nxt = ada_pass(*PASSES[i + 1]) if i + 1 < len(PASSES) else ada(GATE_A, 8)
        plan += spread(tiles, nxt, 0.8)
    o = blocks("o", [(kc, fb) for fb in range(16) for kc in range(8)])
    o += blocks("o", [(kc, fb) for fb in range(16) for kc in range(8, 16)])
    plan += spread(o, ada(SHIFT_F, 8) + ada(SCALE_F, 8), 0.9)

    def glu(g, u):
        first = [(m, kc, fb) for kc in range(16) for m, fb in ((g, 0), (u, 0), (g, 1), (u, 1))]
        rest = [(m, kc, fb) for fb in range(2, FC) for m in (g, u) for kc in range(16)]
        return blocks(None, first + rest)

    part = [(m, kc, fb) for kc in range(8) for m, fb in (("gate", 0), ("up", 0), ("gate", 1), ("up", 1))]
    part += [(m, kc, fb) for fb in range(2, FP) for m in ("gate", "up") for kc in range(8)]
    plan += spread(blocks(None, part), ada(GATE_A + 8, 8) + ada(SHIFT_F + 8, 8) + ada(SCALE_F + 8, 8), 0.8)
    rest = [(m, kc, fb) for fb in range(FP) for m in ("gate", "up") for kc in range(8, 16)]
    rest += [(m, kc, fb) for fb in range(FP, FC) for m in ("gate", "up") for kc in range(16)]
    plan += spread(blocks(None, rest), ada(GATE_F, 16), 0.6)
    plan += blocks("down", [(kc, fb) for fb in range(16) for kc in range(FC)])
    in2 = [(kc, CQ + i) for kc in range(16) for i in range(4)]
    in2 += [(kc, fb) for fb in (CKV, CKV + 1, KPE) for kc in range(16)]
    plan += blocks("in2", in2)
    plan += blocks("qup", [(kc, fb) for fb in range(12) for kc in range(4)])
    plan += blocks("kvup", [(kc, fb) for fb in range(16) for kc in range(2)])
    plan += blocks("in2", [(kc, fb + h) for h in range(8) for fb in (QA, KA, VA) for kc in range(16)])
    plan += blocks("out2", [(kc, fb) for fb in range(16) for kc in range(8, 16)])
    plan += blocks("out2", [(kc, fb) for fb in range(16) for kc in range(8)])
    plan += glu("gate2", "up2")
    plan += blocks("down2", [(kc, fb) for fb in range(16) for kc in range(FC)])
    return plan


def flat(tokens):
    if tokens is None:
        return []
    if isinstance(tokens, tuple) and len(tokens) == 2 and isinstance(tokens[1], int):
        return [tokens]
    return [t for x in tokens for t in flat(x)]


class Engine:

    def __init__(self, sem):
        self.sem, self.n, self.queue, self.seen = sem, 0, [], {}

    def put(self, fn, after=(), signal=True):
        waits = {}
        for sem, value in flat(after):
            if value > self.seen.get(sem.num, 0):
                self.seen[sem.num] = value
                waits[sem.num] = (sem, value)
        if signal:
            self.n += 1
        self.queue.append((fn, list(waits.values()), signal))
        return (self.sem, self.n) if signal else None

    def emit(self, engine):
        for fn, waits, signal in self.queue:
            for sem, value in waits:
                engine.wait_ge(sem, value)
            ins = fn(engine)
            if signal:
                ins.then_inc(self.sem, 1)


class Ring:

    def __init__(self, items, free=None):
        self.items, self.i = items, 0
        self.free = free if free is not None else {k: [] for k in range(len(items))}

    def take(self):
        k = self.i
        self.i = (k + 1) % len(self.items)
        after = self.free[k]
        assert after is not None, "buffer still in use"
        self.free[k] = None
        return k, self.items[k], after

    def give(self, k, *tokens):
        self.free[k] = list(tokens)


def build(nc, wst, xT, metaT, vecs, consts, rope2, rev, cvec, positions, lambdas, rpb, mbias, out):
    ctx = ExitStack()
    with ctx:
        _build(nc, ctx, wst, xT, metaT, vecs, consts, rope2, rev, cvec, positions, lambdas, rpb, mbias, out)


def _build(nc, ctx, wst, xT, metaT, vecs, consts, rope2, rev, cvec, positions, lambdas, rpb, mbias, out):
    def sem(name):
        return ctx.enter_context(nc.semaphore(name))

    BASE = 16512
    LIMIT = 229344
    at = [BASE]
    seq = [0]

    def place(shape, dt, off, name="t"):
        seq[0] += 1
        size = 4
        for s in shape[1:]:
            size *= s
        assert off + size <= LIMIT, (name, off, size)
        return nc.alloc_sbuf_tensor_at(f"{name}_{seq[0]}", list(shape), dt, offset=off)

    def keep(shape, dt, name="t"):
        size = 4
        for s in shape[1:]:
            size *= s
        t = place(shape, dt, at[0], name)
        at[0] += (size + 31) // 32 * 32
        return t

    class Region:
        def __init__(self, start, stop=LIMIT):
            self.at, self.stop = start, stop

        def __call__(self, shape, dt=F32, name="r"):
            size = 4
            for s in shape[1:]:
                size *= s
            t = place(shape, dt, self.at, name)
            self.at += (size + 31) // 32 * 32
            assert self.at <= self.stop, (name, self.at, self.stop)
            return t

    V = Engine(sem("dve"))
    A = Engine(sem("act"))
    G = Engine(sem("pool"))
    PE = Engine(sem("pe"))
    SP = Engine(None)
    dma_sems = {}

    def f32(ap):
        return ap.bitcast(F32)

    def load(dst, src, name, engine=None, after=()):
        s = dma_sems[name] = sem(name)
        e = engine or SP
        e.put(lambda q: q.dma_start(dst, src).then_inc(s, 16), after, signal=False)
        return (s, 16)

    def act(o, i, fn, after=(), **kw):
        return A.put(lambda e: e.activation(o, i, fn, **kw), after)

    def tt(o, a, b, op, after=(), eng=None):
        return (eng or V).put(lambda e: e.tensor_tensor(o, a, b, op), after)

    def ts(o, a, s0, s1, op0, op1=None, after=(), eng=None, **kw):
        if op1 is None:
            return (eng or V).put(lambda e: e.tensor_scalar(o, a, s0, None, op0, **kw), after)
        return (eng or V).put(lambda e: e.tensor_scalar(o, a, s0, s1, op0, op1, **kw), after)

    def stt(o, a, s, b, op0, op1, after=()):
        return V.put(lambda e: e.scalar_tensor_tensor(out=o, in0=a, scalar=s, in1=b, op0=op0, op1=op1), after)

    def ttr(o, a, b, scale, init, op0, op1, acc, after=()):
        return V.put(lambda e: e.tensor_tensor_reduce(o, a, b, scale, init, op0, op1, acc), after)

    def mm(o, w, x, start, stop, after=(), signal=False):
        return PE.put(lambda e: e.matmul(o, w, x, start=start, stop=stop, skip_group_check=True), after, signal)

    def tr(o, i, after=(), signal=False):
        k = i.shape[0]
        return PE.put(lambda e: e.transpose(o, i, ident[0:k, 0:k]), after, signal)

    def memset(ap, v, after=(), eng=None):
        return (eng or G).put(lambda e: e.memset(ap, v), after)

    def table(name):
        A.put(lambda e: e.preload_act_table_set(name), signal=False)

    X = keep([P, KC, TM], F32, "x")
    RS, RW = 5, 4
    stage = keep([P, RS, TILE], F32, "stage")
    whi = keep([P, RW, TILE], F32R, "whi")
    wlo = keep([P, RW, TILE], F32R, "wlo")
    cst = keep([P, NCONST], F32, "cst")
    ones = keep([P, P], F32, "ones")
    vec = keep([P, NVEC], F32, "vec")
    adac = keep([P, 192], F32, "adac")
    mod = keep([P, 96], F32, "mod")
    mul = keep([P, 4, 16], F32, "mul")
    small = keep([P, 8], F32, "small")
    stat = keep([P, 64], F32, "stat")
    tc = keep([P, 8], F32, "tc")
    tc_free = {i: [] for i in range(8)}
    R0 = at[0]
    ident = cst[:, COFF["ident"]:COFF["ident"] + 128]
    swap = cst[:, COFF["swap"]:COFF["swap"] + 128]
    causal = cst[:, COFF["causal"]:COFF["causal"] + 256]
    namask = cst[:, COFF["namask"]:COFF["namask"] + 64]
    freq = cst[:, COFF["freq"]:COFF["freq"] + 16]
    eps = small[:, 0:1]
    nlam = small[:, 1:2]
    gdiff = small[:, 2:3]

    def v_(name, i=0, n=1):
        return vec[:, VOFF[name] + i:VOFF[name] + i + n]

    ps = [ctx.enter_context(nc.psum_tensor(f"ps{i}", [P, 512], F32)) for i in range(8)]
    bank_free = {i: [] for i in range(8)}

    class Banks:

        def __init__(self, ids):
            self.ids, self.i = ids, 0

        def take(self):
            b = self.ids[self.i % len(self.ids)]
            self.i += 1
            after = bank_free[b]
            assert after is not None, f"bank {b} in use"
            bank_free[b] = None
            return b, ps[b], after

    def give(b, *tokens):
        bank_free[b] = list(tokens)

    HID = R0 + 33024
    TMP = HID + 90112
    NTMP = LIMIT - TMP
    hidh = place([P, FC, T], F32R, HID, "hidh")
    hidl = place([P, FC, T], F32R, HID + 45056, "hidl")
    cb = place([P, 2048], F32, TMP - 8192, "cb")

    plan = tile_plan()
    stage_sem = [sem(f"stage{i}") for i in range(RS)]
    stage_free = [[] for _ in range(RS)]
    w_free = [[] for _ in range(RW)]
    st = {"lag": False, "dma": 0, "done": 0, "w": 0, "used": 0, "ready": []}
    ada_tok = {}
    cb_tok = []

    def stream_dma():
        while st["dma"] < len(plan) and st["dma"] - (lows[0][0] if lows else st["done"]) < RS:
            t = st["dma"]
            s = t % RS
            SP.put(lambda q, t=t, s=s: q.dma_start(stage[:, s, :], wst[t]).then_inc(stage_sem[s], 16),
                   stage_free[s], signal=False)
            st["dma"] += 1

    def low_part():
        if lows:
            t, s, k, landed, hi = lows.pop()
            lo = tt(wlo[:, k, :], stage[:, s, :], f32(whi[:, k, :]), ALU.subtract, [landed, hi, w_free[k]])
            stage_free[s] = [lo]
            low_tok[t] = lo

    lows, low_tok = [], {}

    def pump(limit=len(plan)):
        low_part()
        stream_dma()
        while st["done"] < limit:
            t = st["done"]
            s = t % RS
            landed = (stage_sem[s], 16 * (t // RS + 1))
            kind = plan[t]
            if kind[0] == "a":
                j = kind[1]
                h = j % 2
                tok = ttr(stage[:, s, :], stage[:, s, :], cb[:, 1024 * h:1024 * (h + 1)], 1.0, 0.0,
                          ALU.mult, ALU.add, adac[:, j:j + 1], [landed, cb_tok])
                ada_tok[j] = tok
                stage_free[s] = [tok]
            else:
                if st["w"] - st["used"] >= RW:
                    break
                k = st["w"] % RW
                hi = act(whi[:, k, :], stage[:, s, :], ACT.Copy, [landed, w_free[k]])
                low_part()
                lows.append((t, s, k, landed, hi))
                if not st["lag"]:
                    low_part()
                st["ready"].append((kind, k, hi, t))
                st["w"] += 1
            st["done"] += 1
            stream_dma()

    def next_tile():
        pump()
        kind, k, hi, t = st["ready"].pop(0)
        if t not in low_tok:
            low_part()
        return kind, k, hi, low_tok[t]

    def tile_used(k, token):
        w_free[k] = [token]
        st["used"] += 1
        pump()

    pending = []

    def later(n, fn):
        pending.append([n, fn])

    ticks = [0]

    def tick():
        ticks[0] += 1
        due = []
        for p in pending:
            p[0] -= 1
            if p[0] <= 0:
                due.append(p)
        for p in due:
            pending.remove(p)
            p[1]()

    def drain():
        while pending:
            tick()

    def gemm(count, banks, moving, width, done):
        acc = {}
        for _ in range(count):
            (what, blks), k, hi_tok, lo_tok = next_tile()
            assert what == "b"
            last = None
            ticked = False
            for i, (mat, kc, fb) in enumerate(blks):
                key = (mat, fb)
                first = key not in acc
                if first:
                    b, bank, free = banks.take()
                    acc[key] = [b, bank, 0, gemm_n(mat)]
                else:
                    free = []
                b, bank, n, total = acc[key]
                xh, xl, tok = moving(mat, kc)
                w = width(mat, fb)
                wh = whi[:, k, P * i:P * (i + 1)]
                wl = wlo[:, k, P * i:P * (i + 1)]
                acc[key][2] = n + 1
                end = n + 1 == total
                o = bank[:, 0:w]
                mm(o, wh, xh[:, 0:w], first, False, [hi_tok, tok, free])
                mm(o, wh, xl[:, 0:w], False, False)
                sig = end or i == len(blks) - 1
                last = mm(o, wl, xh[:, 0:w], False, end, [lo_tok], signal=sig) or last
                if end:
                    del acc[key]
                    if not ticked:
                        tick()
                        ticked = True
                    done(mat, fb, b, bank, last)
            if not ticked:
                tick()
            tile_used(k, last)
            yield
        assert not acc

    halves = {}

    def gemm_n(mat):
        return halves.get(mat, KCHUNKS[mat])

    def run(main, sides=(), rate=1.0):
        live = list(sides)
        credit = 0.0
        for _ in main:
            credit += rate
            while credit >= 1.0:
                credit -= 1.0
                for s in list(live):
                    if next(s, "end") == "end":
                        live.remove(s)
        return live

    def finish(sides):
        live = list(sides)
        n = 0
        while live:
            for s in list(live):
                if next(s, "end") == "end":
                    live.remove(s)
            tick()
            n += 1
            assert n < 1000, "stuck"

    def rms(o, src, n, after, bias=None):
        a = act(o, src, ACT.Ln, after, scale=1.0 / n, bias=eps)
        b = act(o, o, ACT.Exp, [a], scale=-0.5)
        return a, b

    P1 = Region(TMP)
    P1b = Region(TMP - 16384, TMP - 8192)
    ering = Ring([P1([P, 2, 384], F32, "e") for _ in range(2)])
    ptring = Ring([P1([P, 384], F32, "pt") for _ in range(2)])
    R1 = P1([P, T], F32, "R1")
    rl = [P1b([P, 512], F32, "rl") for _ in range(2)]
    sc = P1b([P, 384], F32, "sc")
    wk = P1b([P, 384], F32, "wk")
    rr1 = P1b([P, T], F32, "rr")
    start_at = TMP - 16384 + 4096
    P1c = Region(TMP - 16384, TMP - 12288)
    oring = Ring([P1c([P, T], F32, "o") for _ in range(2)])
    sqring = Ring([P1c([P, T], F32, "sq") for _ in range(2)])
    rring = Ring([R1, rr1])
    rt = [P1([P, 128], F32, "rt") for _ in range(4)]
    cosT = P1([P, 2, 16], F32, "cosT")
    sinT = P1([P, 2, 16], F32, "sinT")
    iw = P1([P, 2, 16], F32, "iw")

    slot = [HID + 4096 * i for i in range(11)]
    extra = [HID + 45056 + 4096 * i for i in range(3)]
    part = [place([P, 2, 512], F32, slot[g], f"part{g}") for g in range(11)]
    xr = place([P, KC, T], F32, HID + 57344, "xr")
    mxh = place([P, 8, T], F32R, HID + 57344, "mxh")
    mxl = place([P, 8, T], F32R, HID + 57344 + 8192, "mxl")
    assert HID + 57344 + 16384 <= TMP - 16384
    hh = place([P, KC, T], F32R, R0, "hh")
    hl = place([P, KC, T], F32R, R0 + 16384, "hl")
    mdh = place([P, 8, T], F32R, R0, "mdh")
    mdl = place([P, 8, T], F32R, R0 + 16384, "mdl")
    iring = Ring([place([P, 768], F32, HID + 57344 + 3072 * i, "ir") for i in range(2)])

    cb_load = load(cb[:, :], bass.AP(cvec.tensor, 0, [[0, P], [1, 2048]]), "ld_c")
    vec_load = load(vec[:, :], vecs, "ld_vec")
    posi = place([P, 2], I32, start_at, "posi")
    posf = place([P, 2], F32, start_at + 32, "posf")
    ang = [place([P, 2, 16], F32, start_at + 64 + 128 * i, "ang") for i in range(5)]
    lam_in = place([P, 256], F32, start_at + 1024, "lam")
    lamt = place([P, 8], F32, start_at + 2048, "lamt")
    pos_load = load(posi[:, :], positions, "ld_pos", A)
    cst_load = load(cst[:, :], consts, "ld_cst", A)
    x_load = [load(X[:, 4 * i:4 * i + 4, 0:T], xT[:, 4 * i:4 * i + 4, :], f"ld_x{i}", A) for i in range(4)]
    lam_load = load(lam_in[:, :], bass.AP(lambdas.tensor, 0, [[0, P], [1, 256]]), "ld_lam", A)
    meta_load = load(X[:, :, T:TM], metaT, "ld_meta", A)
    stream_dma()

    ones_tok = memset(ones[:, :], 1.0)
    eps_tok = memset(eps, 1e-6)
    stat_tok = memset(stat[:, :], 0.0)
    cb_tok.append(act(cb[:, :], cb[:, :], ACT.Silu, [cb_load]))

    xsq = [rl[i][:, 256 * j:256 * j + 256] for i in range(2) for j in range(2)]
    sq_free = [[] for _ in range(4)]
    b, bank, free = 0, ps[0], []
    for kc in range(KC):
        s = act(xsq[kc % 4], X[:, kc, 0:T], ACT.Square, [x_load[kc // 4], sq_free[kc % 4]])
        t = mm(bank[:, 0:T], ones[:, :], xsq[kc % 4], kc == 0, kc == KC - 1, [s, ones_tok], signal=True)
        sq_free[kc % 4] = [t]
    sum_tok = t

    two_pi = 2.0 * np.pi
    C1 = 6.28125
    C2 = float(np.float32(np.floor((two_pi - C1) * 2.0 ** 22) / 2.0 ** 22))
    C3 = float(np.float32(two_pi - C1 - C2))
    H1 = float(np.float32(np.pi / 2))
    H2 = float(np.float32(np.pi / 2 - H1))
    MAGIC = 12582912.0
    PI = 3.1415925
    p0 = G.put(lambda e: e.tensor_copy(posf[:, :], posi[:, :]), [pos_load])
    a0, kk, r2, *rrs = [a[:, :, :] for a in ang]
    pa = None
    for tb in range(2):
        pa = ts(ang[0][:, tb, :], freq, posf[:, tb:tb + 1], None, ALU.mult, None, [p0, cst_load], G)
    t, trig = pa, []
    for dst, quarter, rr in ((sinT, 0.0, rrs[0]), (cosT, 0.25, rrs[1])):
        t = ts(kk, a0, float(1.0 / two_pi), quarter, ALU.mult, ALU.add, [t], G)
        t = ts(kk, kk, MAGIC, -MAGIC, ALU.add, ALU.add, [t], G)
        src = a0
        for c in (C1, C2, C3):
            t = ts(r2, kk, -c, None, ALU.mult, None, [t], G)
            t = tt(rr, src, r2, ALU.add, [t], G)
            src = rr
        if quarter:
            t = ts(rr, rr, H1, H2, ALU.add, ALU.add, [t], G)
        t = ts(rr, rr, PI, -PI, ALU.min, ALU.max, [t], G)
        trig.append(act(dst[:, :, :], rr, ACT.Sin, [t]))
    trig_tok = trig
    table("natural_log_exp_and_others")

    ra, rb = rms(R1[:, :], bank[:, 0:T], 2048, [sum_tok, eps_tok])
    bank_free[0] = [ra]
    pump(2 * 2 * PASSES[0][1])
    xr_tok = []

    def make_xr(k0, k1, eng):
        for kc in range(k0, k1):
            xr_tok.append(tt(xr[:, kc, :], X[:, kc, 0:T], R1[:, :], ALU.mult, [rb, x_load[kc // 4]], eng))

    make_xr(*PASSES[0], V)

    lam_tok = gdiff_tok = None

    def lambda_():
        nonlocal lam_tok, gdiff_tok
        la = []
        for i in range(2):
            t = ttr(lam_in[:, 128 * i:128 * i + 64], lam_in[:, 128 * i:128 * i + 64], lam_in[:, 128 * i + 64:128 * i + 128],
                    1.0, 0.0, ALU.mult, ALU.add, lamt[:, i:i + 1], [lam_load])
            la.append(t)
        le = act(lamt[:, 2:4], lamt[:, 0:2], ACT.Exp, la)
        l1 = tt(lamt[:, 4:5], lamt[:, 3:4], lamt[:, 2:3], ALU.subtract, [le], G)
        lam_tok = ts(nlam, lamt[:, 4:5], -0.2, None, ALU.add, None, [l1], G)
        gdiff_tok = ts(gdiff, v_("g_diff_sub"), 0.8, None, ALU.mult, None, [vec_load], G)

    def mod_chunks(c0, n):
        t = tt(mod[:, c0:c0 + n], adac[:, 2 * c0:2 * (c0 + n):2], adac[:, 2 * c0 + 1:2 * (c0 + n):2], ALU.add,
               [ada_tok[j] for j in range(2 * c0, 2 * (c0 + n))], G)
        return tt(mod[:, c0:c0 + n], mod[:, c0:c0 + n], v_("b_ada", c0, n), ALU.add, [t, vec_load], G)

    def gain(dst, c0, n, g, one):
        t = mod_chunks(c0, n)
        if one:
            t = ts(mod[:, c0:c0 + n], mod[:, c0:c0 + n], 1.0, None, ALU.add, None, [t], G)
        return tt(dst, mod[:, c0:c0 + n], g, ALU.mult, [t, vec_load], G)

    h_tok = {}

    def make_h(k0, k1):
        n = k1 - k0
        tsh = mod_chunks(SHIFT_A + k0, n)
        tsc = gain(mul[:, 0, k0:k1], SCALE_A + k0, n, v_("g_attn_pre", k0, n), True)
        for kc in range(k0, k1):
            a = ts(xr[:, kc, :], xr[:, kc, :], mul[:, 0, kc:kc + 1], mod[:, SHIFT_A + kc:SHIFT_A + kc + 1],
                   ALU.mult, ALU.add, [xr_tok[kc], tsh, tsc])
            h = act(hh[:, kc, :], xr[:, kc, :], ACT.Copy, [a])
            l = tt(hl[:, kc, :], xr[:, kc, :], f32(hh[:, kc, :]), ALU.subtract, [a, h])
            h_tok[kc] = [h, l]

    fin = {}
    age = {}
    turn_after = {}
    FREED = []
    ROTATED = {g: [(0, 8, 64, 8)] for g in (IQ0, IQ1, DK0, DQ0, DK1, DQ1)}
    ROTATED.update({g: [(0, 4, 128, 16)] for g in (SQ0, SQ1)})
    ROTATED[IKS] = [(0, 2, 64, 8), (128, 1, 128, 16)]
    part_tok = {}
    tmp2 = Ring(rl, {0: sq_free, 1: sq_free})
    gb = Banks([0, 1, 2])
    gb8 = Banks(range(8))

    def project():
        make_h(*PASSES[0])
        make_xr(PASSES[0][1], KC, G)
        pump()
        lambda_()
        for pi, (k0, k1) in enumerate(PASSES):
            lastp = pi == len(PASSES) - 1
            if lastp:
                st["lag"] = True
                FREED.extend([(PE.sem, PE.n), list(tmp2.free.values())])
                for ring in (oring, sqring):
                    for k in ring.free:
                        ring.free[k] = list(FREED)
                for k in iring.free:
                    iring.free[k] = xr_done()
            for g in range(11):
                if g == 10 and not lastp:
                    make_h(*PASSES[pi + 1])
                n = G_COLS[g]
                bk = [(gb if lastp else gb8).take() for _ in range(2)]
                last = None
                for kp in range(k0 // 2, k1 // 2):
                    (what, g_, kp_), k, hi_tok, lo_tok = next_tile()
                    assert (what, g_, kp_) == ("x", g, kp)
                    for i in range(2):
                        kc = 2 * kp + i
                        wh = whi[:, k, 512 * i:512 * i + n]
                        wl = wlo[:, k, 512 * i:512 * i + n]
                        for tb in range(2):
                            o = bk[tb][1][:, 0:n]
                            c = slice(P * tb, P * tb + P)
                            st_ = kc == k0
                            en = kc == k1 - 1
                            mm(o, hh[:, kc, c], wh, st_, False, [h_tok[kc], hi_tok, bk[tb][2]])
                            mm(o, hh[:, kc, c], wl, False, False, [lo_tok])
                            last = mm(o, hl[:, kc, c], wh, False, en, signal=(i == 1)) or last
                            if en and tb == 0:
                                tok0 = last
                    if kp < k1 // 2 - 1:
                        tile_used(k, last)
                        tick()
                        yield
                toks = [tok0, last]
                res = []
                for tb in range(2):
                    b, bank, _ = bk[tb]
                    dst = part[g][:, tb, 0:n]
                    if pi == 0:
                        t = act(dst, bank[:, 0:n], ACT.Copy, [toks[tb]])
                        give(b, t)
                    elif not lastp:
                        r, buf, fr = tmp2.take()
                        t = act(buf[:, 0:n], bank[:, 0:n], ACT.Copy, [toks[tb], fr])
                        give(b, t)
                        t = tt(dst, dst, buf[:, 0:n], ALU.add, [t, part_tok[g, tb]], G)
                        tmp2.give(r, t)
                    else:
                        t = tt(dst, bank[:, 0:n], dst, ALU.add, [toks[tb], part_tok[g, tb]])
                        give(b, t)
                    part_tok[g, tb] = t
                    res.append(t)
                if lastp:
                    fin[g] = res
                    if g in ROTATED:
                        age[g] = ticks[0]
                        turn_after[g] = [rotate(g, *r, fin[g]) for r in ROTATED[g]]
                tile_used(k, last)
                tick()
                yield

    ab = Banks([3, 4, 5, 6, 7])
    rot_free = [[]]

    def rotate(g, c0, heads, dim, half, after):
        v = part[g][:, :, c0:c0 + heads * dim].rearrange("p t (h d) -> p t h d", h=heads)
        step = 16 // half
        cosb = cosT[:, :, 0:16:step].unsqueeze(2).to_broadcast([P, 2, heads, half])
        sinb = sinT[:, :, 0:16:step].unsqueeze(2).to_broadcast([P, 2, heads, half])
        x1 = v[:, :, :, 0:half]
        x2 = v[:, :, :, half:2 * half]
        n = heads * half
        r = [q[:, 0:2 * n].rearrange("p (t h d) -> p t h d", t=2, h=heads) for q in rt]
        a = [after, rot_free[0], trig_tok]
        t1 = tt(r[0], x1, cosb, ALU.mult, a, G)
        t2 = tt(r[1], x2, sinb, ALU.mult, a, G)
        t3 = tt(r[2], x2, cosb, ALU.mult, a, G)
        t4 = tt(r[3], x1, sinb, ALU.mult, a, G)
        t5 = tt(x1, r[0], r[1], ALU.subtract, [t1, t2, t3, t4], G)
        t6 = tt(x2, r[2], r[3], ALU.add, [t3, t4], G)
        rot_free[0] = [t5, t6]
        return [t5, t6]

    def turn(g, cols, evac, after):
        b, bank, free = ab.take()
        for i, c in enumerate(cols):
            for tb in range(2):
                t = tr(bank[:, 256 * i + P * tb:256 * i + P * tb + P], part[g][:, tb, c:c + P], [after, free, cst_load],
                       signal=(i == len(cols) - 1 and tb == 1))
        give(b, *evac(bank, t))
        return t

    iqT = [place([P, 4, T], F32, extra[0], "iqT0"), place([P, 4, T], F32, slot[0], "iqT1")]
    ikz = place([P, 2, T], F32, slot[1], "ikz")
    skT = place([P, T], F32, slot[1] + 2048, "skT")
    M1 = place([P, 384], F32, extra[0], "M1")
    sqT = [place([P, 4, T], F32, slot[8], "sqT0"), place([P, 4, T], F32, slot[9], "sqT1")]
    kz = [place([P, 2, 2, T], F32, o, f"kz{i}")[:, :, :, :] for i, o in enumerate((extra[1], extra[2], slot[5]))]
    kz.append(place([P, 2, 4096], F32, R0 + 8192, "kz3")[:, :, 0:512].rearrange("p b (c t) -> p b c t", c=2))
    dqT = [place([P, 4, T], F32, slot[3], "dqT0"), place([P, 4, T], F32, slot[6], "dqT1")]
    m1p = [place([P, 8, T], F32, R0 + 8192, "m1a"), place([P, 8, T], F32, R0 + 24832, "m1b")]

    def m1(kc):
        return m1p[kc // 8][:, kc % 8, :]

    T_ = {}
    turned = {}

    def prep():
        def ready(g):
            while g not in fin or ticks[0] < age[g] + 2:
                yield

        def plain(g, dst, key, free):
            yield from ready(g)
            toks = []
            for j in range(2):
                def ev(bank, t, j=j):
                    e = act(dst[:, 2 * j:2 * j + 2, :], bank[:, :].rearrange("p (b t) -> p b t", b=2), ACT.Copy, [t, free])
                    T_.setdefault(key, []).append(e)
                    return [e]
                toks.append(turn(g, [256 * j, 256 * j + 128], ev, [fin[g], turn_after[g]]))
                yield
            turned[g] = toks[-1]

        def keys(g, hp, free):
            zero = [memset(kz[hp + j], 0.0, free[j]) for j in range(2)]
            yield from ready(g)
            for j in range(2):
                z = kz[hp + j]

                def ev(bank, t, z=z, j=j):
                    v = bank[:, :].rearrange("p (b t) -> p b t", b=2)
                    e0 = act(z[0:64, :, 0, :], v[0:64], ACT.Copy, [t, zero[j]])
                    e1 = act(z[64:128, :, 1, :], v[64:128], ACT.Copy, [t, zero[j]])
                    for i in range(2):
                        T_[("kz", 2 * (hp + j) + i)] = [e0, e1]
                    return [e0, e1]
                tok = turn(g, [256 * j, 256 * j + 128], ev, [fin[g], turn_after[g]])
                yield
            turned[g] = tok

        yield from plain(IQ0, iqT[0], "iq0", [])
        yield from plain(IQ1, iqT[1], "iq1", [turned[IQ0]])
        zero = memset(ikz[:, :, :], 0.0, [turned[IQ1]])
        yield from ready(IKS)

        def ev(bank, t):
            v = bank[:, :].rearrange("p (b t) -> p b t", b=2)
            e0 = act(ikz[0:64, 0, :], v[0:64, 0, :], ACT.Copy, [t, zero])
            e1 = act(ikz[64:128, 1, :], v[64:128, 0, :], ACT.Copy, [t, zero])
            e2 = act(skT[:, :], v[:, 1, :], ACT.Copy, [t, turned[IQ1]])
            T_["ik"] = [e0, e1]
            T_["sk"] = [e2]
            return [e0, e1, e2]
        turned[IKS] = turn(IKS, [0, 128], ev, [fin[IKS], turn_after[IKS]])
        w = ts(iw[:, :, :], part[IKS][:, :, 384:400], 1.0 / 32, None, ALU.mult, None, fin[IKS], G)
        T_["iw"] = [w]
        yield
        yield from keys(DK0, 0, [[], []])
        yield from plain(DQ0, dqT[0], "dq0", [turned[DK0]])
        yield from keys(DK1, 2, [[turned[DQ0]], FREED])
        yield from plain(DQ1, dqT[1], "dq1", [turned[DK1]])
        yield from plain(SQ0, sqT[0], "sq0", [turned[DQ1]])
        yield from plain(SQ1, sqT[1], "sq1", [turned[SQ0]])

    def turned_tok(g):
        return turned[g]

    def lock(pipe, n):
        for t in range(n + len(pipe) - 1):
            for s in range(len(pipe) - 1, -1, -1):
                i = t - s
                if 0 <= i < n:
                    r = pipe[s](i)
                    if r is not None:
                        yield from r
            yield

    def indexer():
        while not ("ik" in T_ and len(T_.get("iq1", [])) == 2):
            yield
        last = {}
        for p in range(8):
            q = iqT[p // 4][:, p % 4, :]
            qt = [T_["iq0"] if p < 4 else T_["iq1"], T_["ik"]]
            work = []
            r, flatbuf, fr = iring.take()
            for qb in (1, 0):
                n = 256 if qb else 128
                b, bank, free = ab.take()
                t = mm(bank[:, 0:2 * n].rearrange("p (h k) -> p h k", h=2), q[:, P * qb:P * qb + P], ikz[:, :, 0:n], True, True,
                       [free, qt], signal=True)
                buf = flatbuf[:, 0:512] if qb else flatbuf[:, 512:768]
                e = act(buf, bank[:, 0:2 * n], ACT.Relu, [t, fr])
                give(b, e)
                work.append((qb, n, buf, e))
            T_["idx_pe"] = t
            used = {0: [], 1: []}
            for h in range(2):
                for qb, n, buf, e in work:
                    dst = sc[:, 128 * qb:128 * qb + n]
                    w = iw[:, qb, 2 * p + h:2 * p + h + 1]
                    src = buf[:, n * h:n * h + n]
                    if p == 0 and h == 0:
                        t = ts(dst, src, w, None, ALU.mult, None, [e, T_["iw"]])
                    else:
                        t = stt(dst, src, w, dst, ALU.mult, ALU.add, [e, last[qb]])
                    last[qb] = t
                    used[qb].append(t)
            iring.give(r, used[0], used[1])
            yield
        seg = {0: slice(0, 128), 1: slice(128, 384)}
        mask = {0: causal[:, 128:256], 1: causal[:, :]}
        t = {}
        for qb in (1, 0):
            t[qb] = tt(sc[:, seg[qb]], sc[:, seg[qb]], mask[qb], ALU.add, [last[qb], cst_load])
        src = {qb: sc[:, seg[qb]] for qb in (0, 1)}
        m8 = {qb: stat[:, 8 * qb:8 * qb + 8] for qb in (0, 1)}
        for r in range(8):
            for qb in (1, 0):
                t[qb] = V.put(lambda e, qb=qb, s=src[qb]: e.max(m8[qb], s), [t[qb], stat_tok])
            for qb in (1, 0):
                t[qb] = V.put(lambda e, qb=qb, s=src[qb]: e.match_replace(wk[:, seg[qb]], m8[qb], s, USED), [t[qb]])
                src[qb] = wk[:, seg[qb]]
            yield
        toks = []
        for qb in (1, 0):
            t[qb] = tt(wk[:, seg[qb]], wk[:, seg[qb]], sc[:, seg[qb]], ALU.is_equal, [t[qb]])
        for qb in (1, 0):
            toks.append(stt(M1[:, seg[qb]], wk[:, seg[qb]], NEG, mask[qb], ALU.mult, ALU.add, [t[qb], T_["idx_pe"]]))
        T_["M"] = toks
        yield

    seg = {0: slice(0, 128), 1: slice(128, 384)}

    def transposed_p(E, after, key):
        b, bank, free = ab.take()
        for i in range(3):
            t = tr(bank[:, P * i:P * i + P], E[:, (0, 128, 256)[i]:(0, 128, 256)[i] + P], [after, free], signal=(i == 2))
        r, buf, fr = ptring.take()
        e = act(buf[:, :], bank[:, 0:384], ACT.Copy, [t, fr])
        give(b, e)
        return t, r, buf, e

    def weighted_v(v0, v1, buf, after):
        b, bank, free = ab.take()
        mm(bank[:, 0:256], v0, buf[:, 0:256], True, False, [after, free])
        t = mm(bank[:, 128:256], v1, buf[:, 256:384], False, True, signal=True)
        return b, bank, t

    dsa = {}
    mix_tok = {}
    SD = float(128 ** -0.5)

    def dsa_steps():
        while not ("M" in T_ and len(T_.get("sq1", [])) == 2 and 7 in mix_tok):
            yield

        def s0(h):
            b, bank, free = ab.take()
            q = sqT[h // 4][:, h % 4, :]
            qt = [T_["sq0"] if h < 4 else T_["sq1"], T_["sk"]]
            t0 = mm(bank[:, 0:128], q[:, 0:128], skT[:, 0:128], True, True, [free, qt], signal=True)
            t1 = mm(bank[:, 128:384], q[:, 128:256], skT[:, :], False, True, signal=True)
            T_["dsa_pe"] = t1
            r, E, fr = ering.take()
            c = 16 + 4 * (h % 4)
            vs, es = [], []
            for qb, t in ((0, t1), (1, t1)):
                vs.append(ttr(E[:, 0, seg[qb]], bank[:, seg[qb]], M1[:, seg[qb]], -SD, BIG, ALU.add, ALU.min,
                              stat[:, c + qb:c + qb + 1], [t, fr, T_["M"]]))
            give(b, vs)
            for qb in range(2):
                es.append(act(E[:, 0, seg[qb]], E[:, 0, seg[qb]], ACT.Exp, [vs[qb]], scale=-1.0,
                              bias=stat[:, c + qb:c + qb + 1], accum_out=stat[:, c + 2 + qb:c + 3 + qb]))
            dsa[h] = dict(r=r, E=E, es=es, c=c)

        def s1(h):
            d = dsa[h]
            E, c = d["E"], d["c"]
            t = V.put(lambda e: e.reciprocal(stat[:, c:c + 2], stat[:, c + 2:c + 4]), [d["es"]])
            ns = []
            for qb in range(2):
                ns.append(ts(E[:, 0, seg[qb]], E[:, 0, seg[qb]], stat[:, c + qb:c + qb + 1], None, ALU.mult, None, [t]))
            d["ns"] = ns

        def turn_p(h):
            d = dsa[h]
            t, r, buf, e = transposed_p(d["E"][:, 0, :], d["ns"], h)
            ering.give(d["r"], t)
            d.update(pr=r, buf=buf, e=e)

        def s2(h):
            d = dsa[h]
            b, bank, t = weighted_v(part[IKS][:, 0, 256:384], part[IKS][:, 1, 256:384], d["buf"], [d["e"], fin[IKS]])
            ptring.give(d["pr"], t)
            T_["dsa_pv"] = t
            a = act(mxh[:, h, :], bank[:, 0:256], ACT.Copy, [t, xr_done(), T_["M"]])
            l = tt(mxl[:, h, :], bank[:, 0:256], f32(mxh[:, h, :]), ALU.subtract, [a])
            give(b, l)
            mix_tok[8 + h] = [a, l]

        yield from lock([s0, s1, turn_p, s2], 8)

    def xr_done():
        return [h_tok[k] for k in range(KC)]

    diff = {}

    def diff_steps():
        while not (len(T_.get("dq0", [])) == 2 and ("kz", 3) in T_):
            yield

        def s0(h):
            while h == 4 and not (len(T_.get("dq1", [])) == 2 and ("kz", 7) in T_):
                yield
            q = dqT[h // 4][:, h % 4, :]
            z = kz[h // 2][:, h % 2, :, :]
            qt = [T_["dq0"] if h < 4 else T_["dq1"], T_[("kz", h)]]
            bk = []
            for qb in range(2):
                n = 256 if qb else 128
                b, bank, free = ab.take()
                t = mm(bank[:, 0:2 * n].rearrange("p (c k) -> p c k", c=2), q[:, P * qb:P * qb + P], z[:, :, 0:n], True, True,
                       [free, qt], signal=True)
                bk.append((b, bank, t, n))
            r, E, fr = ering.take()
            c = 32 + 8 * (h % 4)
            vs = {}
            for qb, (b, bank, t, n) in enumerate(bk):
                for i in range(2):
                    vs[qb, i] = ttr(E[:, i, seg[qb]], bank[:, n * i:n * i + n], causal[:, 256 - n:256], -0.125, BIG,
                                    ALU.add, ALU.min, stat[:, c + 2 * qb + i:c + 2 * qb + i + 1], [t, fr, cst_load])
                give(b, vs[qb, 0], vs[qb, 1])
            es = []
            for qb in range(2):
                for i in range(2):
                    k = 2 * qb + i
                    es.append(act(E[:, i, seg[qb]], E[:, i, seg[qb]], ACT.Exp, [vs[qb, i]], scale=-1.0,
                                  bias=stat[:, c + k:c + k + 1], accum_out=stat[:, c + 4 + k:c + 5 + k]))
            diff[h] = dict(r=r, E=E, es=es, c=c)

        def s1(h):
            d = diff[h]
            E, c = d["E"], d["c"]
            t = V.put(lambda e: e.reciprocal(stat[:, c:c + 4], stat[:, c + 4:c + 8]), [d["es"]])
            u = ts(stat[:, c + 1:c + 4:2], stat[:, c + 1:c + 4:2], nlam, None, ALU.mult, None, [t, lam_tok])
            ns = []
            for qb in range(2):
                ns.append(ts(E[:, 0, seg[qb]], E[:, 0, seg[qb]], stat[:, c + 2 * qb:c + 2 * qb + 1], None, ALU.mult, None, [t]))
            for qb in range(2):
                ns[qb] = stt(E[:, 0, seg[qb]], E[:, 1, seg[qb]], stat[:, c + 2 * qb + 1:c + 2 * qb + 2], E[:, 0, seg[qb]],
                             ALU.mult, ALU.add, [u, ns[qb]])
            d["ns"] = ns

        def turn_p(h):
            d = diff[h]
            t, r, buf, e = transposed_p(d["E"][:, 0, :], d["ns"], h)
            ering.give(d["r"], t)
            d.update(pr=r, buf=buf, e=e)

        def s2(h):
            d = diff[h]
            g = DV0 if h < 4 else DV1
            c0 = 128 * (h % 4)
            b, bank, t = weighted_v(part[g][:, 0, c0:c0 + 128], part[g][:, 1, c0:c0 + 128], d["buf"], [d["e"], fin[g]])
            ptring.give(d["pr"], t)
            T_["diff_pv"] = t
            r1_, o, fr1 = oring.take()
            r2_, s, fr2 = sqring.take()
            a = act(s[:, :], bank[:, 0:256], ACT.Square, [t, fr2])
            a2 = act(o[:, :], bank[:, 0:256], ACT.Copy, [t, fr1])
            give(b, a, a2)
            d.update(o=o, s=s, ro=r1_, rs=r2_, a=a, a2=a2)

        def s3(h):
            d = diff[h]
            b, bank, free = ab.take()
            t = mm(bank[:, 0:256], ones[:, :], d["s"][:, :], True, True, [free, d["a"]], signal=True)
            sqring.give(d["rs"], t)
            rk, R, fr = rring.take()
            a, e = rms(R[:, :], bank[:, 0:256], 128, [t, fr])
            give(b, a)
            f = d["o"]
            t = stt(f[:, :], f[:, :], gdiff, R[:, :], ALU.mult, ALU.mult, [e, d["a2"], gdiff_tok])
            rring.give(rk, t)
            a = act(mdh[:, h, :], f[:, :], ACT.Copy, [t, FREED])
            l = tt(mdl[:, h, :], f[:, :], f32(mdh[:, h, :]), ALU.subtract, [t, a, FREED])
            oring.give(d["ro"], l)
            mix_tok[h] = [a, l]

        yield from lock([s0, s1, turn_p, s2, s3], 8)

    sides = [prep(), diff_steps(), indexer(), dsa_steps()]
    sides = run(project(), sides, 1.0)
    n = 0
    while 7 not in mix_tok:
        for s in list(sides):
            if next(s, "end") == "end":
                sides.remove(s)
        tick()
        n += 1
        assert n < 500

    R2 = place([P, TM], F32, LIMIT - 1088, "R2")
    halves["o"] = 8
    m_tok = {}
    phase = {"half": 0}

    def o_moving(mat, kc):
        return (mxh[:, kc - 8, :], mxl[:, kc - 8, :], mix_tok[kc]) if kc >= 8 else (mdh[:, kc, :], mdl[:, kc, :], mix_tok[kc])

    o_free = [T_["diff_pv"]]

    def o_first(mat, fb, b, bank, tok):
        t = act(m1(fb), bank[:, 0:T], ACT.Copy, [tok, o_free])
        give(b, t)
        m_tok[fb] = t

    sides = run(gemm(16, gb, o_moving, lambda m, f: T, o_first), sides, 1.5)
    finish(sides)

    F = Region(TMP, LIMIT - 1088)
    sqf = Ring([F([P, TM], F32, "sqf") for _ in range(2)])
    ssum = F([P, TM], F32, "ssum")
    zr = Ring([F([P, TQ], F32, "z") for _ in range(2)])
    ur = Ring([F([P, T], F32, "u") for _ in range(2)])
    hr = Ring([F([P, T], F32, "hf") for _ in range(2)])
    cr = Ring([F([P, T], F32, "c") for _ in range(1)])
    Rm = zr.items[0]
    guard1 = [(V.sem, V.n), (A.sem, A.n), (PE.sem, PE.n), (G.sem, G.n)]
    for ring in (sqf, zr, ur, hr, cr):
        for k in ring.free:
            ring.free[k] = list(guard1)
    acc_tok = [[]]

    def square_in(src, n, after, first):
        if first:
            t = act(ssum[:, 0:n], src, ACT.Square, [after, acc_tok[0]])
            acc_tok[0] = [t]
            return t
        k, buf, fr = sqf.take()
        s = act(buf[:, 0:n], src, ACT.Square, [after, fr])
        t = tt(ssum[:, 0:n], ssum[:, 0:n], buf[:, 0:n], ALU.add, [s, acc_tok[0]], G)
        sqf.give(k, t)
        acc_tok[0] = [t]
        return s

    def rms_of_sum(o, n, after, div=2048):
        b, bank, free = ab.take()
        t = mm(bank[:, 0:n], ones[:, :], ssum[:, 0:n], True, True, [free, acc_tok[0]], signal=True)
        acc_tok[0] = [acc_tok[0], t]
        a, e = rms(o[:, 0:n], bank[:, 0:n], div, [t, after])
        give(b, a)
        return e

    acc_tok[0] = list(guard1)

    def o_second(mat, fb, b, bank, tok):
        t = tt(m1(fb), bank[:, 0:T], m1(fb), ALU.add, [tok, m_tok[fb]])
        give(b, t)
        m_tok[fb] = [t]

        def squares():
            m_tok[fb] = [t, square_in(m1(fb), T, [t], fb == 0)]
        later(1, squares)

    for _ in gemm(16, gb8, o_moving, lambda m, f: T, o_second):
        pass
    halves.clear()
    drain()

    yh = place([P, KC, TQ], F32R, R0, "yh")
    yl = place([P, KC, TQ], F32R, R0 + 16512, "yl")
    x_tok = {kc: [x_load[kc // 4], meta_load] for kc in range(KC)}
    y_tok = {}

    def add_residual(m, kc, s, R, Rtok, after):
        k, buf, fr = hr.take()
        t = stt(buf[:, 0:T], m(kc), s, R[:, 0:T], ALU.mult, ALU.mult, [Rtok, after, fr])
        t = tt(X[:, kc, 0:T], X[:, kc, 0:T], buf[:, 0:T], ALU.add, [t, x_tok[kc]])
        hr.give(k, t)
        x_tok[kc] = [t]
        return t

    def operand(yh, yl, kc, n, s, after):
        a = act(yh[:, kc, 0:n], X[:, kc, 0:n], ACT.Copy, [x_tok[kc], after], scale=s)
        l = stt(yl[:, kc, 0:n], X[:, kc, 0:n], s, f32(yh[:, kc, 0:n]), ALU.mult, ALU.subtract, [x_tok[kc], after, a])
        y_tok[kc] = [a, l]

    def shift_columns(k0, after):
        tsh = mod_chunks(SHIFT_F + k0, 8)
        th, tl = [], []
        for c in range(T, TQ):
            src = mod[:, SHIFT_F + k0:SHIFT_F + k0 + 8]
            th.append(act(yh[:, k0:k0 + 8, c], src, ACT.Copy, [tsh, after]))
            tl.append(tt(yl[:, k0:k0 + 8, c], src, f32(yh[:, k0:k0 + 8, c]), ALU.subtract, [tsh, th, after]))
        return [th, tl]

    def gains(k0):
        sl = slice(k0, k0 + 8)
        gate_tok.append(gain(mul[:, 1, sl], GATE_A + k0, 8, v_("g_attn_post", k0, 8), False))
        scale_tok.append(gain(mul[:, 2, sl], SCALE_F + k0, 8, v_("g_ffn_pre", k0, 8), True))

    gate_tok, scale_tok = [], []
    gains(0)
    rm_tok = rms_of_sum(Rm, T, [])
    y_guard = [(PE.sem, PE.n)]
    def residual_chunks(m, s_of, R, Rtok, gain_of, after, yh, yl, n, extra):
        lows = []
        for kc in range(KC):
            add_residual(m, kc, s_of(kc), R, [Rtok], m_tok[kc])
            if lows:
                lows.pop()()
            g = gain_of(kc)
            a = act(yh[:, kc, 0:n], X[:, kc, 0:n], ACT.Copy, [x_tok[kc], after], scale=g)
            square_in(X[:, kc, 0:n], n, [x_tok[kc], meta_load], kc == 0)

            def low(kc=kc, g=g, a=a):
                l = stt(yl[:, kc, 0:n], X[:, kc, 0:n], g, f32(yh[:, kc, 0:n]), ALU.mult, ALU.subtract, [x_tok[kc], after, a])
                y_tok[kc] = [a, l, extra(kc)]
            lows.append(low)
            if kc % 8 == 7:
                lows.pop()()
            yield

    chunks = residual_chunks(m1, lambda kc: mul[:, 1, kc:kc + 1], Rm, [rm_tok, gate_tok], lambda kc: mul[:, 2, kc:kc + 1],
                             [scale_tok, y_guard], yh, yl, T, lambda kc: [shift_tok] if kc < 8 else [])

    next(chunks)
    shift_tok = shift_columns(0, [y_guard, x_tok[0]])
    upto = [7]

    def ahead(kc, n):
        while min(kc + n, upto[0]) not in y_tok:
            next(chunks)

    def all_chunks():
        for _ in chunks:
            pass

    gb4 = Banks([0, 1, 2, 3])
    ab = Banks([4, 5, 6, 7])
    hid_tok = {}
    hid_free = []
    HALF2 = 54

    partg = place([P, FP, T], F32, HID, "partg")
    partu = place([P, FP, T], F32, HID + 45056, "partu")
    pcol = F([P, 2 * FP], F32, "pcol")
    pg_tok = {}

    def part_done(mat, fb, b, bank, tok):
        dst = (partg if mat == "gate" else partu)[:, fb, :]
        i = 2 * fb + (mat == "up")
        t = act(dst, bank[:, 0:T], ACT.Copy, [tok, part_free])
        t2 = act(pcol[:, i:i + 1], bank[:, T:T + 1], ACT.Copy, [tok])
        give(b, t, t2)
        pg_tok[mat, fb] = [t, t2]

    def glu_rest(mat, fb, b, bank, tok):
        i = 2 * fb + (mat == "up")
        k, z, fr = (zr if mat == "gate" else ur).take()
        c = tc[:, 4 * (i % 2) + fb % 4:4 * (i % 2) + fb % 4 + 1]
        ci = 4 * (i % 2) + fb % 4
        src = (partg if mat == "gate" else partu)[:, fb, :]
        t = tt(z[:, 0:T], bank[:, 0:T], src, ALU.add, [tok, fr, pg_tok[mat, fb]])
        t2 = tt(c, bank[:, T:T + 1], pcol[:, i:i + 1], ALU.add, [tok, tc_free[ci]])
        give(b, t, t2)
        m = tt(z[:, 0:T], z[:, 0:T], R2[:, 0:T], ALU.mult, [t, r2_tok], G)
        if mat == "gate":
            def silu():
                s = act(z[:, 0:T], z[:, 0:T], ACT.Silu, [m, t2], bias=c)
                tc_free[ci] = [s]
                gates[fb] = (k, z, s, t)
            later(1, silu)
            return
        def product():
            gk, g, s, tg = gates.pop(fb)
            hk, h, hf = hr.take()
            p = stt(h[:, :], z[:, :], c, g[:, 0:T], ALU.add, ALU.mult, [m, t2, s, hf])
            tc_free[ci] = [p]
            zr.give(gk, p)
            ur.give(k, p)

            def high():
                a = act(hidh[:, fb, :], h[:, :], ACT.Copy, [p, hid_free, tg, t])

                def low():
                    l = tt(hidl[:, fb, :], h[:, :], f32(hidh[:, fb, :]), ALU.subtract, [a, hid_free, t])
                    hr.give(hk, l)
                    hid_tok[fb] = [a, l]
                later(1, low)
            later(1, high)
        later(1, product)

    gates = {}

    def glu_done(conv):
        gate_done = {}

        def done(mat, fb, b, bank, tok):
            if mat in ("gate", "gate2"):
                k, z, fr = zr.take()
                if not conv:
                    t = tt(z[:, 0:T], bank[:, 0:T], R2[:, 0:T], ALU.mult, [tok, r2_tok, fr])
                    c = tc[:, fb % 4:fb % 4 + 1]
                    t2 = V.put(lambda e: e.tensor_copy(c, bank[:, T:T + 1]), [tok, tc_free[fb % 4]])
                    s = act(z[:, 0:T], z[:, 0:T], ACT.Silu, [t, t2], bias=c)
                    tc_free[fb % 4] = [s]
                    give(b, t, t2)
                else:
                    t = tt(z[:, 1:T + 1], bank[:, 0:T], R2[:, 0:T], ALU.mult, [tok, r2_tok, fr])
                    t2 = tt(z[:, 0:1], bank[:, T:T + 1], R2[:, T:T + 1], ALU.mult, [tok, r2_tok, fr])
                    give(b, t, t2)
                    ck, c, cf = cr.take()
                    w = [v_("conv_w_2", FC * i + fb) for i in range(3)]
                    u = ts(c[:, :], z[:, 1:T + 1], w[1], v_("conv_b_2", fb), ALU.mult, ALU.add, [t, cf])
                    u = stt(c[:, :], z[:, 0:T], w[0], c[:, :], ALU.mult, ALU.add, [u, t2])
                    u = stt(c[:, :], z[:, 2:T + 2], w[2], c[:, :], ALU.mult, ALU.add, [u])
                    s = act(z[:, 1:T + 1], c[:, :], ACT.Silu, [u])
                    cr.give(ck, s)
                gate_done[fb] = (k, z, s)
                return
            k, z, s = gate_done.pop(fb)
            uk, u, uf = ur.take()
            c = tc[:, 4 + fb % 4:5 + fb % 4]
            t2 = [] if conv else V.put(lambda e: e.tensor_copy(c, bank[:, T:T + 1]), [tok, tc_free[4 + fb % 4]])
            t = tt(u[:, :], bank[:, 0:T], R2[:, 0:T], ALU.mult, [tok, r2_tok, uf])
            give(b, t, t2)
            hk, h, hf = hr.take()
            if not conv:
                t = stt(h[:, :], u[:, :], c, z[:, 0:T], ALU.add, ALU.mult, [t, t2, s, hf])
                tc_free[4 + fb % 4] = [t]
            else:
                t = tt(h[:, :], u[:, :], z[:, 1:T + 1], ALU.mult, [t, s, hf])
            zr.give(k, t)
            ur.give(uk, t)
            a = act(hidh[:, fb, :], h[:, :], ACT.Copy, [t, hid_free])

            def rest():
                l = tt(hidl[:, fb, :], h[:, :], f32(hidh[:, fb, :]), ALU.subtract, [a, hid_free])
                hr.give(hk, l)
                hid_tok[fb] = [a, l]
            later(1, rest)
        return done

    def y_moving(mat, kc):
        ahead(kc, 2)
        return yh[:, kc, :], yl[:, kc, :], y_tok[kc]

    def hid_moving(mat, kc):
        return hidh[:, kc, :], hidl[:, kc, :], hid_tok[kc]

    def after_first(gen, n, fn):
        for i, _ in enumerate(gen):
            if i == n:
                fn()

    def ffn1_norm():
        nonlocal r2_tok
        all_chunks()
        zr.free[0] = [x_tok[15]]
        r2_tok = rms_of_sum(R2, T, guard1)
        table("silu_and_others")

    part_free = [y_guard]
    halves.update(gate=8, up=8)
    for i, _ in enumerate(gemm(2 * FP, gb4, y_moving, lambda m, f: TQ, part_done)):
        if i == HALF2:
            gains(8)
            upto[0] = 15
        if i > HALF2 and (i - HALF2) % 2 == 0 and 15 not in y_tok:
            next(chunks)
    all_chunks()
    shift_tok = shift_columns(8, [y_tok[15], x_tok[15], y_guard])
    for kc in range(8, KC):
        y_tok[kc].append(shift_tok)
    zr.free[0] = [x_tok[15]]
    r2_tok = rms_of_sum(R2, T, guard1)
    table("silu_and_others")
    for _ in gemm(2 * FP, gb4, y_moving, lambda m, f: TQ, glu_rest):
        pass
    halves.clear()
    for _ in gemm(4 * (FC - FP), gb4, y_moving, lambda m, f: TQ, glu_done(False)):
        pass
    drain()

    m2 = place([P, KC, T], F32, R0, "m2")
    y_free = [(PE.sem, PE.n)]

    def down_done(mat, fb, b, bank, tok):
        s = square_in(bank[:, 0:T], T, [tok], fb == 0)
        t = act(m2[:, fb, :], bank[:, 0:T], ACT.Copy, [tok, y_free])
        give(b, s, t)
        m_tok[fb] = [t]

    table("natural_log_exp_and_others")
    gate_tok = gain(mul[:, 3, :], GATE_F, 16, v_("g_ffn_post", 0, 16), False)
    for _ in gemm(88, gb, hid_moving, lambda m, f: T, down_done):
        pass
    drain()
    rm_tok = rms_of_sum(Rm, T, [zr.free[0]])
    rm_users = []

    B2 = Region(R0)
    B2.at = R0 + 16384
    gh = place([P, KC, TM], F32R, HID, "gh")
    gl = place([P, KC, TM], F32R, HID + 17408, "gl")
    hid_used = [(PE.sem, PE.n)]
    y_tok.clear()
    chunks = residual_chunks(lambda kc: m2[:, kc, :], lambda kc: mul[:, 3, kc:kc + 1], Rm, [rm_tok, gate_tok], lambda kc: v_("mix_norm_g_2", kc),
                             [hid_used, vec_load, meta_load], gh, gl, TM, lambda kc: [])
    next(chunks)
    next(chunks)

    TD = TM - T
    guard2 = [(V.sem, V.n), (A.sem, A.n), (PE.sem, PE.n), (G.sem, G.n)]
    RA = Region(R0, R0 + 33024)
    kn = RA([P, 8, TM], F32, "kn")
    qn = RA([P, 8, TQ], F32, "qn")
    vm = RA([P, 3, 1024], F32, "vm")
    cs2 = RA([P, 2, TM], F32, "cs2")
    kpr = RA([P, TM], F32, "kpr")
    mb2 = RA([P, 8, TD], F32, "mb2")
    outa = place([P, 8, TQ], F32, R0, "outa")
    RB = Region(HID + 34816, TMP)
    krz = RB([P, 8, TM], F32, "krz")
    qr = RB([P, 4, TQ], F32, "qr")
    b_at = RB.at
    cq = RB([P, 4, TQ], F32, "cq")
    ckv = RB([P, 2, TM], F32, "ckv")
    cqh = RB([P, 4, TQ], F32R, "cqh")
    cql = RB([P, 4, TQ], F32R, "cql")
    ckh = RB([P, 2, TM], F32R, "ckh")
    ckl = RB([P, 2, TM], F32R, "ckl")
    mbh = place([P, 8, TQ], F32R, b_at, "mbh")
    mbl = place([P, 8, TQ], F32R, b_at + 8256, "mbl")
    naq = [RB([P, TQ], F32, "naq") for _ in range(3)]
    nak = [RB([P, TM], F32, "nak") for _ in range(3)]
    nav = [RB([P, 3, P], F32, "nav") for _ in range(3)]
    bt = Ring([RB([P, 2, TM], F32, "bt")])
    kpsq = place([P, TM], F32, RB.at, "kpsq")
    tz = Ring([RB([P, 6, 64], F32, "tz")])
    revt = causal[:, 0:P]
    er2 = Ring([RB([P, 2, TM], F32, "er2") for _ in range(2)])
    em = Ring([RB([P, TM], F32, "em") for _ in range(2)])
    tmpr = Ring([RB([P, TM], F32, "tmp") for _ in range(2)])
    RC = Region(TMP + 3 * 1088, LIMIT - 1088)
    pt2 = Ring([RC([P, 3, TQ], F32, "pt2") for _ in range(2)])
    rhr = Ring([RC([P, TM], F32, "rh") for _ in range(2)])
    mah = place([P, 8, TQ], F32R, HID, "mah")
    mal = place([P, 8, TQ], F32R, HID + 8256, "mal")
    for ring in (bt, tz, er2, em, tmpr, pt2, rhr):
        for k in ring.free:
            ring.free[k] = list(guard2)
    nar = Ring([0, 1, 2], {k: list(guard2) for k in range(3)})

    zero2 = [memset(krz[:, :, :], 0.0, guard2), memset(vm[:, 2, :], 0.0, guard2)]
    zero2 += [memset(b[:, 2, :], 0.0, guard2) for b in nav]
    cs_load = load(cs2[:, :, :], rope2, "ld_rope2", after=guard2)
    rev_load = load(revt, rev, "ld_rev", after=guard2)
    mb_load = load(mb2[:, :, :], bass.AP(mbias.tensor, 0, [[0, P], [1, 8 * TD]]), "ld_mb", after=guard2)
    naq_gain = small[:, 3:4]
    ng_tok = ts(naq_gain, v_("na_q_g_2"), float(128 ** -0.5), None, ALU.mult, None, [vec_load], G)
    SM = float(192 ** -0.5)

    tz_sem = [sem(f"tz{i}") for i in range(2)]

    def bias_load(h):
        k, Z, fr = tz.take()
        toks = []
        for a in range(2):
            src = bass.AP(rpb.tensor, (h * 15 + 4 + a) * RPB_ROW + 16, [[1, 64], [RPB_ROW, 6], [1, 64]])
            SP.put(lambda q, a=a, src=src: q.dma_start(Z[64 * a:64 * a + 64, :, :], src).then_inc(tz_sem[a], 16), fr, signal=False)
            toks.append((tz_sem[a], 16 * (h + 1)))
        return k, Z, toks

    def bias_tile(h):
        zk, Z, ztok = B_["tz", h]
        b, bank, free = ab.take()
        p = mm(bank[:, 0:384], revt, Z[:, :, :].rearrange("p j c -> p (j c)"), True, True, [free, ztok, rev_load], signal=True)
        tz.give(zk, p)
        if h + 1 < 8:
            B_["tz", h + 1] = bias_load(h + 1)
        k, B, fr = bt.take()
        mask = namask.unsqueeze(1).to_broadcast([P, 4, 64])
        toks = []
        for qb in range(2):
            src = bank[:, 128 - 128 * qb:384 - 128 * qb].rearrange("p (j c) -> p j c", j=4)
            toks.append(tt(B[:, qb, 0:T].rearrange("p (j c) -> p j c", j=4), src, mask, ALU.add, [p, fr]))
        give(b, toks)
        toks.append(G.put(lambda e: e.tensor_copy(B[:, :, T:TM], mb2[:, h, :].unsqueeze(1).to_broadcast([P, 2, TD])), [mb_load, fr]))
        return k, B, toks

    def head_rms(sq, n, after, div):
        b, bank, free = ab.take()
        t = mm(bank[:, 0:n], ones[:, :], sq[:, 0:n], True, True, [free, after], signal=True)
        k, R, fr = rhr.take()
        a, e = rms(R[:, 0:n], bank[:, 0:n], div, [t, fr])
        give(b, a)
        return k, R, t, e

    def rotate2(dst, n, after, then):
        k, a, fr = tmpr.take()
        t = tt(a[:, 0:n], dst, cs2[:, 1, 0:n], ALU.mult, [after, fr, cs_load], G)
        u = tt(dst, dst, cs2[:, 0, 0:n], ALU.mult, [after, t, cs_load], G)

        def f():
            b, bank, free = ab.take()
            p = mm(bank[:, 0:n], swap, a[:, 0:n], True, True, [free, t], signal=True)
            tmpr.give(k, p)
            r = tt(dst, bank[:, 0:n], dst, ALU.add, [p, u])
            give(b, r)
            then(r)
        later(1, f)

    B_ = {}

    def cq_done(mat, fb, b, bank, tok):
        if fb < CKV:
            i = fb - CQ
            t = tt(cq[:, i, :], bank[:, 0:TQ], R2[:, 0:TQ], ALU.mult, [tok, r2_tok, guard2])
            give(b, t)
            square_in(cq[:, i, :], TQ, [t], i == 0)
            B_["cq", i] = t
            if i == 3:
                def f():
                    k, R, fr = rhr.take()
                    e = rms_of_sum(R, TQ, [fr], 512)
                    last = []
                    for i in range(4):
                        t = stt(cq[:, i, :], cq[:, i, :], v_("mla_cq_g_2", i), R[:, 0:TQ], ALU.mult, ALU.mult, [e, B_["cq", i]])
                        a = act(cqh[:, i, :], cq[:, i, :], ACT.Copy, [t, guard2])
                        l = tt(cql[:, i, :], cq[:, i, :], f32(cqh[:, i, :]), ALU.subtract, [t, a])
                        B_["cqn", i] = [a, l]
                        last.append(t)
                    rhr.give(k, last)
                later(2, f)
        elif fb < KPE:
            i = fb - CKV
            t = tt(ckv[:, i, :], bank[:, 0:TM], R2[:, :], ALU.mult, [tok, r2_tok, guard2])
            give(b, t)
            square_in(ckv[:, i, :], TM, [t], i == 0)
            B_["ckv", i] = t
            if i == 1:
                def f():
                    k, R, fr = rhr.take()
                    e = rms_of_sum(R, TM, [fr], 256)
                    last = []
                    for i in range(2):
                        t = stt(ckv[:, i, :], ckv[:, i, :], v_("mla_ckv_g_2", i), R[:, :], ALU.mult, ALU.mult, [e, B_["ckv", i]])
                        a = act(ckh[:, i, :], ckv[:, i, :], ACT.Copy, [t, guard2])
                        l = tt(ckl[:, i, :], ckv[:, i, :], f32(ckh[:, i, :]), ALU.subtract, [t, a])
                        B_["ckn", i] = [a, l]
                        last.append(t)
                    rhr.give(k, last)
                later(1, f)
        else:
            t = tt(kpr[:, :], bank[:, 0:TM], R2[:, :], ALU.mult, [tok, r2_tok, guard2])
            give(b, t)
            s = act(kpsq[:, :], kpr[:, :], ACT.Square, [t, guard2])
            s = ts(kpsq[:, :], kpsq[:, :], 0.5, None, ALU.mult, None, [s], G)
            B_["kpsq"] = s
            t = ts(kpr[:, :], kpr[:, :], v_("mk_r"), None, ALU.mult, None, [t, s])

            rotate2(kpr[:, :], TM, [t], lambda r: B_.update({"kpr": r}))

    def g_moving(mat, kc):
        ahead(kc, 2)
        return gh[:, kc, :], gl[:, kc, :], y_tok[kc]

    def in2_width(mat, fb):
        return TQ if fb < KA or CQ <= fb < CKV else TM

    def chain(mat, fb, b, bank, tok):
        cq_done(mat, fb, b, bank, tok)

    def in2_norm():
        nonlocal r2_tok
        all_chunks()
        zr.free[0] = [x_tok[15]]
        zero2.extend(memset(b[:, :, :], 0.0, [guard2, x_tok[15], y_tok[15]]) for b in pt2.items)
        r2_tok = rms_of_sum(R2, TM, [hid_tok[FC - 1]])

    after_first(gemm(8, gb4, g_moving, in2_width, chain), 6, in2_norm)
    ab = Banks([3, 4, 5, 6, 7])
    for _ in gemm(6, gb, g_moving, in2_width, chain):
        pass

    def q_done(mat, fb, b, bank, tok):
        p, r = divmod(fb, 3)
        if r == 0:
            t = ts(qr[:, p, :], bank[:, 0:TQ], v_("mq_r"), None, ALU.mult, None, [tok, guard2])
            k, s, fr = tmpr.take()
            a = act(s[:, 0:TQ], bank[:, 0:TQ], ACT.Square, [t, fr])
            give(b, a)
            B_["sqr", p] = (k, s, a)

            rotate2(qr[:, p, :], TQ, [t], lambda r: B_.update({("qr", p): r}))
            return
        h = 2 * p + r - 1
        t = V.put(lambda e: e.tensor_copy(qn[:, h, :], bank[:, 0:TQ]), [tok, guard2])
        give(b, t)
        k, sq, fr = sqf.take()
        a = act(sq[:, 0:TQ], qn[:, h, :], ACT.Square, [t, fr])
        half = slice(64 * (h % 2), 64 * (h % 2) + 64)
        rk, rs, ra = B_["sqr", p]
        t2 = tt(sq[half, 0:TQ], sq[half, 0:TQ], rs[half, 0:TQ], ALU.add, [a, ra])
        if r == 2:
            tmpr.give(rk, t2, B_["rs0"])
        B_["rs0"] = t2

        def f():
            k2, R, t3, e = head_rms(sq, TQ, [t2], 192)
            sqf.give(k, t3)
            u = stt(qn[:, h, :], qn[:, h, :], v_("mq_n"), R[:, 0:TQ], ALU.mult, ALU.mult, [e])
            w = tt(qr[half, p, :], qr[half, p, :], R[half, 0:TQ], ALU.mult, [e, B_["qr", p]])
            rhr.give(k2, u, w)
            B_["q", h] = [u, w]
        later(1, f)

    def k_done(mat, fb, b, bank, tok):
        h, r = divmod(fb, 2)
        if r == 0:
            t = V.put(lambda e: e.tensor_copy(kn[:, h, :], bank[:, 0:TM]), [tok, guard2])
            give(b, t)
            k, sq, fr = sqf.take()
            a = act(sq[:, :], kn[:, h, :], ACT.Square, [t, fr])
            t2 = tt(sq[:, :], sq[:, :], kpsq[:, :], ALU.add, [a, B_["kpsq"]], G)
            half = slice(64 * (h % 2), 64 * (h % 2) + 64)
            B_["kpsq_used"] = t2

            def f():
                k2, R, t3, e = head_rms(sq, TM, [t2], 192)
                sqf.give(k, t3)
                u = stt(kn[:, h, :], kn[:, h, :], v_("mk_n"), R[:, :], ALU.mult, ALU.mult, [e])
                w = tt(krz[half, h, :], kpr[half, :], R[half, :], ALU.mult, [e, B_["kpr"], zero2])
                rhr.give(k2, u, w)
                B_["k", h] = [u, w]
            later(1, f)
            return
        k, v, fr = tmpr.take()
        t = act(v[:, :], bank[:, 0:TM], ACT.Copy, [tok, fr])
        give(b, t)

        def f():
            c = slice(P * h, P * h + P)
            p, e = values(v, t, vm[:, 0:2, c], vm[0:16, 2, c])
            tmpr.give(k, p)
            B_["v", h] = e
        later(1, f)

    def values(v, after, dst, dst_meta):
        b, bank, free = ab.take()
        tr(bank[:, 0:P], v[:, 0:P], [free, after])
        tr(bank[:, P:2 * P], v[:, P:2 * P])
        p = tr(bank[0:TD, 2 * P:3 * P], v[:, T:TM], signal=True)
        e0 = act(dst, bank[:, 0:2 * P].rearrange("p (k d) -> p k d", k=2), ACT.Copy, [p, guard2])
        e1 = act(dst_meta, bank[0:TD, 2 * P:3 * P], ACT.Copy, [p, zero2])
        give(b, e0, e1)
        return p, [e0, e1]

    def cq_moving(mat, kc):
        return cqh[:, kc, :], cql[:, kc, :], B_["cqn", kc]

    def ck_moving(mat, kc):
        return ckh[:, kc, :], ckl[:, kc, :], B_["ckn", kc]

    for _ in gemm(6, gb, cq_moving, lambda m, f: TQ, q_done):
        pass
    for _ in gemm(4, gb, ck_moving, lambda m, f: TM, k_done):
        pass
    kv_done_pe = [(PE.sem, PE.n)]

    def normalise(d):
        E, M, c, mk = d["E"], d["M"], d["c"], d["mk"]
        t = V.put(lambda e: e.reciprocal(stat[:, c:c + 2], stat[:, c + 3:c + 5]), [d["es"][0:2]])
        t2 = V.put(lambda e: e.reciprocal(stat[0:1, c + 2:c + 3], stat[0:1, c + 5:c + 6]), [d["es"][2]])
        ns = [ts(E[:, qb, :], E[:, qb, :], stat[:, c + qb:c + qb + 1], None, ALU.mult, None, [t]) for qb in range(2)]
        ns.append(ts(M[0:1, mk], M[0:1, mk], stat[0:1, c + 2:c + 3], None, ALU.mult, None, [t2]))
        d["ns"] = ns

    def turn_p2(d):
        E, M, mk, ns = d["E"], d["M"], d["mk"], d["ns"]
        b, bank, free = ab.take()
        for kc in range(2):
            for qb in range(2):
                p = tr(bank[:, T * kc + P * qb:T * kc + P * qb + P], E[:, qb, P * kc:P * kc + P], [free, ns[qb]],
                       signal=(kc == 1 and qb == 1))
        b2, bank2, free2 = ab.take()
        for qb in range(2):
            tr(bank2[0:TD, P * qb:P * qb + P], E[:, qb, T:TM], [free2])
        full = mk.stop > TD
        if full:
            for kc in range(2):
                tr(bank2[:, T + kc:T + kc + 1], M[0:1, P * kc:P * kc + P], [ns[2]])
            p2 = tr(bank2[0:TD, T + 2:T + 3], M[0:1, T:TM], signal=True)
        else:
            p2 = tr(bank2[0:TD, T + 2:T + 3], M[0:1, 0:TD], [ns[2]], signal=True)
        er2.give(d["er"], p2)
        em.give(d["emk"], p2)
        r, buf, fr = pt2.take()
        es = [act(buf[:, 0:2, 0:T], bank[:, :].rearrange("p (k q) -> p k q", k=2), ACT.Copy, [p, fr, zero2])]
        give(b, es[0])
        es.append(act(buf[0:TD, 2, 0:T], bank2[0:TD, 0:T], ACT.Copy, [p2, fr, zero2]))
        es.append(act(buf[0:TD, 2, T:T + 1], bank2[0:TD, T + 2:T + 3], ACT.Copy, [p2]))
        if full:
            es.append(act(buf[:, 0:2, T:T + 1], bank2[:, T:T + 2].unsqueeze(2), ACT.Copy, [p2]))
        give(b2, es[1:])
        d.update(pr=r, buf=buf, ps=es)

    def out_of(d, dst, after, first):
        b, bank, p = d["ob"]
        s = square_in(bank[:, 0:TQ], TQ, [p], first)
        a = act(dst, bank[:, 0:TQ], ACT.Copy, [p, after])
        give(b, s, a)
        return a

    mla, na = {}, {}

    def exps(d):
        E, M, c, mk, vs = d["E"], d["M"], d["c"], d["mk"], d["vs"]
        es = [act(E[:, qb, :], E[:, qb, :], ACT.Exp, [vs[qb]], scale=-1.0, bias=stat[:, c + qb:c + qb + 1],
                  accum_out=stat[:, c + 3 + qb:c + 4 + qb]) for qb in range(2)]
        es.append(act(M[0:1, mk], M[0:1, mk], ACT.Exp, [vs[2]], scale=-1.0, bias=stat[0:1, c + 2:c + 3],
                      accum_out=stat[0:1, c + 5:c + 6]))
        d["es"] = es

    def mla_steps():
        def s0(h):
            while not all((k, h) in B_ for k in ("q", "k", "v")):
                yield
            er, E, fr = er2.take()
            emk, M, fr2 = em.take()
            c = 8 * (h % 4)
            vs = []
            for i, q in enumerate((slice(0, P), slice(P, T), slice(T, T + 1))):
                b, bank, free = ab.take()
                m = 1 if i == 2 else P
                mm(bank[0:m, 0:TM], qn[:, h, q], kn[:, h, :], True, False, [free, B_["q", h], B_["k", h]])
                p = mm(bank[0:m, 0:TM], qr[:, h // 2, q], krz[:, h, :], False, True, signal=True)
                dst = M[0:1, :] if i == 2 else E[:, i, :]
                f2 = fr2 if i == 2 else fr
                v = ts(dst, bank[0:m, 0:TM], -SM, None, ALU.mult, ALU.min, [p, f2], accum_out=stat[0:m, c + i:c + i + 1])
                give(b, v)
                vs.append(v)
            d = mla[h] = dict(E=E, M=M, c=c, mk=slice(0, TM), vs=vs, er=er, emk=emk)
            exps(d)

        def s1(h):
            normalise(mla[h])

        def s1b(h):
            turn_p2(mla[h])

        def s2(h):
            d = mla[h]
            b, bank, free = ab.take()
            for kc in range(3):
                p = mm(bank[:, 0:TQ], vm[:, kc, P * h:P * h + P], d["buf"][:, kc, :], kc == 0, kc == 2,
                       [free, d["ps"], B_["v", h]], signal=(kc == 2))
            pt2.give(d["pr"], p)
            d["ob"] = (b, bank, p)
            B_["outb", h] = out_of(d, qn[:, h, :], [p], h == 0)

        yield from lock([s0, s1, s1b, s2], 8)
        yield
        k, R, fr = rhr.take()
        e = rms_of_sum(R, TQ, [fr], 1024)
        yield
        for h in range(8):
            t = stt(qn[:, h, :], qn[:, h, :], v_("mla_out_g_2", h), R[:, 0:TQ], ALU.mult, ALU.mult, [e, B_["outb", h]])
            a = act(mbh[:, h, :], qn[:, h, :], ACT.Copy, [t, kv_done_pe])
            l = tt(mbl[:, h, :], qn[:, h, :], f32(mbh[:, h, :]), ALU.subtract, [t, a, kv_done_pe])
            B_["mix", 8 + h] = [a, l]
            if h % 2:
                yield
        rhr.give(k, t)
        B_["mla"] = True

    def na_done(mat, fb, b, bank, tok):
        kind, h = divmod(fb, 8)
        if kind == 0:
            force(lambda: nar.free[nar.i] is not None)
            k, _, fr = nar.take()
            B_["na", h] = (k, fr)
        k, fr = B_["na", h]
        n = TQ if kind == 0 else TM
        if kind < 2:
            dst = (naq, nak)[kind][k]
            t = tt(dst[:, :], bank[:, 0:n], R2[:, 0:n], ALU.mult, [tok, r2_tok, fr])
            give(b, t)
            sk, sq, sf = sqf.take()
            a = act(sq[:, 0:n], dst[:, :], ACT.Square, [t, sf])

            def f():
                k2, R, t3, e = head_rms(sq, n, [a], 128)
                sqf.give(sk, t3)
                g = naq_gain if kind == 0 else v_("na_k_g_2")
                u = stt(dst[:, :], dst[:, :], g, R[:, 0:n], ALU.mult, ALU.mult, [e, ng_tok])
                rhr.give(k2, u)
                B_["naqk"[0:2] + str(kind), h] = u
            later(1, f)
            return
        tk, v, tf = tmpr.take()
        t = tt(v[:, :], bank[:, 0:TM], R2[:, :], ALU.mult, [tok, r2_tok, tf])
        give(b, t)
        B_["r2_used"] = t

        def f():
            p, e = values(v, [t, fr], nav[k][:, 0:2, :], nav[k][0:TD, 2, :])
            tmpr.give(tk, p)
            B_["nav", h] = e
        later(1, f)

    def na_steps():
        def s0(h):
            while not (("nav", h) in B_ and "mla" in B_):
                yield
            k, fr = B_["na", h]
            bk, B, btok = bias_tile(h)
            er, E, fr = er2.take()
            emk, M, fr2 = em.take()
            c = 8 * (h % 4)
            vs = []
            for i, q in enumerate((slice(0, P), slice(P, T), slice(T, T + 1))):
                b, bank, free = ab.take()
                toks = [free, B_["na0", h], B_["na1", h]]
                if i < 2:
                    p = mm(bank[:, 0:TM], naq[k][:, q], nak[k][:, :], True, True, toks, signal=True)
                    v = ttr(E[:, i, :], bank[:, 0:TM], B[:, i, :], -1.0, BIG, ALU.add, ALU.min, stat[:, c + i:c + i + 1],
                            [p, btok, fr])
                else:
                    p = mm(bank[0:1, 0:TD], naq[k][:, q], nak[k][:, T:TM], True, True, toks, signal=True)
                    v = ttr(M[0:1, 0:TD], bank[0:1, 0:TD], B[0:1, 0, T:TM], -1.0, BIG, ALU.add, ALU.min,
                            stat[0:1, c + i:c + i + 1], [p, btok, fr2])
                give(b, v)
                vs.append(v)
            bt.give(bk, vs)
            d = na[h] = dict(E=E, M=M, c=c, mk=slice(0, TD), vs=vs, er=er, emk=emk)
            exps(d)

        def s1(h):
            normalise(na[h])

        def s1b(h):
            turn_p2(na[h])

        def s2(h):
            d = na[h]
            k, _ = B_["na", h]
            b, bank, free = ab.take()
            mm(bank[:, 0:TQ], nav[k][:, 2, :], d["buf"][:, 2, :], True, False, [free, d["ps"], B_["nav", h]])
            for kc in range(2):
                p = mm(bank[:, 0:T], nav[k][:, kc, :], d["buf"][:, kc, 0:T], False, kc == 1, signal=(kc == 1))
            pt2.give(d["pr"], p)
            nar.give(k, p)
            d["ob"] = (b, bank, p)
            B_["outa", h] = out_of(d, outa[:, h, :], [B_["outb", 7]], h == 0)

        yield from lock([s0, s1, s1b, s2], 8)
        yield
        k, R, fr = rhr.take()
        e = rms_of_sum(R, TQ, [fr], 1024)
        yield
        for h in range(8):
            t = stt(outa[:, h, :], outa[:, h, :], v_("na_out_g_2", h), R[:, 0:TQ], ALU.mult, ALU.mult, [e, B_["outa", h]])
            a = act(mah[:, h, :], outa[:, h, :], ACT.Copy, [t, in2_pe])
            l = tt(mal[:, h, :], outa[:, h, :], f32(mah[:, h, :]), ALU.subtract, [t, a, in2_pe])
            B_["mix", h] = [a, l]
            if h % 2:
                yield
        rhr.give(k, t)

    sides = []

    def step_sides():
        for s in list(sides):
            if next(s, "end") == "end":
                sides.remove(s)

    def force(cond):
        n = 0
        while not cond():
            step_sides()
            n += 1
            assert n < 200, "stuck"

    def run_with(main, rate):
        credit = 0.0
        for _ in main:
            credit += rate
            while credit >= 1.0:
                credit -= 1.0
                step_sides()

    in2_pe = []
    sides += [mla_steps(), na_steps()]
    tz.free[0] = [guard2, B_["kpsq_used"]]
    B_["tz", 0] = bias_load(0)
    run_with(gemm(48, gb, g_moving, in2_width, na_done), 0.8)
    in2_pe.append((PE.sem, PE.n))
    drain()
    force(lambda: "mla" in B_)

    halves["out2"] = 8

    def mix_moving(mat, kc):
        return (mbh[:, kc - 8, :], mbl[:, kc - 8, :], B_["mix", kc]) if kc >= 8 else (mah[:, kc, :], mal[:, kc, :], B_["mix", kc])

    def out_first(mat, fb, b, bank, tok):
        t = tt(X[:, fb, 0:TQ], bank[:, 0:TQ], X[:, fb, 0:TQ], ALU.add, [tok, x_tok[fb]])
        give(b, t)
        x_tok[fb] = [t]

    run_with(gemm(16, gb, mix_moving, lambda m, f: TQ, out_first), 1.0)
    n = 0
    while sides:
        step_sides()
        tick()
        n += 1
        assert n < 500
    guard3 = [(V.sem, V.n), (A.sem, A.n), (PE.sem, PE.n), (G.sem, G.n)]
    for ring in (zr, ur, hr, cr):
        for k in ring.free:
            ring.free[k] = list(guard3)

    def out_second(mat, fb, b, bank, tok):
        t = tt(X[:, fb, 0:TQ], bank[:, 0:TQ], X[:, fb, 0:TQ], ALU.add, [tok, x_tok[fb]])
        give(b, t)
        x_tok[fb] = [t]
        operand(yh, yl, fb, TQ, v_("ffn_norm_g_2", fb), [guard3])
        square_in(X[:, fb, 0:TQ], TQ, [t], fb == 0)

    run_with(gemm(16, gb, mix_moving, lambda m, f: TQ, out_second), 1.0)
    halves.clear()
    r2_tok = rms_of_sum(R2, TQ, [B_["r2_used"]])
    table("silu_and_others")
    for i in range(2):
        zt = memset(zr.items[i][:, TQ - 1:TQ], 0.0, guard3)
        zr.free[i] = [guard3, zt]

    ab = Banks([4, 5, 6, 7])
    hid_free = [(PE.sem, PE.n), (A.sem, A.n)]
    for _ in gemm(176, gb4, y_moving, lambda m, f: TQ if m == "gate2" else T, glu_done(True)):
        pass
    drain()

    oring2 = [ur.items[0], ur.items[1], hr.items[0], hr.items[1]]
    ofree = [ur.free[0], ur.free[1], hr.free[0], hr.free[1]]
    osem = [sem(f"out{i}") for i in range(4)]
    ocount = [0] * 4

    def last_done(mat, fb, b, bank, tok):
        k = fb % 4
        o, s = oring2[k], osem[k]
        t = tt(o[:, :], bank[:, 0:T], X[:, fb, 0:T], ALU.add, [tok, x_tok[fb], ofree[k]])
        give(b, t)
        SP.put(lambda q: q.dma_start(out[:, fb, :], o[:, :]).then_inc(s, 16), [t], signal=False)
        ocount[k] += 16
        ofree[k] = [(s, ocount[k])]

    for _ in gemm(88, gb, hid_moving, lambda m, f: T, last_done):
        pass
    assert not st["ready"] and st["done"] == len(plan)
    out_sems = [(osem[k], ocount[k]) for k in range(4)]

    with nc.Block() as block:
        @block.sync
        def _(e):
            SP.emit(e)
            for s, v in out_sems:
                e.wait_ge(s, v)

        @block.tensor
        def _(e):
            PE.emit(e)

        @block.vector
        def _(e):
            V.emit(e)

        @block.scalar
        def _(e):
            A.emit(e)

        @block.gpsimd
        def _(e):
            G.emit(e)


def layout(inputs):
    g = {k: np.asarray(v) for k, v in inputs.items()}

    def part(name, n=None):
        return np.asarray(g[name]).reshape(-1, P).T

    def rows(a):
        return a.T.reshape(KC, P, -1).transpose(1, 0, 2)

    n, r = 128, 64
    conv = g["conv_w_2"][0].reshape(3, FC, P).transpose(2, 0, 1).reshape(P, 3 * FC)
    mq, mk = g["mla_q_g_2"][0], g["mla_k_g_2"][0]
    vec = {"conv_w_2": conv, "mq_n": mq[:n, None], "mk_n": mk[:n, None],
           "mq_r": np.concatenate([mq[n:], mq[n:]])[:, None], "mk_r": np.concatenate([mk[n:], mk[n:]])[:, None]}
    vecs = np.concatenate([vec[k] if k in vec else part(k) for k, _ in VECS], axis=1)
    assert vecs.shape == (P, NVEC)

    w_in = g["w_in"][0]
    w_ada = g["w_ada"][0]
    w_in2 = g["w_in_2"][0]
    kpe = w_in2[:, 3840:3904]
    qup = g["w_q_up_2"][0].reshape(512, 8, 192)
    qcols = []
    for p in range(4):
        a, b = qup[:, 2 * p], qup[:, 2 * p + 1]
        qcols += [a[:, n:], b[:, n:], a[:, :n], b[:, :n]]
    mats = {"o": g["w_o"][0], "gate": g["w_gate"][0], "up": g["w_up"][0], "down": g["w_down"][0],
            "in2": np.concatenate([w_in2, kpe], axis=1), "qup": np.concatenate(qcols, axis=1), "kvup": g["w_kv_up_2"][0],
            "out2": g["w_out_2"][0], "gate2": g["w_gate_2"][0], "up2": g["w_up_2"][0], "down2": g["w_down_2"][0]}
    plan = tile_plan()
    wst = np.zeros((len(plan), P, TILE), np.float32)
    for t, what in enumerate(plan):
        if what[0] == "a":
            c, h = divmod(what[1], 2)
            wst[t] = w_ada[1024 * h:1024 * (h + 1), P * c:P * (c + 1)].T
        elif what[0] == "x":
            _, grp, kp = what
            d = wst[t].reshape(P, 2, 512)
            for i in range(2):
                at = 0
                for a, b in W_IN_GROUPS[grp]:
                    d[:, i, at:at + b - a] = w_in[(2 * kp + i) * P:(2 * kp + i + 1) * P, a:b]
                    at += b - a
        else:
            for i, (m, kc, fb) in enumerate(what[1]):
                wst[t, :, P * i:P * (i + 1)] = mats[m][kc * P:(kc + 1) * P, fb * P:(fb + 1) * P]

    meta = np.concatenate([g["meta_tokens_2"][15:], g["meta_tokens_2"][:15]])
    rpb = np.zeros((8, 15, RPB_ROW), np.float32)
    rpb[:, :, 64:95] = g["na_rpb_2"][0]
    mb = g["na_meta_bias_2"][0]
    mbias = np.concatenate([mb[:, 15:], mb[:, :15]], axis=1)

    ident = np.eye(P, dtype=np.float32)
    swap = np.zeros((P, P), np.float32)
    for hd in (0, 64):
        for j in range(32):
            swap[hd + 32 + j, hd + j] = -1.0
            swap[hd + j, hd + 32 + j] = 1.0
    q, k = np.arange(P)[:, None], np.arange(P)[None, :]
    causal = np.concatenate([np.zeros((P, P)), np.where(k <= q, 0.0, NEG)], axis=1)
    c = np.arange(P) % 64
    start = np.clip(c - 8, 0, 48)[:, None]
    kk = np.arange(64)[None, :]
    namask = np.where((kk >= start) & (kk < start + 16), 0.0, NEG)
    inv = np.power(np.float32(500000.0), -(np.arange(0, 32, 2, dtype=np.float32) / np.float32(32)))
    freq = np.broadcast_to(inv, (P, 16))
    consts = np.concatenate([ident, swap, causal, namask, freq], axis=1).astype(np.float32)
    inv2 = np.power(np.float32(10000.0), -np.arange(0, 64, 2, dtype=np.float32) / np.float32(64)).astype(np.float32)
    posn = np.concatenate([np.arange(16, 272), [15], np.arange(15)]).astype(np.float32)
    angle = (posn[None, :] * inv2[np.arange(P) % 32][:, None]).astype(np.float32)
    rope2 = np.stack([np.cos(angle), np.sin(angle)], axis=1).astype(np.float32)

    return {"wst": wst, "xT": rows(g["x"][0]), "metaT": rows(meta), "vecs": vecs, "consts": consts, "rope2": rope2, "rev": ident[::-1],
            "cvec": g["c"], "positions": g["positions"][0].reshape(2, P).T,
            "lambdas": np.concatenate([g["lambda_q1"], g["lambda_k1"], g["lambda_q2"], g["lambda_k2"]]),
            "rpb": rpb, "mbias": mbias}


def kernel(**inputs):
    import concourse.bacc as bacc
    from concourse.bass_utils import run_bass_kernel_spmd

    nc = bacc.Bacc("TRN2", target_bir_lowering=False, num_devices=1)
    arrays = {f"in_{k}": np.ascontiguousarray(a) for k, a in layout(inputs).items()}
    args = [nc.dram_tensor(k, a.shape, mybir.dt.from_np(a.dtype), kind="ExternalInput").ap() for k, a in arrays.items()]
    args.append(nc.dram_tensor("out_0", (P, KC, T), F32, kind="ExternalOutput").ap())
    build(nc, *args)
    r = run_bass_kernel_spmd(nc, [arrays], core_ids=[0])
    got = r.results[0]["out_0"]
    return np.ascontiguousarray(got.transpose(2, 1, 0).reshape(1, T, KC * P))
```

```python
from contextlib import ExitStack

import numpy as np

import concourse.bass as bass
from concourse import mybir

F32 = mybir.dt.float32
F32R = mybir.dt.float32r
I32 = mybir.dt.int32
ALU = mybir.AluOpType
ACT = mybir.ActivationFunctionType

P = 128
T = 256
TM = 272
TQ = 258
KC = 16
FC = 44
FP = 36
NEG = -1.0e30
USED = -3.0e38
BIG = 3.0e38
TILE = 1024

SHIFT_A, SCALE_A, GATE_A, SHIFT_F, SCALE_F, GATE_F = range(0, 96, 16)

W_IN_GROUPS = [
    [(4352, 4864)],
    [(4864, 5376)],
    [(4096, 4224), (4224, 4352), (5440, 5456), (5376, 5440)],
    [(1024, 1536)],
    [(2048, 2560)],
    [(0, 512)],
    [(1536, 2048)],
    [(2560, 3072)],
    [(512, 1024)],
    [(3072, 3584)],
    [(3584, 4096)],
]
G_COLS = [sum(b - a for a, b in g) for g in W_IN_GROUPS]
IQ0, IQ1, IKS, DK0, DV0, DQ0, DK1, DV1, DQ1, SQ0, SQ1 = range(11)
RATE1, RATE1B = (1.3, 4), (1.2, 4)
PASSES = [(0, 2), (2, 4), (4, 8), (8, 12), (12, 16)]
TOGETHER = [1, 1, 4, 1, 1]
AHEAD = [[((2, 4), 0, 9, 6)], [((4, 6), 0, 10, 7)], [((6, 8), 0, 4, 1), ((8, 12), 4, 19, 16)], [((12, 16), 0, 17, 14)], []]
BY_DVE = (1, 5, 9, 13, 17, 21)
LATE_POOL = {DV1, DQ1, SQ1}


def pass_tiles(p):
    k0, k1 = PASSES[p]
    groups = [list(range(TOGETHER[p]))] + [[g] for g in range(TOGETHER[p], 11)]
    return [(g, kp) for gs in groups for kp in range(k0 // 2, k1 // 2) for g in gs]


QA, KA, VA, CQ, CKV, KPE = 0, 8, 16, 24, 28, 30

OI = 3

UP_AFTER, UP_SHARE = 1, 0.2

KCHUNKS = {"o": 16, "gate": 16, "up": 16, "down": 44, "in2": 16, "qup": 4, "kvup": 2,
           "out2": 16, "gate2": 16, "up2": 16, "down2": 44}

VECS = [("b_ada", 96), ("g_attn_pre", 16), ("g_attn_post", 16), ("g_ffn_pre", 16), ("g_ffn_post", 16),
        ("mix_norm_g_2", 16), ("ffn_norm_g_2", 16), ("conv_w_2", 132), ("conv_b_2", 44),
        ("na_q_g_2", 1), ("na_k_g_2", 1), ("g_diff_sub", 1), ("mla_cq_g_2", 4), ("mla_ckv_g_2", 2),
        ("mq_n", 1), ("mq_r", 1), ("mk_n", 1), ("mk_r", 1), ("na_out_g_2", 8), ("mla_out_g_2", 8)]
VOFF = {}
for _name, _n in VECS:
    VOFF[_name] = sum(n for _, n in VECS[:len(VOFF)])
NVEC = sum(n for _, n in VECS)

CONSTS = [("ident", 128), ("swap", 128), ("causal", 256), ("namask", 64), ("freq", 16)]
COFF = {}
for _name, _n in CONSTS:
    COFF[_name] = sum(n for _, n in CONSTS[:len(COFF)])
NCONST = sum(n for _, n in CONSTS)
RPB_ROW = 160


def spread(main, extra, share=1.0):
    out, done = [], 0
    for i, m in enumerate(main):
        out.append(m)
        upto = min(len(extra), round((i + 1) * len(extra) / (len(main) * share)))
        out += extra[done:upto]
        done = max(done, upto)
    return out + extra[done:]


def blocks(mat, order):
    order = [(mat, kc, fb) for kc, fb in order] if isinstance(mat, str) else order
    assert len(order) % 8 == 0, (mat, len(order))
    return [("b", tuple(order[i:i + 8])) for i in range(0, len(order), 8)]


def tile_plan():
    def ada(c0, n):
        return [("a", 2 * c + h) for c in range(c0, c0 + n) for h in range(2)]

    def ada_pass(k0, k1):
        return ada(SHIFT_A + k0, k1 - k0) + ada(SCALE_A + k0, k1 - k0)

    plan = ada_pass(*PASSES[0])
    for p in range(len(PASSES)):
        tiles = [("x", g, kp) for g, kp in pass_tiles(p)]
        if not AHEAD[p]:
            plan += spread(tiles, ada(GATE_A, 8), 0.8)
            continue
        done = 0
        for ks, t0, t1, _ in AHEAD[p]:
            plan += tiles[done:t0] + spread(tiles[t0:t1], ada_pass(*ks))
            done = t1
        plan += tiles[done:]
    o = []
    for k in (0, 8):
        o += [(kc, fb) for kc in range(k, k + 8) for fb in range(OI)]
        o += [(kc, fb) for fb in range(OI, 16) for kc in range(k, k + 8)]
    o = blocks("o", o)
    plan += spread(o, ada(SHIFT_F, 8) + ada(SCALE_F, 8), 1.0)

    def glu(g, u):
        first = [(m, kc, fb) for kc in range(16) for fb in range(3) for m in (g, u)]
        rest = [(m, kc, fb) for fb in range(3, FC) for m in (g, u) for kc in range(16)]
        return blocks(None, first + rest)

    part = [(m, kc, fb) for kc in range(8) for fb in range(3) for m in ("gate", "up")]
    part += [(m, kc, fb) for fb in range(3, FP) for m in ("gate", "up") for kc in range(8)]
    plan += spread(blocks(None, part), ada(GATE_A + 8, 8) + ada(SHIFT_F + 8, 8) + ada(SCALE_F + 8, 8), 0.8)
    rest = [(m, kc, fb) for fb in range(FP) for m in ("gate", "up") for kc in range(8, 16)]
    rest += [(m, kc, fb) for fb in range(FP, FC) for m in ("gate", "up") for kc in range(16)]
    plan += spread(blocks(None, rest), ada(GATE_F, 16), 0.6)
    plan += blocks("down", [(kc, fb) for fb in range(16) for kc in range(FC)])
    in2 = [(kc, CQ + i) for kc in range(16) for i in range(6)]
    in2 += [(kc, KPE) for kc in range(16)]
    plan += blocks("in2", in2)
    up = []
    for pair in range(4):
        up += [("qup", kc, 3 * pair + i) for i in range(3) for kc in range(4)]
        up += [("kvup", kc, 4 * pair + i) for i in range(4) for kc in range(2)]
    na = blocks("in2", [(kc, fb + h) for h in range(8) for fb in (QA, KA, VA) for kc in range(16)])
    plan += na[:UP_AFTER] + spread(na[UP_AFTER:], blocks(None, up), UP_SHARE)
    plan += blocks("out2", [(kc, fb) for fb in range(16) for kc in range(8, 16)])
    plan += blocks("out2", [(kc, fb) for fb in range(16) for kc in range(8)])
    plan += glu("gate2", "up2")
    plan += blocks("down2", [(kc, fb) for fb in range(16) for kc in range(FC)])
    return plan


def flat(tokens):
    if tokens is None:
        return []
    if isinstance(tokens, tuple) and len(tokens) == 2 and isinstance(tokens[1], int):
        return [tokens]
    return [t for x in tokens for t in flat(x)]


class Engine:

    def __init__(self, sem):
        self.sem, self.n, self.queue, self.seen = sem, 0, [], {}

    def put(self, fn, after=(), signal=True):
        waits = {}
        for sem, value in flat(after):
            if value > self.seen.get(sem.num, 0):
                self.seen[sem.num] = value
                waits[sem.num] = (sem, value)
        if signal:
            self.n += 1
        self.queue.append((fn, list(waits.values()), signal))
        return (self.sem, self.n) if signal else None

    def emit(self, engine):
        for fn, waits, signal in self.queue:
            for sem, value in waits:
                engine.wait_ge(sem, value)
            ins = fn(engine)
            if signal:
                ins.then_inc(self.sem, 1)


class Ring:

    def __init__(self, items, free=None):
        self.items, self.i = items, 0
        self.free = free if free is not None else {k: [] for k in range(len(items))}

    def take(self):
        k = self.i
        self.i = (k + 1) % len(self.items)
        after = self.free[k]
        assert after is not None, "buffer still in use"
        self.free[k] = None
        return k, self.items[k], after

    def give(self, k, *tokens):
        self.free[k] = list(tokens)


def build(nc, wst, xT, metaT, vecs, consts, rope2, rev, cvec, positions, lambdas, rpb, mbias, out):
    ctx = ExitStack()
    with ctx:
        _build(nc, ctx, wst, xT, metaT, vecs, consts, rope2, rev, cvec, positions, lambdas, rpb, mbias, out)


def _build(nc, ctx, wst, xT, metaT, vecs, consts, rope2, rev, cvec, positions, lambdas, rpb, mbias, out):
    def sem(name):
        return ctx.enter_context(nc.semaphore(name))

    BASE = 16512
    LIMIT = 229344
    at = [BASE]
    seq = [0]

    def place(shape, dt, off, name="t"):
        seq[0] += 1
        size = 4
        for s in shape[1:]:
            size *= s
        assert off + size <= LIMIT, (name, off, size)
        return nc.alloc_sbuf_tensor_at(f"{name}_{seq[0]}", list(shape), dt, offset=off)

    def keep(shape, dt, name="t"):
        size = 4
        for s in shape[1:]:
            size *= s
        t = place(shape, dt, at[0], name)
        at[0] += (size + 31) // 32 * 32
        return t

    class Region:
        def __init__(self, start, stop=LIMIT):
            self.at, self.stop = start, stop

        def __call__(self, shape, dt=F32, name="r"):
            size = 4
            for s in shape[1:]:
                size *= s
            t = place(shape, dt, self.at, name)
            self.at += (size + 31) // 32 * 32
            assert self.at <= self.stop, (name, self.at, self.stop)
            return t

    V = Engine(sem("dve"))
    A = Engine(sem("act"))
    G = Engine(sem("pool"))
    PE = Engine(sem("pe"))
    SP = Engine(None)
    dma_sems = {}

    def f32(ap):
        return ap.bitcast(F32)

    def load(dst, src, name, engine=None, after=()):
        s = dma_sems[name] = sem(name)
        e = engine or SP
        e.put(lambda q: q.dma_start(dst, src).then_inc(s, 16), after, signal=False)
        return (s, 16)

    def act(o, i, fn, after=(), **kw):
        return A.put(lambda e: e.activation(o, i, fn, **kw), after)

    def tt(o, a, b, op, after=(), eng=None):
        return (eng or V).put(lambda e: e.tensor_tensor(o, a, b, op), after)

    def ts(o, a, s0, s1, op0, op1=None, after=(), eng=None, **kw):
        if op1 is None:
            return (eng or V).put(lambda e: e.tensor_scalar(o, a, s0, None, op0, **kw), after)
        return (eng or V).put(lambda e: e.tensor_scalar(o, a, s0, s1, op0, op1, **kw), after)

    def stt(o, a, s, b, op0, op1, after=()):
        return V.put(lambda e: e.scalar_tensor_tensor(out=o, in0=a, scalar=s, in1=b, op0=op0, op1=op1), after)

    def ttr(o, a, b, scale, init, op0, op1, acc, after=()):
        return V.put(lambda e: e.tensor_tensor_reduce(o, a, b, scale, init, op0, op1, acc), after)

    def mm(o, w, x, start, stop, after=(), signal=False):
        return PE.put(lambda e: e.matmul(o, w, x, start=start, stop=stop, skip_group_check=True), after, signal)

    def tr(o, i, after=(), signal=False):
        k = i.shape[0]
        return PE.put(lambda e: e.transpose(o, i, ident[0:k, 0:k]), after, signal)

    def memset(ap, v, after=(), eng=None):
        return (eng or G).put(lambda e: e.memset(ap, v), after)

    def table(name):
        A.put(lambda e: e.preload_act_table_set(name), signal=False)

    X = keep([P, KC, TM], F32, "x")
    RS, RW = 5, 4
    stage = keep([P, RS, TILE], F32, "stage")
    whi = keep([P, RW, TILE], F32R, "whi")
    wlo = keep([P, RW, TILE], F32R, "wlo")
    cst = keep([P, NCONST], F32, "cst")
    ones = keep([P, P], F32, "ones")
    vec = keep([P, NVEC], F32, "vec")
    adac = keep([P, 192], F32, "adac")
    mod = keep([P, 96], F32, "mod")
    mul = keep([P, 4, 16], F32, "mul")
    small = keep([P, 8], F32, "small")
    stat = keep([P, 64], F32, "stat")
    tc = keep([P, 8], F32, "tc")
    tc_free = {i: [] for i in range(8)}
    R0 = at[0]
    ident = cst[:, COFF["ident"]:COFF["ident"] + 128]
    swap = cst[:, COFF["swap"]:COFF["swap"] + 128]
    causal = cst[:, COFF["causal"]:COFF["causal"] + 256]
    namask = cst[:, COFF["namask"]:COFF["namask"] + 64]
    freq = cst[:, COFF["freq"]:COFF["freq"] + 16]
    eps = small[:, 0:1]
    nlam = small[:, 1:2]
    gdiff = small[:, 2:3]

    def v_(name, i=0, n=1):
        return vec[:, VOFF[name] + i:VOFF[name] + i + n]

    ps = [ctx.enter_context(nc.psum_tensor(f"ps{i}", [P, 512], F32)) for i in range(8)]
    bank_free = {i: [] for i in range(8)}

    class Banks:

        def __init__(self, ids):
            self.ids, self.i = ids, 0

        def take(self):
            for _ in self.ids:
                b = self.ids[self.i % len(self.ids)]
                self.i += 1
                if bank_free[b] is not None:
                    break
            after = bank_free[b]
            assert after is not None, f"bank {b} in use"
            bank_free[b] = None
            return b, ps[b], after

    def give(b, *tokens):
        bank_free[b] = list(tokens)

    HID = R0 + 33024
    TMP = HID + 90112
    NTMP = LIMIT - TMP
    hidh = place([P, FC, T], F32R, HID, "hidh")
    hidl = place([P, FC, T], F32R, HID + 45056, "hidl")
    cb = place([P, 2048], F32, TMP - 8192, "cb")

    plan = tile_plan()
    stage_sem = [sem(f"stage{i}") for i in range(RS)]
    stage_free = [[] for _ in range(RS)]
    w_free = [[] for _ in range(RW)]
    st = {"lag": False, "dma": 0, "done": 0, "w": 0, "used": 0, "ready": []}
    ada_tok = {}
    cb_tok = []

    def tile_of(x, kind):
        if kind[0] != "x" or G_COLS[kind[1]] == 512:
            return x
        return x.rearrange("p (i n) -> p i n", i=2)[:, :, 0:G_COLS[kind[1]]]

    def stream_dma():
        while st["dma"] < len(plan) and st["dma"] - min([st["done"]] + [x[0] for x in lows]) < RS:
            t = st["dma"]
            s = t % RS
            dst, src = (tile_of(x, plan[t]) for x in (stage[:, s, :], wst[t]))
            SP.put(lambda q, dst=dst, src=src, s=s: q.dma_start(dst, src).then_inc(stage_sem[s], 16), stage_free[s], signal=False)
            st["dma"] += 1

    def low_part():
        if lows:
            t, s, k, landed, hi = lows.pop()
            w, x, h = (tile_of(v, plan[t]) for v in (wlo[:, k, :], stage[:, s, :], whi[:, k, :]))
            lo = tt(w, x, f32(h), ALU.subtract, [landed, hi, w_free[k]])
            stage_free[s] = [lo]
            low_tok[t] = lo

    lows, low_tok = [], {}

    def pump(limit=len(plan)):
        low_part()
        stream_dma()
        while st["done"] < limit:
            t = st["done"]
            s = t % RS
            landed = (stage_sem[s], 16 * (t // RS + 1))
            kind = plan[t]
            if kind[0] == "a":
                j = kind[1]
                h = j % 2
                tok = ttr(stage[:, s, :], stage[:, s, :], cb[:, 1024 * h:1024 * (h + 1)], 1.0, 0.0,
                          ALU.mult, ALU.add, adac[:, j:j + 1], [landed, cb_tok])
                ada_tok[j] = tok
                stage_free[s] = [tok]
            else:
                if st["w"] - st["used"] >= RW:
                    break
                k = st["w"] % RW
                hi = act(tile_of(whi[:, k, :], kind), tile_of(stage[:, s, :], kind), ACT.Copy, [landed, w_free[k]])
                low_part()
                lows.append((t, s, k, landed, hi))
                if not st["lag"]:
                    low_part()
                st["ready"].append((kind, k, hi, t))
                st["w"] += 1
            st["done"] += 1
            stream_dma()

    def next_tile():
        pump()
        kind, k, hi, t = st["ready"].pop(0)
        if t not in low_tok:
            low_part()
        return kind, k, hi, low_tok[t]

    def tile_used(k, token):
        w_free[k] = [token]
        st["used"] += 1
        pump()

    pending = []

    def later(n, fn):
        pending.append([n, fn])

    ticks = [0]

    def tick():
        ticks[0] += 1
        due = []
        for p in pending:
            p[0] -= 1
            if p[0] <= 0:
                due.append(p)
        for p in due:
            pending.remove(p)
            p[1]()

    def drain():
        while pending:
            tick()

    def gemm(count, banks, moving, width, done):
        acc = {}
        for _ in range(count):
            (what, blks), k, hi_tok, lo_tok = next_tile()
            assert what == "b"
            last = None
            ticked = False
            for i, (mat, kc, fb) in enumerate(blks):
                key = (mat, fb)
                first = key not in acc
                if first:
                    b, bank, free = banks.take()
                    acc[key] = [b, bank, 0, gemm_n(mat)]
                else:
                    free = []
                b, bank, n, total = acc[key]
                xh, xl, tok = moving(mat, kc)
                w = width(mat, fb)
                wh = whi[:, k, P * i:P * (i + 1)]
                wl = wlo[:, k, P * i:P * (i + 1)]
                acc[key][2] = n + 1
                end = n + 1 == total
                o = bank[:, 0:w]
                mm(o, wh, xh[:, 0:w], first, False, [hi_tok, tok, free])
                mm(o, wh, xl[:, 0:w], False, False)
                sig = end or i == len(blks) - 1
                last = mm(o, wl, xh[:, 0:w], False, end, [lo_tok], signal=sig) or last
                if end:
                    del acc[key]
                    if not ticked:
                        tick()
                        ticked = True
                    done(mat, fb, b, bank, last)
            if not ticked:
                tick()
            tile_used(k, last)
            yield
        assert not acc

    halves = {}

    def gemm_n(mat):
        return halves.get(mat, KCHUNKS[mat])

    def run(main, sides=(), rate=1.0):
        live = list(sides)
        credit = 0.0
        for _ in main:
            credit += rate
            while credit >= 1.0:
                credit -= 1.0
                for s in list(live):
                    if next(s, "end") == "end":
                        live.remove(s)
        return live

    def finish(sides):
        live = list(sides)
        n = 0
        while live:
            for s in list(live):
                if next(s, "end") == "end":
                    live.remove(s)
            tick()
            n += 1
            assert n < 1000, "stuck"

    def rms(o, src, n, after, bias=None):
        a = act(o, src, ACT.Ln, after, scale=1.0 / n, bias=eps)
        b = act(o, o, ACT.Exp, [a], scale=-0.5)
        return a, b

    P1 = Region(TMP)
    P1b = Region(TMP - 16384, TMP - 8192)
    ering = Ring([P1([P, 2, 384], F32, "e") for _ in range(2)])
    ptring = Ring([P1([P, 384], F32, "pt") for _ in range(2)])
    R1 = P1([P, T], F32, "R1")
    rl = [P1b([P, 512], F32, "rl") for _ in range(2)]
    sc = P1b([P, 384], F32, "sc")
    wk = P1b([P, 384], F32, "wk")
    rr1 = P1b([P, T], F32, "rr")
    start_at = TMP - 16384 + 4096
    P1c = Region(TMP - 16384, TMP - 12288)
    oring = Ring([P1c([P, T], F32, "o") for _ in range(2)])
    sqring = Ring([P1c([P, T], F32, "sq") for _ in range(2)])
    rring = Ring([R1, rr1])
    rt = [P1([P, 128], F32, "rt") for _ in range(4)]
    cosT = P1([P, 2, 16], F32, "cosT")
    sinT = P1([P, 2, 16], F32, "sinT")
    iw = P1([P, 2, 16], F32, "iw")

    slot = [HID + 4096 * i for i in range(11)]
    extra = [HID + 45056 + 4096 * i for i in range(3)]
    part = [place([P, 2, 512], F32, slot[g], f"part{g}") for g in range(11)]
    xr = place([P, KC, T], F32, HID + 57344, "xr")
    mxh = place([P, 8, T], F32R, HID + 57344, "mxh")
    mxl = place([P, 8, T], F32R, HID + 57344 + 8192, "mxl")
    assert HID + 57344 + 16384 <= TMP - 16384
    hh = place([P, KC, T], F32R, R0, "hh")
    hl = place([P, KC, T], F32R, R0 + 16384, "hl")
    mdh = place([P, 8, T], F32R, R0, "mdh")
    mdl = place([P, 8, T], F32R, R0 + 16384, "mdl")
    iring = Ring([place([P, 768], F32, HID + 57344 + 3072 * i, "ir") for i in range(2)])

    cb_load = load(cb[0:1, :], cvec, "ld_c")
    vec_load = load(vec[:, :], vecs, "ld_vec")
    posi = place([P, 2], I32, start_at, "posi")
    posf = place([P, 2], F32, start_at + 32, "posf")
    ang = [place([P, 2, 16], F32, start_at + 64 + 128 * i, "ang") for i in range(5)]
    lam_in = place([P, 256], F32, start_at + 1024, "lam")
    lamt = place([P, 8], F32, start_at + 2048, "lamt")
    pos_load = load(posi[:, :], positions, "ld_pos", A)
    freq_load = load(freq, consts[:, COFF["freq"]:], "ld_freq", A)
    x_load = [load(X[:, 4 * i:4 * i + 4, 0:T], xT[:, 4 * i:4 * i + 4, :], f"ld_x{i}", A) for i in range(4)]
    stream_dma()

    ones_tok = memset(ones[:, :], 1.0)
    eps_tok = memset(eps, 1e-6)
    stat_tok = memset(stat[:, :], 0.0)
    for j in range(4):
        c = slice(512 * j, 512 * j + 512)
        p = mm(ps[4 + j][:, 0:512], ones[0:1, :], cb[0:1, c], True, True, [cb_load, ones_tok], signal=True)
        cb_tok.append(act(cb[:, c], ps[4 + j][:, 0:512], ACT.Silu, [p]))
        bank_free[4 + j] = [cb_tok[-1]]

    xsq = [rl[i][:, 256 * j:256 * j + 256] for i in range(2) for j in range(2)]
    sq_free = [[] for _ in range(4)]
    b, bank, free = 0, ps[0], []
    for kc in range(KC):
        s = act(xsq[kc % 4], X[:, kc, 0:T], ACT.Square, [x_load[kc // 4], sq_free[kc % 4]])
        t = mm(bank[:, 0:T], ones[:, :], xsq[kc % 4], kc == 0, kc == KC - 1, [s, ones_tok], signal=True)
        sq_free[kc % 4] = [t]
    sum_tok = t

    two_pi = 2.0 * np.pi
    C1 = 6.28125
    C2 = float(np.float32(np.floor((two_pi - C1) * 2.0 ** 22) / 2.0 ** 22))
    C3 = float(np.float32(two_pi - C1 - C2))
    H1 = float(np.float32(np.pi / 2))
    H2 = float(np.float32(np.pi / 2 - H1))
    MAGIC = 12582912.0
    PI = 3.1415925
    p0 = G.put(lambda e: e.tensor_copy(posf[:, :], posi[:, :]), [pos_load])
    a0, kk, r2, *rrs = [a[:, :, :] for a in ang]
    pa = None
    for tb in range(2):
        pa = ts(ang[0][:, tb, :], freq, posf[:, tb:tb + 1], None, ALU.mult, None, [p0, freq_load], G)
    t, trig = pa, []
    for dst, quarter, rr in ((sinT, 0.0, rrs[0]), (cosT, 0.25, rrs[1])):
        t = ts(kk, a0, float(1.0 / two_pi), quarter, ALU.mult, ALU.add, [t], G)
        t = ts(kk, kk, MAGIC, -MAGIC, ALU.add, ALU.add, [t], G)
        src = a0
        for c in (C1, C2, C3):
            t = ts(r2, kk, -c, None, ALU.mult, None, [t], G)
            t = tt(rr, src, r2, ALU.add, [t], G)
            src = rr
        if quarter:
            t = ts(rr, rr, H1, H2, ALU.add, ALU.add, [t], G)
        t = ts(rr, rr, PI, -PI, ALU.min, ALU.max, [t], G)
        trig.append(act(dst[:, :, :], rr, ACT.Sin, [t]))
    trig_tok = trig
    table("natural_log_exp_and_others")

    ra, rb = rms(R1[:, :], bank[:, 0:T], 2048, [sum_tok, eps_tok])
    bank_free[0] = [ra]
    pump(2 * 2 * PASSES[0][1])
    xr_tok = []

    def make_xr(k0, k1, eng):
        for kc in range(k0, k1):
            xr_tok.append(tt(xr[:, kc, :], X[:, kc, 0:T], R1[:, :], ALU.mult, [rb, x_load[kc // 4]], eng))

    make_xr(*PASSES[0], V)

    lam_tok = gdiff_tok = cst_load = None

    def lambda_():
        nonlocal lam_tok, gdiff_tok
        lam_load = load(lam_in[:, :], bass.AP(lambdas.tensor, 0, [[0, P], [1, 256]]), "ld_lam", A)
        yield
        la = []
        for i in range(2):
            t = ttr(lam_in[:, 128 * i:128 * i + 64], lam_in[:, 128 * i:128 * i + 64], lam_in[:, 128 * i + 64:128 * i + 128],
                    1.0, 0.0, ALU.mult, ALU.add, lamt[:, i:i + 1], [lam_load])
            la.append(t)
        le = act(lamt[:, 2:4], lamt[:, 0:2], ACT.Exp, la)
        l1 = tt(lamt[:, 4:5], lamt[:, 3:4], lamt[:, 2:3], ALU.subtract, [le], G)
        lam_tok = ts(nlam, lamt[:, 4:5], -0.2, None, ALU.add, None, [l1], G)
        gdiff_tok = ts(gdiff, v_("g_diff_sub"), 0.8, None, ALU.mult, None, [vec_load], G)

    def mod_chunks(c0, n):
        t = tt(mod[:, c0:c0 + n], adac[:, 2 * c0:2 * (c0 + n):2], adac[:, 2 * c0 + 1:2 * (c0 + n):2], ALU.add,
               [ada_tok[j] for j in range(2 * c0, 2 * (c0 + n))], G)
        return tt(mod[:, c0:c0 + n], mod[:, c0:c0 + n], v_("b_ada", c0, n), ALU.add, [t, vec_load], G)

    def gain(dst, c0, n, g, one):
        t = mod_chunks(c0, n)
        if one:
            t = ts(mod[:, c0:c0 + n], mod[:, c0:c0 + n], 1.0, None, ALU.add, None, [t], G)
        return tt(dst, mod[:, c0:c0 + n], g, ALU.mult, [t, vec_load], G)

    h_tok = {}

    def make_h(k0, k1):
        n = k1 - k0
        tsh = mod_chunks(SHIFT_A + k0, n)
        tsc = gain(mul[:, 0, k0:k1], SCALE_A + k0, n, v_("g_attn_pre", k0, n), True)
        a, h = {}, {}
        for kc in range(k0, k1):
            a[kc] = ts(xr[:, kc, :], xr[:, kc, :], mul[:, 0, kc:kc + 1], mod[:, SHIFT_A + kc:SHIFT_A + kc + 1],
                       ALU.mult, ALU.add, [xr_tok[kc], tsh, tsc])
            h[kc] = act(hh[:, kc, :], xr[:, kc, :], ACT.Copy, [a[kc]])
        for kc in range(k0, k1):
            l = tt(hl[:, kc, :], xr[:, kc, :], f32(hh[:, kc, :]), ALU.subtract, [a[kc], h[kc]])
            h_tok[kc] = [h[kc], l]

    fin = {}
    age = {}
    turn_after = {}
    FREED = []
    ROTATED = {g: [(0, 8, 64, 8)] for g in (IQ0, IQ1, DK0, DQ0, DK1, DQ1)}
    ROTATED.update({g: [(0, 4, 128, 16)] for g in (SQ0, SQ1)})
    ROTATED[IKS] = [(272, 1, 64, 8), (0, 1, 128, 16)]
    part_tok = {}
    tmp2 = Ring(rl, {0: sq_free, 1: sq_free})
    tmp3 = Ring([place([P, 512], F32, at, "tmp3") for at in (R0 + 10240, R0 + 26624)])
    gb = Banks([0, 1, 2])
    gb8 = Banks(range(8))
    gbm = Banks([3, 0, 1, 2])

    def project():
        nonlocal cst_load
        make_h(*PASSES[0])
        make_xr(PASSES[0][1], KC, G)
        pump()
        lam = lambda_()
        for pi, (k0, k1) in enumerate(PASSES):
            next(lam, None)
            lastp = pi == len(PASSES) - 1
            if lastp:
                cst_load = load(cst[:, 0:COFF["freq"]], consts[:, 0:COFF["freq"]], "ld_cst", A)
                st["lag"] = True
                FREED.extend([(PE.sem, PE.n), list(tmp2.free.values())])
                for ring in (oring, sqring):
                    for k in ring.free:
                        ring.free[k] = list(FREED)
                for k in iring.free:
                    iring.free[k] = xr_done()
                tmp3.free.update({0: FREED, 1: FREED})
            bks = {}
            for ti, (g, kp) in enumerate(pass_tiles(pi)):
                for ks, _, _, at in AHEAD[pi]:
                    if ti == at:
                        make_h(*ks)
                n = G_COLS[g]
                if kp == k0 // 2:
                    bks[g] = [(gb if lastp else gb8).take() for _ in range(2)]
                bk = bks[g]
                last = None
                (what, g_, kp_), k, hi_tok, lo_tok = next_tile()
                assert (what, g_, kp_) == ("x", g, kp)
                for i in range(2):
                    kc = 2 * kp + i
                    wh = whi[:, k, 512 * i:512 * i + n]
                    wl = wlo[:, k, 512 * i:512 * i + n]
                    for tb in range(2):
                        o = bk[tb][1][:, 0:n]
                        c = slice(P * tb, P * tb + P)
                        st_ = kc == k0
                        en = kc == k1 - 1
                        mm(o, hh[:, kc, c], wh, st_, False, [h_tok[kc], hi_tok, bk[tb][2]])
                        mm(o, hh[:, kc, c], wl, False, False, [lo_tok])
                        last = mm(o, hl[:, kc, c], wh, False, en, signal=(i == 1)) or last
                        if en and tb == 0:
                            tok0 = last
                if kp < k1 // 2 - 1:
                    tile_used(k, last)
                    tick()
                    yield
                    continue
                toks = [tok0, last]
                res = []
                for tb in range(2):
                    b, bank, _ = bk[tb]
                    dst = part[g][:, tb, 0:n]
                    if pi == 0:
                        t = act(dst, bank[:, 0:n], ACT.Copy, [toks[tb]])
                        give(b, t)
                    elif 2 * g + tb not in BY_DVE if not lastp else g in LATE_POOL:
                        tmp = tmp3 if lastp else tmp2
                        r, buf, fr = tmp.take()
                        t = act(buf[:, 0:n], bank[:, 0:n], ACT.Copy, [toks[tb], fr])
                        give(b, t)
                        t = tt(dst, dst, buf[:, 0:n], ALU.add, [t, part_tok[g, tb]], G)
                        tmp.give(r, t)
                    else:
                        t = tt(dst, bank[:, 0:n], dst, ALU.add, [toks[tb], part_tok[g, tb]])
                        give(b, t)
                    part_tok[g, tb] = t
                    res.append(t)
                if lastp:
                    fin[g] = res
                    if g in ROTATED:
                        age[g] = ticks[0]
                        turn_after[g] = [rotate(g, *r, fin[g]) for r in ROTATED[g]]
                    if g == IKS:
                        turn_after[g].append(G.put(lambda e, p=part[g]: e.tensor_copy(p[:, :, 336:400], p[:, :, 272:336]),
                                                   turn_after[g][0]))
                tile_used(k, last)
                tick()
                yield

    ab = Banks([3, 4, 5, 6, 7])
    rot_free = [[]]

    def rotate(g, c0, heads, dim, half, after):
        v = part[g][:, :, c0:c0 + heads * dim].rearrange("p t (h d) -> p t h d", h=heads)
        step = 16 // half
        cosb = cosT[:, :, 0:16:step].unsqueeze(2).to_broadcast([P, 2, heads, half])
        sinb = sinT[:, :, 0:16:step].unsqueeze(2).to_broadcast([P, 2, heads, half])
        x1 = v[:, :, :, 0:half]
        x2 = v[:, :, :, half:2 * half]
        n = heads * half
        r = [q[:, 0:2 * n].rearrange("p (t h d) -> p t h d", t=2, h=heads) for q in rt]
        a = [after, rot_free[0], trig_tok]
        t1 = tt(r[0], x1, cosb, ALU.mult, a, G)
        t2 = tt(r[1], x2, sinb, ALU.mult, a, G)
        t3 = tt(r[2], x2, cosb, ALU.mult, a, G)
        t4 = tt(r[3], x1, sinb, ALU.mult, a, G)
        t5 = tt(x1, r[0], r[1], ALU.subtract, [t1, t2, t3, t4], G)
        t6 = tt(x2, r[2], r[3], ALU.add, [t3, t4], G)
        rot_free[0] = [t5, t6]
        return [t5, t6]

    def turn(g, cols, evac, after):
        b, bank, free = ab.take()
        for i, c in enumerate(cols):
            for tb in range(2):
                t = tr(bank[:, 256 * i + P * tb:256 * i + P * tb + P], part[g][:, tb, c:c + P], [after, free, cst_load],
                       signal=(i == len(cols) - 1 and tb == 1))
        give(b, *evac(bank, t))
        return t

    iqT = [place([P, 4, T], F32, extra[0], "iqT0"), place([P, 4, T], F32, slot[0], "iqT1")]
    ikz = place([P, 2, T], F32, slot[1], "ikz")
    skT = place([P, T], F32, slot[1] + 2048, "skT")
    M1 = place([P, 384], F32, extra[0], "M1")
    sqT = [place([P, 4, T], F32, slot[8], "sqT0"), place([P, 4, T], F32, slot[9], "sqT1")]
    kz = [place([P, 2, 2, T], F32, o, f"kz{i}")[:, :, :, :] for i, o in enumerate((extra[1], extra[2], slot[5]))]
    kz.append(place([P, 2, 4096], F32, R0 + 8192, "kz3")[:, :, 0:512].rearrange("p b (c t) -> p b c t", c=2))
    dqT = [place([P, 4, T], F32, slot[3], "dqT0"), place([P, 4, T], F32, slot[6], "dqT1")]
    m1p = [place([P, 8, T], F32, R0 + 8192, "m1a"), place([P, 8, T], F32, R0 + 24832, "m1b")]

    def m1(kc):
        return m1p[kc // 8][:, kc % 8, :]

    T_ = {}
    turned = {}

    def prep():
        def ready(g):
            while g not in fin or ticks[0] < age[g] + 2:
                yield

        def plain(g, dst, key, free):
            yield from ready(g)
            toks = []
            for j in range(2):
                def ev(bank, t, j=j):
                    e = act(dst[:, 2 * j:2 * j + 2, :], bank[:, :].rearrange("p (b t) -> p b t", b=2), ACT.Copy, [t, free])
                    T_.setdefault(key, []).append(e)
                    return [e]
                toks.append(turn(g, [256 * j, 256 * j + 128], ev, [fin[g], turn_after[g]]))
                yield
            turned[g] = toks[-1]

        def keys(g, hp, free):
            zero = [memset(kz[hp + j], 0.0, free[j]) for j in range(2)]
            yield from ready(g)
            for j in range(2):
                z = kz[hp + j]

                def ev(bank, t, z=z, j=j):
                    v = bank[:, :].rearrange("p (b t) -> p b t", b=2)
                    e0 = act(z[0:64, :, 0, :], v[0:64], ACT.Copy, [t, zero[j]])
                    e1 = act(z[64:128, :, 1, :], v[64:128], ACT.Copy, [t, zero[j]])
                    for i in range(2):
                        T_[("kz", 2 * (hp + j) + i)] = [e0, e1]
                    return [e0, e1]
                tok = turn(g, [256 * j, 256 * j + 128], ev, [fin[g], turn_after[g]])
                yield
            turned[g] = tok

        yield from plain(IQ0, iqT[0], "iq0", [])
        yield from plain(IQ1, iqT[1], "iq1", [turned[IQ0]])
        zero = memset(ikz[:, :, :], 0.0, [turned[IQ1]])
        yield from ready(IKS)

        def ev(bank, t):
            v = bank[:, :].rearrange("p (b t) -> p b t", b=2)
            e0 = act(ikz[0:64, 0, :], v[0:64, 0, :], ACT.Copy, [t, zero])
            e1 = act(ikz[64:128, 1, :], v[64:128, 0, :], ACT.Copy, [t, zero])
            e2 = act(skT[:, :], v[:, 1, :], ACT.Copy, [t, turned[IQ1]])
            T_["ik"] = [e0, e1]
            T_["sk"] = [e2]
            return [e0, e1, e2]
        turned[IKS] = turn(IKS, [272, 0], ev, [fin[IKS], turn_after[IKS]])
        w = ts(iw[:, :, :], part[IKS][:, :, 256:272], 1.0 / 32, None, ALU.mult, None, fin[IKS], G)
        T_["iw"] = [w]
        yield
        yield from keys(DK0, 0, [[], []])
        yield from plain(DQ0, dqT[0], "dq0", [turned[DK0]])
        yield from keys(DK1, 2, [[turned[DQ0]], FREED])
        yield from plain(DQ1, dqT[1], "dq1", [turned[DK1]])
        yield from plain(SQ0, sqT[0], "sq0", [turned[DQ1]])
        yield from plain(SQ1, sqT[1], "sq1", [turned[SQ0]])

    def turned_tok(g):
        return turned[g]

    def lock(pipe, n):
        for t in range(n + len(pipe) - 1):
            for s in range(len(pipe) - 1, -1, -1):
                i = t - s
                if 0 <= i < n:
                    r = pipe[s](i)
                    if r is not None:
                        yield from r
            yield

    def indexer():
        while not ("ik" in T_ and len(T_.get("iq1", [])) == 2):
            yield
        last = {}
        for p in range(8):
            q = iqT[p // 4][:, p % 4, :]
            qt = [T_["iq0"] if p < 4 else T_["iq1"], T_["ik"]]
            work = []
            r, flatbuf, fr = iring.take()
            for qb in (1, 0):
                n = 256 if qb else 128
                b, bank, free = ab.take()
                t = mm(bank[:, 0:2 * n].rearrange("p (h k) -> p h k", h=2), q[:, P * qb:P * qb + P], ikz[:, :, 0:n], True, True,
                       [free, qt], signal=True)
                buf = flatbuf[:, 0:512] if qb else flatbuf[:, 512:768]
                e = act(buf, bank[:, 0:2 * n], ACT.Relu, [t, fr])
                give(b, e)
                work.append((qb, n, buf, e))
            T_["idx_pe"] = t
            used = {0: [], 1: []}
            for h in range(2):
                for qb, n, buf, e in work:
                    dst = sc[:, 128 * qb:128 * qb + n]
                    w = iw[:, qb, 2 * p + h:2 * p + h + 1]
                    src = buf[:, n * h:n * h + n]
                    if p == 0 and h == 0:
                        t = ts(dst, src, w, None, ALU.mult, None, [e, T_["iw"]])
                    else:
                        t = stt(dst, src, w, dst, ALU.mult, ALU.add, [e, last[qb]])
                    last[qb] = t
                    used[qb].append(t)
            iring.give(r, used[0], used[1])
            yield
        seg = {0: slice(0, 128), 1: slice(128, 384)}
        mask = {0: causal[:, 128:256], 1: causal[:, :]}
        t = {}
        for qb in (1, 0):
            t[qb] = tt(sc[:, seg[qb]], sc[:, seg[qb]], mask[qb], ALU.add, [last[qb], cst_load])
        src = {qb: sc[:, seg[qb]] for qb in (0, 1)}
        m8 = {qb: stat[:, 8 * qb:8 * qb + 8] for qb in (0, 1)}
        for r in range(8):
            for qb in (1, 0):
                t[qb] = V.put(lambda e, qb=qb, s=src[qb]: e.max(m8[qb], s), [t[qb], stat_tok])
            for qb in (1, 0):
                t[qb] = V.put(lambda e, qb=qb, s=src[qb]: e.match_replace(wk[:, seg[qb]], m8[qb], s, USED), [t[qb]])
                src[qb] = wk[:, seg[qb]]
            yield
        toks = []
        for qb in (1, 0):
            t[qb] = tt(wk[:, seg[qb]], wk[:, seg[qb]], sc[:, seg[qb]], ALU.is_equal, [t[qb]])
        for qb in (1, 0):
            toks.append(stt(M1[:, seg[qb]], wk[:, seg[qb]], NEG, mask[qb], ALU.mult, ALU.add, [t[qb], T_["idx_pe"]]))
        T_["M"] = toks
        yield

    seg = {0: slice(0, 128), 1: slice(128, 384)}

    def schedule(heads, stages, may):
        n = len(heads)
        at = [0] * n
        last = [-1] * n
        while any(at[i] < len(stages[heads[i][0]]) for i in range(n)):
            for i, (kind, h) in enumerate(heads):
                if at[i] < len(stages[kind]) and ticks[0] > last[i] and may(kind, h, at[i]):
                    stages[kind][at[i]](h)
                    at[i] += 1
                    last[i] = ticks[0]
                    break
                if at[i] == 0:
                    break
            yield

    def transposed_p(E, after, key):
        b, bank, free = ab.take()
        for i in range(3):
            t = tr(bank[:, P * i:P * i + P], E[:, (0, 128, 256)[i]:(0, 128, 256)[i] + P], [after, free], signal=(i == 2))
        r, buf, fr = ptring.take()
        e = act(buf[:, :], bank[:, 0:384], ACT.Copy, [t, fr])
        give(b, e)
        return t, r, buf, e

    def weighted_v(v0, v1, buf, after):
        b, bank, free = ab.take()
        mm(bank[:, 0:256], v0, buf[:, 0:256], True, False, [after, free])
        t = mm(bank[:, 128:256], v1, buf[:, 256:384], False, True, signal=True)
        return b, bank, t

    dsa = {}
    mix_tok = {}
    SD = float(128 ** -0.5)

    def dsa_stages():
        def s0(h):
            b, bank, free = ab.take()
            q = sqT[h // 4][:, h % 4, :]
            qt = [T_["sq0"] if h < 4 else T_["sq1"], T_["sk"]]
            t0 = mm(bank[:, 0:128], q[:, 0:128], skT[:, 0:128], True, True, [free, qt], signal=True)
            t1 = mm(bank[:, 128:384], q[:, 128:256], skT[:, :], False, True, signal=True)
            T_["dsa_pe"] = t1
            r, E, fr = ering.take()
            c = 16 + 4 * (h % 4)
            vs, es = [], []
            for qb, t in ((0, t1), (1, t1)):
                vs.append(ttr(E[:, 0, seg[qb]], bank[:, seg[qb]], M1[:, seg[qb]], -SD, BIG, ALU.add, ALU.min,
                              stat[:, c + qb:c + qb + 1], [t, fr, T_["M"]]))
            give(b, vs)
            for qb in range(2):
                es.append(act(E[:, 0, seg[qb]], E[:, 0, seg[qb]], ACT.Exp, [vs[qb]], scale=-1.0,
                              bias=stat[:, c + qb:c + qb + 1], accum_out=stat[:, c + 2 + qb:c + 3 + qb]))
            dsa[h] = dict(r=r, E=E, es=es, c=c)

        def s1(h):
            d = dsa[h]
            E, c = d["E"], d["c"]
            t = V.put(lambda e: e.reciprocal(stat[:, c:c + 2], stat[:, c + 2:c + 4]), [d["es"]])
            ns = []
            for qb in range(2):
                ns.append(ts(E[:, 0, seg[qb]], E[:, 0, seg[qb]], stat[:, c + qb:c + qb + 1], None, ALU.mult, None, [t]))
            d["ns"] = ns

        def turn_p(h):
            d = dsa[h]
            t, r, buf, e = transposed_p(d["E"][:, 0, :], d["ns"], h)
            ering.give(d["r"], t)
            d.update(pr=r, buf=buf, e=e)

        def s2(h):
            d = dsa[h]
            b, bank, t = weighted_v(part[IKS][:, 0, 128:256], part[IKS][:, 1, 128:256], d["buf"], [d["e"], fin[IKS]])
            ptring.give(d["pr"], t)
            T_["dsa_pv"] = t
            a = act(mxh[:, h, :], bank[:, 0:256], ACT.Copy, [t, xr_done(), T_["M"]])
            l = tt(mxl[:, h, :], bank[:, 0:256], f32(mxh[:, h, :]), ALU.subtract, [a])
            give(b, l)
            mix_tok[8 + h] = [a, l]

        return [s0, s1, turn_p, s2]

    def xr_done():
        return [h_tok[k] for k in range(KC)]

    diff = {}

    def diff_stages():
        def s0(h):
            q = dqT[h // 4][:, h % 4, :]
            z = kz[h // 2][:, h % 2, :, :]
            qt = [T_["dq0"] if h < 4 else T_["dq1"], T_[("kz", h)]]
            bk = []
            for qb in range(2):
                n = 256 if qb else 128
                b, bank, free = ab.take()
                t = mm(bank[:, 0:2 * n].rearrange("p (c k) -> p c k", c=2), q[:, P * qb:P * qb + P], z[:, :, 0:n], True, True,
                       [free, qt], signal=True)
                bk.append((b, bank, t, n))
            r, E, fr = ering.take()
            c = 32 + 8 * (h % 4)
            vs = {}
            for qb, (b, bank, t, n) in enumerate(bk):
                for i in range(2):
                    vs[qb, i] = ttr(E[:, i, seg[qb]], bank[:, n * i:n * i + n], causal[:, 256 - n:256], -0.125, BIG,
                                    ALU.add, ALU.min, stat[:, c + 2 * qb + i:c + 2 * qb + i + 1], [t, fr, cst_load])
                give(b, vs[qb, 0], vs[qb, 1])
            es = []
            for qb in range(2):
                for i in range(2):
                    k = 2 * qb + i
                    es.append(act(E[:, i, seg[qb]], E[:, i, seg[qb]], ACT.Exp, [vs[qb, i]], scale=-1.0,
                                  bias=stat[:, c + k:c + k + 1], accum_out=stat[:, c + 4 + k:c + 5 + k]))
            diff[h] = dict(r=r, E=E, es=es, c=c)

        def s1(h):
            d = diff[h]
            E, c = d["E"], d["c"]
            t = V.put(lambda e: e.reciprocal(stat[:, c:c + 4], stat[:, c + 4:c + 8]), [d["es"]])
            u = ts(stat[:, c + 1:c + 4:2], stat[:, c + 1:c + 4:2], nlam, None, ALU.mult, None, [t, lam_tok])
            ns = []
            for qb in range(2):
                ns.append(ts(E[:, 0, seg[qb]], E[:, 0, seg[qb]], stat[:, c + 2 * qb:c + 2 * qb + 1], None, ALU.mult, None, [t]))
            for qb in range(2):
                ns[qb] = stt(E[:, 0, seg[qb]], E[:, 1, seg[qb]], stat[:, c + 2 * qb + 1:c + 2 * qb + 2], E[:, 0, seg[qb]],
                             ALU.mult, ALU.add, [u, ns[qb]])
            d["ns"] = ns

        def turn_p(h):
            d = diff[h]
            t, r, buf, e = transposed_p(d["E"][:, 0, :], d["ns"], h)
            ering.give(d["r"], t)
            d.update(pr=r, buf=buf, e=e)

        def s2(h):
            d = diff[h]
            g = DV0 if h < 4 else DV1
            c0 = 128 * (h % 4)
            b, bank, t = weighted_v(part[g][:, 0, c0:c0 + 128], part[g][:, 1, c0:c0 + 128], d["buf"], [d["e"], fin[g]])
            ptring.give(d["pr"], t)
            T_["diff_pv"] = t
            r1_, o, fr1 = oring.take()
            r2_, s, fr2 = sqring.take()
            a = act(s[:, :], bank[:, 0:256], ACT.Square, [t, fr2])
            a2 = act(o[:, :], bank[:, 0:256], ACT.Copy, [t, fr1])
            give(b, a, a2)
            d.update(o=o, s=s, ro=r1_, rs=r2_, a=a, a2=a2)

        def s3(h):
            d = diff[h]
            b, bank, free = ab.take()
            t = mm(bank[:, 0:256], ones[:, :], d["s"][:, :], True, True, [free, d["a"]], signal=True)
            sqring.give(d["rs"], t)
            rk, R, fr = rring.take()
            a, e = rms(R[:, :], bank[:, 0:256], 128, [t, fr])
            give(b, a)
            f = d["o"]
            t = stt(f[:, :], f[:, :], gdiff, R[:, :], ALU.mult, ALU.mult, [e, d["a2"], gdiff_tok])
            rring.give(rk, t)
            a = act(mdh[:, h, :], f[:, :], ACT.Copy, [t, FREED])
            l = tt(mdl[:, h, :], f[:, :], f32(mdh[:, h, :]), ALU.subtract, [t, a, FREED])
            oring.give(d["ro"], l)
            mix_tok[h] = [a, l]

        return [s0, s1, turn_p, s2, s3]

    def may(kind, h, s):
        if s == 0:
            if kind == "diff":
                ready = len(T_.get("dq0" if h < 4 else "dq1", [])) == 2 and ("kz", 3 if h < 4 else 7) in T_
            else:
                ready = "M" in T_ and len(T_.get("sq0" if h < 4 else "sq1", [])) == 2
            return ready and ering.free[ering.i] is not None
        if s == 2:
            return ptring.free[ptring.i] is not None
        if s == 3 and kind == "diff":
            return oring.free[oring.i] is not None and sqring.free[sqring.i] is not None
        return True

    sides = [prep(), indexer(), schedule([(kind, h) for kind in ("diff", "dsa") for h in range(8)],
                                         {"diff": diff_stages(), "dsa": dsa_stages()}, may)]
    fast = [sides[2]]

    def step_sides(gens):
        for s in list(gens):
            if s in sides and next(s, "end") == "end":
                sides.remove(s)

    def run_sides(main, rate, rate_fast):
        c, f = 0.0, 0.0
        for _ in main:
            c += rate
            f += rate_fast
            while c >= 1.0 or f >= 1.0:
                if c >= 1.0:
                    step_sides([s for s in sides if s not in fast])
                    c -= 1.0
                if f >= 1.0:
                    step_sides(fast)
                    f -= 1.0

    def force(cond):
        n = 0
        while not cond():
            tick()
            step_sides(sides)
            for _ in range(4):
                step_sides(fast)
            n += 1
            assert n < 500

    run_sides(project(), *RATE1)
    R2 = place([P, TM], F32, LIMIT - 1088, "R2")
    halves["o"] = 8
    m_tok = {}
    phase = {"half": 0}

    def o_moving(mat, kc):
        force(lambda: kc in mix_tok)
        return (mxh[:, kc - 8, :], mxl[:, kc - 8, :], mix_tok[kc]) if kc >= 8 else (mdh[:, kc, :], mdl[:, kc, :], mix_tok[kc])

    o_free = [T_["diff_pv"], list(tmp3.free.values())]

    def o_first(mat, fb, b, bank, tok):
        t = act(m1(fb), bank[:, 0:T], ACT.Copy, [tok, o_free])
        give(b, t)
        m_tok[fb] = t

    run_sides(gemm(16, gb, o_moving, lambda m, f: T, o_first), *RATE1B)

    F = Region(TMP, LIMIT - 1088)
    sqf = Ring([F([P, TM], F32, "sqf") for _ in range(2)])
    ssum = F([P, TM], F32, "ssum")
    zr = Ring([F([P, TQ], F32, "z") for _ in range(2)])
    ur = Ring([F([P, T], F32, "u") for _ in range(2)])
    hr = Ring([F([P, T], F32, "hf") for _ in range(3)])
    cr = Ring([F([P, T], F32, "c") for _ in range(1)])
    Rm = zr.items[0]
    guard1 = []

    def attention_ended():
        force(lambda: not sides)
        guard1.extend([(V.sem, V.n), (A.sem, A.n), (PE.sem, PE.n), (G.sem, G.n)])
        main_sum.tok = list(guard1)
        for ring in (sqf, zr, ur, hr, cr):
            for k in ring.free:
                ring.free[k] = list(guard1)

    class Sum:

        def __init__(self, buf):
            self.buf, self.tok, self.rest, self.heads = buf, [], [], 0

        def add(self):
            if self.rest:
                k, buf, n, s = self.rest.pop()
                t = tt(self.buf[:, 0:n], self.buf[:, 0:n], buf[:, 0:n], ALU.add, [s, self.tok], G)
                sqf.give(k, t)
                self.tok = [t]

    main_sum = Sum(ssum)

    def square_in(src, n, after, first, late=False, to=main_sum):
        if first:
            t = act(to.buf[:, 0:n], src, ACT.Square, [after, to.tok])
            to.tok = [t]
            return t
        to.add()
        k, buf, fr = sqf.take()
        s = act(buf[:, 0:n], src, ACT.Square, [after, fr])
        to.rest.append((k, buf, n, s))
        if not late:
            to.add()
        return s

    def rms_of_sum(o, n, after, div=2048, of=main_sum):
        b, bank, free = ab.take()
        mm(bank[:, 0:n], ones[:, :], of.buf[:, 0:n], True, not of.rest, [free, of.tok], signal=not of.rest)
        t = (PE.sem, PE.n)
        if of.rest:
            k, buf, n, s = of.rest.pop()
            t = mm(bank[:, 0:n], ones[:, :], buf[:, 0:n], False, True, [s], signal=True)
            sqf.give(k, t)
        of.tok = [of.tok, t]
        a, e = rms(o[:, 0:n], bank[:, 0:n], div, [t, after])
        give(b, a)
        return e

    def o_second(mat, fb, b, bank, tok):
        if not guard1:
            attention_ended()
        t = tt(m1(fb), bank[:, 0:T], m1(fb), ALU.add, [tok, m_tok[fb]])
        give(b, t)
        m_tok[fb] = [t]

        def squares():
            m_tok[fb] = [t, square_in(m1(fb), T, [t], fb == 0, fb == 15)]
        later(1, squares)

    meta_load = load(X[:, :, T:TM], metaT, "ld_meta")
    for _ in gemm(16, gb8, o_moving, lambda m, f: T, o_second):
        pass
    halves.clear()
    drain()

    yh = place([P, KC, TQ], F32R, R0, "yh")
    yl = place([P, KC, TQ], F32R, R0 + 16512, "yl")
    x_tok = {kc: [x_load[kc // 4], meta_load] for kc in range(KC)}
    y_tok = {}

    def add_residual(m, kc, s, R, Rtok, after, eng):
        k, buf, fr = hr.take()
        t = stt(buf[:, 0:T], m(kc), s, R[:, 0:T], ALU.mult, ALU.mult, [Rtok, after, fr])
        t = tt(X[:, kc, 0:T], X[:, kc, 0:T], buf[:, 0:T], ALU.add, [t, x_tok[kc]], eng)
        hr.give(k, t)
        x_tok[kc] = [t]
        return t

    def shift_columns(k0, after):
        tsh = mod_chunks(SHIFT_F + k0, 8)
        th, tl = [], []
        for c in range(T, TQ):
            src = mod[:, SHIFT_F + k0:SHIFT_F + k0 + 8]
            th.append(act(yh[:, k0:k0 + 8, c], src, ACT.Copy, [tsh, after]))
            tl.append(tt(yl[:, k0:k0 + 8, c], src, f32(yh[:, k0:k0 + 8, c]), ALU.subtract, [tsh, th, after]))
        return [th, tl]

    def gains(k0):
        sl = slice(k0, k0 + 8)
        gate_tok.append(gain(mul[:, 1, sl], GATE_A + k0, 8, v_("g_attn_post", k0, 8), False))
        scale_tok.append(gain(mul[:, 2, sl], SCALE_F + k0, 8, v_("g_ffn_pre", k0, 8), True))

    gate_tok, scale_tok = [], []
    low_part()
    gains(0)
    rm_tok = rms_of_sum(Rm, T, [])
    y_guard = [(PE.sem, PE.n)]
    def residual_chunks(m, s_of, R, Rtok, gain_of, after, yh, yl, n, extra):
        lows = []
        for kc in range(KC):
            add_residual(m, kc, s_of(kc), R, [Rtok], m_tok[kc], V if kc == 0 else G)
            if len(lows) > (kc > 1):
                lows.pop(0)()
            g = gain_of(kc)
            a = act(yh[:, kc, 0:n], X[:, kc, 0:n], ACT.Copy, [x_tok[kc], after], scale=g)

            def low(kc=kc, g=g, a=a):
                l = stt(yl[:, kc, 0:n], X[:, kc, 0:n], g, f32(yh[:, kc, 0:n]), ALU.mult, ALU.subtract, [x_tok[kc], after, a])
                y_tok[kc] = [a, l, extra(kc)]
            lows.append(low)
            if kc % 8 == 7:
                while lows:
                    lows.pop(0)()
            yield

    chunks = residual_chunks(m1, lambda kc: mul[:, 1, kc:kc + 1], Rm, [rm_tok, gate_tok], lambda kc: mul[:, 2, kc:kc + 1],
                             [scale_tok, y_guard], yh, yl, T, lambda kc: [shift_tok] if kc < 8 else [])

    next(chunks)
    shift_tok = shift_columns(0, [y_guard, x_tok[0]])
    upto = [7]

    def ahead(kc, n):
        while min(kc + n, upto[0]) not in y_tok:
            next(chunks)

    def all_chunks():
        for _ in chunks:
            pass

    def squares(n):
        for kc in range(KC):
            while kc not in y_tok:
                yield
            square_in(X[:, kc, 0:n], n, [x_tok[kc], meta_load], kc == 0, True)
            yield

    def steps(gen, n):
        for _ in range(n):
            next(gen, None)


    gb6 = Banks([0, 1, 2, 3, 4, 5])
    ab = Banks([6, 7])
    hid_tok = {}
    hid_free = []
    HALF2 = 58
    SQ2 = 1
    RATE, RATE2 = 1.15, 1.2

    partg = place([P, FP, T], F32, HID, "partg")
    partu = place([P, FP, T], F32, HID + 45056, "partu")
    pcol = adac[:, 0:2 * FP]
    pg_tok = {}

    def part_done(mat, fb, b, bank, tok):
        dst = (partg if mat == "gate" else partu)[:, fb, :]
        i = 2 * fb + (mat == "up")
        t = act(dst, bank[:, 0:T], ACT.Copy, [tok, part_free])
        t2 = act(pcol[:, i:i + 1], bank[:, T:T + 1], ACT.Copy, [tok])
        give(b, t, t2)
        pg_tok[mat, fb] = [t, t2]

    def glu_rest(mat, fb, b, bank, tok):
        i = 2 * fb + (mat == "up")
        k, z, fr = (zr if mat == "gate" else ur).take()
        c = tc[:, 4 * (i % 2) + fb % 4:4 * (i % 2) + fb % 4 + 1]
        ci = 4 * (i % 2) + fb % 4
        src = (partg if mat == "gate" else partu)[:, fb, :]
        t = tt(z[:, 0:T], bank[:, 0:T], src, ALU.add, [tok, fr, pg_tok[mat, fb]])
        t2 = tt(c, bank[:, T:T + 1], pcol[:, i:i + 1], ALU.add, [tok, tc_free[ci]])
        give(b, t, t2)
        m = tt(z[:, 0:T], z[:, 0:T], R2[:, 0:T], ALU.mult, [t, r2_tok], G)
        if mat == "gate":
            def silu():
                s = act(z[:, 0:T], z[:, 0:T], ACT.Silu, [m, t2], bias=c)
                tc_free[ci] = [s]
                gates[fb] = (k, z, s, t)
            later(1, silu)
            return
        def product():
            gk, g, s, tg = gates.pop(fb)
            hk, h, hf = hr.take()
            p = stt(h[:, :], z[:, :], c, g[:, 0:T], ALU.add, ALU.mult, [m, t2, s, hf])
            tc_free[ci] = [p]
            zr.give(gk, p)
            ur.give(k, p)

            def high():
                a = act(hidh[:, fb, :], h[:, :], ACT.Copy, [p, hid_free, tg, t])

                def low():
                    l = tt(hidl[:, fb, :], h[:, :], f32(hidh[:, fb, :]), ALU.subtract, [a, hid_free, t])
                    hr.give(hk, l)
                    hid_tok[fb] = [a, l]
                later(1, low)
            later(1, high)
        later(1, product)

    gates = {}

    def glu_done(conv):
        gate_done, put_off = {}, {}

        def done(mat, fb, b, bank, tok):
            if mat in ("gate", "gate2"):
                k, z, fr = zr.take()
                if not conv:
                    t = tt(z[:, 0:T], bank[:, 0:T], R2[:, 0:T], ALU.mult, [tok, r2_tok, fr])
                    c = tc[:, fb % 4:fb % 4 + 1]
                    t2 = V.put(lambda e: e.tensor_copy(c, bank[:, T:T + 1]), [tok, tc_free[fb % 4]])
                    s = act(z[:, 0:T], z[:, 0:T], ACT.Silu, [t, t2], bias=c)
                    tc_free[fb % 4] = [s]
                    give(b, t, t2)
                else:
                    t = tt(z[:, 1:T + 1], bank[:, 0:T], R2[:, 0:T], ALU.mult, [tok, r2_tok, fr])
                    t2 = tt(z[:, 0:1], bank[:, T:T + 1], R2[:, T:T + 1], ALU.mult, [tok, r2_tok, fr])
                    give(b, t, t2)
                    ck, c, cf = cr.take()
                    w = [v_("conv_w_2", FC * i + fb) for i in range(3)]
                    u = ts(c[:, :], z[:, 1:T + 1], w[1], v_("conv_b_2", fb), ALU.mult, ALU.add, [t, cf])
                    u = stt(c[:, :], z[:, 0:T], w[0], c[:, :], ALU.mult, ALU.add, [u, t2])
                    u = stt(c[:, :], z[:, 2:T + 2], w[2], c[:, :], ALU.mult, ALU.add, [u])

                    def silu():
                        if fb in put_off:
                            del put_off[fb]
                            s = act(z[:, 1:T + 1], c[:, :], ACT.Silu, [u])
                            cr.give(ck, s)
                            gate_done[fb] = (k, z, s)
                    put_off[fb] = silu
                    later(1, silu)
                    return
                gate_done[fb] = (k, z, s)
                return
            if fb in put_off:
                put_off[fb]()
            k, z, s = gate_done.pop(fb)
            uk, u, uf = ur.take()
            c = tc[:, 4 + fb % 4:5 + fb % 4]
            t2 = [] if conv else V.put(lambda e: e.tensor_copy(c, bank[:, T:T + 1]), [tok, tc_free[4 + fb % 4]])
            t = tt(u[:, :], bank[:, 0:T], R2[:, 0:T], ALU.mult, [tok, r2_tok, uf])
            give(b, t, t2)
            hk, h, hf = hr.take()
            if not conv:
                t = stt(h[:, :], u[:, :], c, z[:, 0:T], ALU.add, ALU.mult, [t, t2, s, hf])
                tc_free[4 + fb % 4] = [t]
            else:
                t = tt(h[:, :], u[:, :], z[:, 1:T + 1], ALU.mult, [t, s, hf])
            zr.give(k, t)
            ur.give(uk, t)

            def high():
                a = act(hidh[:, fb, :], h[:, :], ACT.Copy, [t, hid_free])

                def low():
                    l = tt(hidl[:, fb, :], h[:, :], f32(hidh[:, fb, :]), ALU.subtract, [a, hid_free])
                    hr.give(hk, l)
                    hid_tok[fb] = [a, l]
                later(1, low)
            later(1, high)
        return done

    def y_moving(mat, kc):
        ahead(kc, 4)
        return yh[:, kc, :], yl[:, kc, :], y_tok[kc]

    def hid_moving(mat, kc):
        return hidh[:, kc, :], hidl[:, kc, :], hid_tok[kc]

    def after_first(gen, n, fn, each=None):
        for i, _ in enumerate(gen):
            if each:
                each(i)
            if i == n:
                fn()

    def ffn1_norm():
        nonlocal r2_tok
        all_chunks()
        zr.free[0] = [x_tok[15]]
        r2_tok = rms_of_sum(R2, T, guard1)
        table("silu_and_others")

    part_free = [y_guard, gate_tok]
    sq_steps = squares(T)
    halves.update(gate=8, up=8)
    for i, _ in enumerate(gemm(2 * FP, gb6, y_moving, lambda m, f: TQ, part_done)):
        if i > 6:
            steps(sq_steps, 1)
        if i == HALF2:
            gains(8)
            upto[0] = 15
        if i > HALF2 and (i - HALF2) % 2 == 0 and 15 not in y_tok:
            next(chunks)
    all_chunks()
    steps(sq_steps, KC)
    shift_tok = shift_columns(8, [y_tok[15], x_tok[15], y_guard])
    for kc in range(8, KC):
        y_tok[kc].append(shift_tok)
    zr.free[0] = [x_tok[15]]
    r2_tok = rms_of_sum(R2, T, guard1)
    table("silu_and_others")
    for _ in gemm(2 * FP, gb6, y_moving, lambda m, f: TQ, glu_rest):
        pass
    halves.clear()
    for _ in gemm(4 * (FC - FP), gb6, y_moving, lambda m, f: TQ, glu_done(False)):
        pass
    drain()

    m2 = place([P, KC, T], F32, R0, "m2")
    y_free = [(PE.sem, PE.n)]

    def down_done(mat, fb, b, bank, tok):
        s = square_in(bank[:, 0:T], T, [tok], fb == 0, fb == 15)
        t = act(m2[:, fb, :], bank[:, 0:T], ACT.Copy, [tok, y_free])
        give(b, s, t)
        m_tok[fb] = [t]

    table("natural_log_exp_and_others")
    gate_tok = gain(mul[:, 3, :], GATE_F, 16, v_("g_ffn_post", 0, 16), False)
    for _ in gemm(88, gb, hid_moving, lambda m, f: T, down_done):
        pass
    drain()
    low_part()
    rm_tok = rms_of_sum(Rm, T, [zr.free[0]])
    rm_users = []

    B2 = Region(R0)
    B2.at = R0 + 16384
    gh = place([P, KC, TM], F32R, HID, "gh")
    gl = place([P, KC, TM], F32R, HID + 17408, "gl")
    hid_used = [(PE.sem, PE.n)]
    y_tok.clear()
    chunks = residual_chunks(lambda kc: m2[:, kc, :], lambda kc: mul[:, 3, kc:kc + 1], Rm, [rm_tok, gate_tok], lambda kc: v_("mix_norm_g_2", kc),
                             [hid_used, vec_load, meta_load], gh, gl, TM, lambda kc: [])
    next(chunks)
    next(chunks)

    TD = TM - T
    guard2 = [(V.sem, V.n), (A.sem, A.n), (PE.sem, PE.n), (G.sem, G.n)]
    RA = Region(R0, R0 + 33024)
    kn = RA([P, 8, TM], F32, "kn")
    qn = RA([P, 8, TQ], F32, "qn")
    vm_at = RA.at
    vm = RA([P, 3, 1024], F32, "vm")
    cs2 = RA([P, 2, TM], F32, "cs2")
    kpr = RA([P, TM], F32, "kpr")
    mb2 = RA([P, 8, TD], F32, "mb2")
    RB = Region(HID + 34816, TMP)
    krz = RB([P, 8, TM], F32, "krz")
    qr = RB([P, 4, TQ], F32, "qr")
    b_at = RB.at
    cq = RB([P, 4, TQ], F32, "cq")
    ckv = RB([P, 2, TM], F32, "ckv")
    cqh = RB([P, 4, TQ], F32R, "cqh")
    cql = RB([P, 4, TQ], F32R, "cql")
    ckh = RB([P, 2, TM], F32R, "ckh")
    ckl = RB([P, 2, TM], F32R, "ckl")
    mbh = place([P, 8, TQ], F32R, R0, "mbh")
    mbl = place([P, 8, TQ], F32R, vm_at, "mbl")
    RD = Region(b_at, RB.at)
    outa = RD([P, 8, TQ], F32, "outa")
    na_sum = Sum(RD([P, TM], F32, "ssum"))
    mla_R = place([P, TM], F32, vm_at + 8256, "R")
    na_R = RD([P, TM], F32, "R")
    naq = [R([P, TQ], F32, "naq") for R in (RB, RB, RB, RD, RD)]
    nak = [R([P, TM], F32, "nak") for R in (RB, RB, RB, RD, RD)]
    nav = [R([P, 3, P], F32, "nav") for R in (RB, RB, RB, RD, RD)]
    bt_at = RB.at
    bt = Ring([RB([P, 2, TM], F32, "bt")])
    rotr = Ring([place([P, TM], F32, bt_at + 1088 * i, "rot") for i in range(2)])
    kpsq = place([P, TM], F32, RB.at, "kpsq")
    tz = Ring([RB([P, 6, 64], F32, "tz")])
    revt = causal[:, 0:P]
    er2 = Ring([RB([P, 2, TM], F32, "er2") for _ in range(2)])
    em = Ring([RB([P, TM], F32, "em") for _ in range(2)])
    tmpr = Ring([RB([P, TM], F32, "tmp") for _ in range(2)])
    RC = Region(TMP + 3 * 1088, LIMIT - 1088)
    pt2 = Ring([RC([P, 3, TQ], F32, "pt2") for _ in range(2)])
    rhr = Ring([RC([P, TM], F32, "rh") for _ in range(2)])
    mah = place([P, 8, TQ], F32R, HID, "mah")
    mal = place([P, 8, TQ], F32R, HID + 8256, "mal")
    ckv_sum = Sum(kn[:, 7, :])
    ckv_sum.tok = list(guard2)
    for ring in (rotr, tz, er2, em, tmpr, pt2, rhr):
        for k in ring.free:
            ring.free[k] = list(guard2)
    nar = Ring([0, 1, 2, 3, 4], {k: list(guard2) if k < 3 else None for k in range(5)})

    zero2 = []
    cs_load = load(cs2[:, :, :], rope2, "ld_rope2", after=guard2)
    rev_load = load(revt, rev, "ld_rev", after=guard2)
    mb_load = load(mb2[:, :, :], bass.AP(mbias.tensor, 0, [[0, P], [1, 8 * TD]]), "ld_mb", after=guard2)
    naq_gain = small[:, 3:4]
    ng_tok = ts(naq_gain, v_("na_q_g_2"), float(128 ** -0.5), None, ALU.mult, None, [vec_load], G)
    SM = float(192 ** -0.5)

    tz_sem = [sem(f"tz{i}") for i in range(2)]

    def bias_load(h):
        k, Z, fr = tz.take()
        toks = []
        for a in range(2):
            src = bass.AP(rpb.tensor, (h * 15 + 4 + a) * RPB_ROW + 16, [[1, 64], [RPB_ROW, 6], [1, 64]])
            SP.put(lambda q, a=a, src=src: q.dma_start(Z[64 * a:64 * a + 64, :, :], src).then_inc(tz_sem[a], 16), fr, signal=False)
            toks.append((tz_sem[a], 16 * (h + 1)))
        return k, Z, toks

    def bias_tile(h):
        zk, Z, ztok = B_["tz", h]
        b, bank, free = ab.take()
        p = mm(bank[:, 0:384], revt, Z[:, :, :].rearrange("p j c -> p (j c)"), True, True, [free, ztok, rev_load], signal=True)
        tz.give(zk, p)
        if h + 1 < 8:
            B_["tz", h + 1] = bias_load(h + 1)
        k, B, fr = bt.take()
        mask = namask.unsqueeze(1).to_broadcast([P, 4, 64])
        toks = []
        for qb in range(2):
            src = bank[:, 128 - 128 * qb:384 - 128 * qb].rearrange("p (j c) -> p j c", j=4)
            toks.append(tt(B[:, qb, 0:T].rearrange("p (j c) -> p j c", j=4), src, mask, ALU.add, [p, fr]))
        give(b, toks)
        toks.append(G.put(lambda e: e.tensor_copy(B[:, :, T:TM], mb2[:, h, :].unsqueeze(1).to_broadcast([P, 2, TD])), [mb_load, fr]))
        return k, B, toks

    def head_rms(sq, n, after, div):
        b, bank, free = ab.take()
        t = mm(bank[:, 0:n], ones[:, :], sq[:, 0:n], True, True, [free, after], signal=True)
        k, R, fr = rhr.take()
        a, e = rms(R[:, 0:n], bank[:, 0:n], div, [t, fr])
        give(b, a)
        return k, R, t, e

    def rotate2(dst, n, after, then, wait=1):
        k, a, fr = rotr.take()
        t = tt(a[:, 0:n], dst, cs2[:, 1, 0:n], ALU.mult, [after, fr, cs_load], G)
        u = tt(dst, dst, cs2[:, 0, 0:n], ALU.mult, [after, t, cs_load], G)

        def f():
            b, bank, free = ab.take()
            p = mm(bank[:, 0:n], swap, a[:, 0:n], True, True, [free, t], signal=True)
            rotr.give(k, p)
            r = tt(dst, bank[:, 0:n], dst, ALU.add, [p, u])
            give(b, r)
            then(r)
        later(wait, f)

    B_ = {}

    def cq_done(mat, fb, b, bank, tok):
        if fb < CKV:
            i = fb - CQ
            t = tt(cq[:, i, :], bank[:, 0:TQ], R2[:, 0:TQ], ALU.mult, [tok, r2_tok, guard2])
            give(b, t)
            square_in(cq[:, i, :], TQ, [t], i == 0)
            B_["cq", i] = t
            if i == 3:
                def f():
                    k, R, fr = rhr.take()
                    e = rms_of_sum(R, TQ, [fr], 512)
                    last, high = [], []
                    for i in range(4):
                        t = stt(cq[:, i, :], cq[:, i, :], v_("mla_cq_g_2", i), R[:, 0:TQ], ALU.mult, ALU.mult, [e, B_["cq", i]])
                        high.append(act(cqh[:, i, :], cq[:, i, :], ACT.Copy, [t, guard2]))
                        last.append(t)
                    rhr.give(k, last)
                    for i in range(4):
                        l = tt(cql[:, i, :], cq[:, i, :], f32(cqh[:, i, :]), ALU.subtract, [last[i], high[i]])
                        B_["cqn", i] = [high[i], l]
                later(1, f)
        elif fb < KPE:
            i = fb - CKV
            t = tt(ckv[:, i, :], bank[:, 0:TM], R2[:, :], ALU.mult, [tok, r2_tok, guard2])
            give(b, t)
            square_in(ckv[:, i, :], TM, [t], i == 0, to=ckv_sum)
            B_["ckv", i] = t
            if i == 1:
                def f():
                    k, R, fr = rhr.take()
                    e = rms_of_sum(R, TM, [fr], 256, ckv_sum)
                    last, high = [], []
                    for i in range(2):
                        t = stt(ckv[:, i, :], ckv[:, i, :], v_("mla_ckv_g_2", i), R[:, :], ALU.mult, ALU.mult, [e, B_["ckv", i]])
                        high.append(act(ckh[:, i, :], ckv[:, i, :], ACT.Copy, [t, guard2]))
                        last.append(t)
                    rhr.give(k, last)
                    for i in range(2):
                        l = tt(ckl[:, i, :], ckv[:, i, :], f32(ckh[:, i, :]), ALU.subtract, [last[i], high[i]])
                        B_["ckn", i] = [high[i], l]
                later(2, f)
        else:
            t = tt(kpr[:, :], bank[:, 0:TM], R2[:, :], ALU.mult, [tok, r2_tok, guard2])
            give(b, t)
            a = act(kpsq[:, :], kpr[:, :], ACT.Square, [t, guard2])
            s = ts(kpsq[:, :], kpsq[:, :], 0.5, None, ALU.mult, None, [a], G)
            B_["kpsq"] = s
            t = ts(kpr[:, :], kpr[:, :], v_("mk_r"), None, ALU.mult, None, [t, a])

            rotate2(kpr[:, :], TM, [t], lambda r: B_.update({"kpr": r}), 2)

    def g_moving(mat, kc):
        ahead(kc, 4)
        return gh[:, kc, :], gl[:, kc, :], y_tok[kc]

    def in2_width(mat, fb):
        return TQ if fb < KA or CQ <= fb < CKV else TM

    def chain(mat, fb, b, bank, tok):
        cq_done(mat, fb, b, bank, tok)

    def in2_norm():
        nonlocal r2_tok
        all_chunks()
        steps(sq_steps, KC)
        zr.free[0] = [x_tok[15]]
        r2_tok = rms_of_sum(R2, TM, [hid_tok[FC - 1]])

    sq_steps = squares(TM)

    def beside(i):
        if 1 <= i <= 8:
            zero2.append(memset(krz[:, i - 1, :], 0.0, guard2))
            zero2.append(memset(vm[:, 2, 128 * i - 128:128 * i], 0.0, guard2))
        if i >= SQ2:
            steps(sq_steps, 2)

    after_first(gemm(12, gb6, g_moving, in2_width, chain), 10, in2_norm, beside)
    ab = Banks([3, 4, 5, 6, 7])
    for _ in gemm(2, gb, g_moving, in2_width, chain):
        pass
    zero2.extend(memset(b[:, 2, :], 0.0, guard2) for b in nav[0:3])
    zero2.extend(memset(b[:, :, :], 0.0, [guard2, x_tok[15], y_tok[15]]) for b in pt2.items)

    def q_done(mat, fb, b, bank, tok):
        p, r = divmod(fb, 3)
        if r == 0:
            t = ts(qr[:, p, :], bank[:, 0:TQ], v_("mq_r"), None, ALU.mult, None, [tok, guard2])
            k, s, fr = rotr.take()
            a = act(s[:, 0:TQ], bank[:, 0:TQ], ACT.Square, [t, fr])
            give(b, a)
            B_["sqr", p] = (k, s, a)

            rotate2(qr[:, p, :], TQ, [t], lambda r: B_.update({("qr", p): r}))
            return
        h = 2 * p + r - 1
        t = act(qn[:, h, :], bank[:, 0:TQ], ACT.Copy, [tok, guard2])
        k, sq, fr = sqf.take()
        a = act(sq[:, 0:TQ], bank[:, 0:TQ], ACT.Square, [tok, fr])
        give(b, t, a)
        half = slice(64 * (h % 2), 64 * (h % 2) + 64)
        rk, rs, ra = B_["sqr", p]
        t2 = tt(sq[half, 0:TQ], sq[half, 0:TQ], rs[half, 0:TQ], ALU.add, [a, ra])
        if r == 2:
            rotr.give(rk, t2, B_["rs0"])
        B_["rs0"] = t2

        def f():
            k2, R, t3, e = head_rms(sq, TQ, [t2], 192)
            sqf.give(k, t3)
            u = stt(qn[:, h, :], qn[:, h, :], v_("mq_n"), R[:, 0:TQ], ALU.mult, ALU.mult, [e, t])
            w = tt(qr[half, p, :], qr[half, p, :], R[half, 0:TQ], ALU.mult, [e, B_["qr", p]])
            rhr.give(k2, u, w)
            B_["q", h] = [u, w]
        later(1, f)

    def k_done(mat, fb, b, bank, tok):
        h, r = divmod(fb, 2)
        if r == 0:
            t = act(kn[:, h, :], bank[:, 0:TM], ACT.Copy, [tok, guard2])
            k, sq, fr = sqf.take()
            a = act(sq[:, :], bank[:, 0:TM], ACT.Square, [tok, fr])
            give(b, t, a)
            t2 = tt(sq[:, :], sq[:, :], kpsq[:, :], ALU.add, [a, B_["kpsq"]], G)
            half = slice(64 * (h % 2), 64 * (h % 2) + 64)
            B_["kpsq_used"] = t2

            def f():
                k2, R, t3, e = head_rms(sq, TM, [t2], 192)
                sqf.give(k, t3)
                u = stt(kn[:, h, :], kn[:, h, :], v_("mk_n"), R[:, :], ALU.mult, ALU.mult, [e, t])
                w = tt(krz[half, h, :], kpr[half, :], R[half, :], ALU.mult, [e, B_["kpr"], zero2])
                rhr.give(k2, u, w)
                B_["k", h] = [u, w]
            later(1, f)
            return
        k, v, fr = tmpr.take()
        t = act(v[:, :], bank[:, 0:TM], ACT.Copy, [tok, fr])
        give(b, t)

        def f():
            c = slice(P * h, P * h + P)
            p, e = values(v, t, vm[:, 0:2, c], vm[0:16, 2, c])
            tmpr.give(k, p)
            B_["v", h] = e
        later(1, f)

    def values(v, after, dst, dst_meta):
        b, bank, free = ab.take()
        tr(bank[:, 0:P], v[:, 0:P], [free, after])
        tr(bank[:, P:2 * P], v[:, P:2 * P])
        p = tr(bank[0:TD, 2 * P:3 * P], v[:, T:TM], signal=True)
        e0 = act(dst, bank[:, 0:2 * P].rearrange("p (k d) -> p k d", k=2), ACT.Copy, [p, guard2])
        e1 = act(dst_meta, bank[0:TD, 2 * P:3 * P], ACT.Copy, [p, zero2])
        give(b, e0, e1)
        return p, [e0, e1]

    def cq_moving(mat, kc):
        return cqh[:, kc, :], cql[:, kc, :], B_["cqn", kc]

    def ck_moving(mat, kc):
        return ckh[:, kc, :], ckl[:, kc, :], B_["ckn", kc]

    kv_done = []

    def normalise(d):
        E, M, c, mk = d["E"], d["M"], d["c"], d["mk"]
        t = V.put(lambda e: e.reciprocal(stat[:, c:c + 2], stat[:, c + 3:c + 5]), [d["es"][0:2]])
        t2 = V.put(lambda e: e.reciprocal(stat[0:1, c + 2:c + 3], stat[0:1, c + 5:c + 6]), [d["es"][2]])
        ns = [ts(E[:, qb, :], E[:, qb, :], stat[:, c + qb:c + qb + 1], None, ALU.mult, None, [t]) for qb in range(2)]
        ns.append(ts(M[0:1, mk], M[0:1, mk], stat[0:1, c + 2:c + 3], None, ALU.mult, None, [t2]))
        d["ns"] = ns

    def turn_p2(d):
        E, M, mk, ns = d["E"], d["M"], d["mk"], d["ns"]
        b, bank, free = ab.take()
        for kc in range(2):
            for qb in range(2):
                p = tr(bank[:, T * kc + P * qb:T * kc + P * qb + P], E[:, qb, P * kc:P * kc + P], [free, ns[qb]],
                       signal=(kc == 1 and qb == 1))
        b2, bank2, free2 = ab.take()
        for qb in range(2):
            tr(bank2[0:TD, P * qb:P * qb + P], E[:, qb, T:TM], [free2])
        full = mk.stop > TD
        if full:
            for kc in range(2):
                tr(bank2[:, T + kc:T + kc + 1], M[0:1, P * kc:P * kc + P], [ns[2]])
            p2 = tr(bank2[0:TD, T + 2:T + 3], M[0:1, T:TM], signal=True)
        else:
            p2 = tr(bank2[0:TD, T + 2:T + 3], M[0:1, 0:TD], [ns[2]], signal=True)
        er2.give(d["er"], p2)
        em.give(d["emk"], p2)
        r, buf, fr = pt2.take()
        es = [act(buf[:, 0:2, 0:T], bank[:, :].rearrange("p (k q) -> p k q", k=2), ACT.Copy, [p, fr, zero2])]
        give(b, es[0])
        es.append(act(buf[0:TD, 2, 0:T], bank2[0:TD, 0:T], ACT.Copy, [p2, fr, zero2]))
        es.append(act(buf[0:TD, 2, T:T + 1], bank2[0:TD, T + 2:T + 3], ACT.Copy, [p2]))
        if full:
            es.append(act(buf[:, 0:2, T:T + 1], bank2[:, T:T + 2].unsqueeze(2), ACT.Copy, [p2]))
        give(b2, es[1:])
        d.update(pr=r, buf=buf, ps=es)

    def out_of(d, dst, after, first, to, sq):
        b, bank, p = d["ob"]
        if first:
            s = square_in(bank[:, 0:TQ], TQ, [p], True, False, to)
        else:
            s = act(sq[:, 0:TQ], bank[:, 0:TQ], ACT.Square, [p])

            def total():
                to.tok = [tt(to.buf[:, 0:TQ], to.buf[:, 0:TQ], sq[:, 0:TQ], ALU.add, [s, to.tok], G)]
                to.heads += 1
            later(1, total)
        a = act(dst, bank[:, 0:TQ], ACT.Copy, [p, after])
        give(b, s, a)
        return a

    mla, na = {}, {}

    def exps(d):
        E, M, c, mk, vs = d["E"], d["M"], d["c"], d["mk"], d["vs"]
        es = [act(E[:, qb, :], E[:, qb, :], ACT.Exp, [vs[qb]], scale=-1.0, bias=stat[:, c + qb:c + qb + 1],
                  accum_out=stat[:, c + 3 + qb:c + 4 + qb]) for qb in range(2)]
        es.append(act(M[0:1, mk], M[0:1, mk], ACT.Exp, [vs[2]], scale=-1.0, bias=stat[0:1, c + 2:c + 3],
                      accum_out=stat[0:1, c + 5:c + 6]))
        d["es"] = es

    def mla_stages():
        def s0(h):
            er, E, fr = er2.take()
            emk, M, fr2 = em.take()
            c = 8 * (h % 4)
            vs = []
            for i, q in enumerate((slice(0, P), slice(P, T), slice(T, T + 1))):
                b, bank, free = ab.take()
                m = 1 if i == 2 else P
                mm(bank[0:m, 0:TM], qn[:, h, q], kn[:, h, :], True, False, [free, B_["q", h], B_["k", h]])
                p = mm(bank[0:m, 0:TM], qr[:, h // 2, q], krz[:, h, :], False, True, signal=True)
                dst = M[0:1, :] if i == 2 else E[:, i, :]
                f2 = fr2 if i == 2 else fr
                v = ts(dst, bank[0:m, 0:TM], -SM, None, ALU.mult, ALU.min, [p, f2], accum_out=stat[0:m, c + i:c + i + 1])
                give(b, v)
                vs.append(v)
            d = mla[h] = dict(E=E, M=M, c=c, mk=slice(0, TM), vs=vs, er=er, emk=emk)
            exps(d)

        def s1(h):
            normalise(mla[h])

        def s1b(h):
            turn_p2(mla[h])

        def s2(h):
            d = mla[h]
            b, bank, free = ab.take()
            for kc in range(3):
                p = mm(bank[:, 0:TQ], vm[:, kc, P * h:P * h + P], d["buf"][:, kc, :], kc == 0, kc == 2,
                       [free, d["ps"], B_["v", h]], signal=(kc == 2))
            pt2.give(d["pr"], p)
            d["ob"] = (b, bank, p)
            B_["outb", h] = out_of(d, qn[:, h, :], [p], h == 0, main_sum, kn[:, h, :])

        return [s0, s1, s1b, s2]

    def mla_norm():
        while main_sum.heads < 7:
            yield
        yield
        R = mla_R
        free = [(PE.sem, PE.n)]
        e = rms_of_sum(R, TQ, free, 1024)
        yield
        for h in range(8):
            t = stt(qn[:, h, :], qn[:, h, :], v_("mla_out_g_2", h), R[:, 0:TQ], ALU.mult, ALU.mult, [e, B_["outb", h]])
            a = act(mbh[:, h, :], qn[:, h, :], ACT.Copy, [t, free])
            l = tt(mbl[:, h, :], qn[:, h, :], f32(mbh[:, h, :]), ALU.subtract, [t, a, free])
            B_["mix", 8 + h] = [a, l]
            if h % 2:
                yield
        B_["mla"] = True

    def na_done(mat, fb, b, bank, tok):
        kind, h = divmod(fb, 8)
        if kind == 0:
            force(lambda: nar.free[nar.i] is not None)
            k, _, fr = nar.take()
            B_["na", h] = (k, fr)
        k, fr = B_["na", h]
        n = TQ if kind == 0 else TM
        if kind < 2:
            dst = (naq, nak)[kind][k]
            t = tt(dst[:, :], bank[:, 0:n], R2[:, 0:n], ALU.mult, [tok, r2_tok, fr])
            give(b, t)
            sk, sq, sf = sqf.take()
            a = act(sq[:, 0:n], dst[:, :], ACT.Square, [t, sf])

            def f():
                k2, R, t3, e = head_rms(sq, n, [a], 128)
                sqf.give(sk, t3)
                g = naq_gain if kind == 0 else v_("na_k_g_2")
                u = stt(dst[:, :], dst[:, :], g, R[:, 0:n], ALU.mult, ALU.mult, [e, ng_tok])
                rhr.give(k2, u)
                B_["naqk"[0:2] + str(kind), h] = u
            later(1, f)
            return
        tk, v, tf = tmpr.take()
        t = tt(v[:, :], bank[:, 0:TM], R2[:, :], ALU.mult, [tok, r2_tok, tf])
        give(b, t)
        B_["r2_used"] = t

        def f():
            p, e = values(v, [t, fr], nav[k][:, 0:2, :], nav[k][0:TD, 2, :])
            tmpr.give(tk, p)
            B_["nav", h] = e
        later(1, f)

    def na_stages():
        def s0(h):
            k, fr = B_["na", h]
            bk, B, btok = bias_tile(h)
            er, E, fr = er2.take()
            emk, M, fr2 = em.take()
            c = 8 * (h % 4)
            vs = []
            for i, q in enumerate((slice(0, P), slice(P, T), slice(T, T + 1))):
                b, bank, free = ab.take()
                toks = [free, B_["na0", h], B_["na1", h]]
                if i < 2:
                    p = mm(bank[:, 0:TM], naq[k][:, q], nak[k][:, :], True, True, toks, signal=True)
                    v = ttr(E[:, i, :], bank[:, 0:TM], B[:, i, :], -1.0, BIG, ALU.add, ALU.min, stat[:, c + i:c + i + 1],
                            [p, btok, fr])
                else:
                    p = mm(bank[0:1, 0:TD], naq[k][:, q], nak[k][:, T:TM], True, True, toks, signal=True)
                    v = ttr(M[0:1, 0:TD], bank[0:1, 0:TD], B[0:1, 0, T:TM], -1.0, BIG, ALU.add, ALU.min,
                            stat[0:1, c + i:c + i + 1], [p, btok, fr2])
                give(b, v)
                vs.append(v)
            bt.give(bk, vs)
            d = na[h] = dict(E=E, M=M, c=c, mk=slice(0, TD), vs=vs, er=er, emk=emk)
            exps(d)

        def s1(h):
            normalise(na[h])

        def s1b(h):
            turn_p2(na[h])

        def s2(h):
            d = na[h]
            k, _ = B_["na", h]
            b, bank, free = ab.take()
            mm(bank[:, 0:TQ], nav[k][:, 2, :], d["buf"][:, 2, :], True, False, [free, d["ps"], B_["nav", h]])
            for kc in range(2):
                p = mm(bank[:, 0:T], nav[k][:, kc, :], d["buf"][:, kc, 0:T], False, kc == 1, signal=(kc == 1))
            pt2.give(d["pr"], p)
            d["ob"] = (b, bank, p)
            B_["outa", h] = out_of(d, outa[:, h, :], [kv_done], h == 0, na_sum, naq[k])
            later(1, lambda: nar.give(k, p, na_sum.tok))

        return [s0, s1, s1b, s2]

    def na_norm():
        while na_sum.heads < 7:
            yield
        yield
        R = na_R
        e = rms_of_sum(R, TQ, [kv_done], 1024, na_sum)
        yield
        for h in range(8):
            t = stt(outa[:, h, :], outa[:, h, :], v_("na_out_g_2", h), R[:, 0:TQ], ALU.mult, ALU.mult, [e, B_["outa", h]])
            a = act(mah[:, h, :], outa[:, h, :], ACT.Copy, [t, in2_pe])
            l = tt(mal[:, h, :], outa[:, h, :], f32(mah[:, h, :]), ALU.subtract, [t, a, in2_pe])
            B_["mix", h] = [a, l]
            if h % 2:
                yield

    sides = []

    def step_sides():
        for s in list(sides):
            if next(s, "end") == "end":
                sides.remove(s)

    def force(cond):
        n = 0
        while not cond():
            tick()
            step_sides()
            n += 1
            assert n < 200, "stuck"

    def run_with(main, rate):
        credit = 0.0
        for _ in main:
            credit += rate
            while credit >= 1.0:
                credit -= 1.0
                step_sides()

    in2_pe = []
    HEADS = "MMMMNMMMNMNNNNNN"
    heads = [(kind, HEADS[:i].count(kind)) for i, kind in enumerate(HEADS)]

    def may2(kind, h, s):
        if s == 0:
            need = [("nav", h), "kv"] if kind == "N" else [("q", h), ("k", h), ("v", h)]
            return all(x in B_ for x in need) and er2.free[er2.i] is not None and em.free[em.i] is not None
        return s != 2 or pt2.free[pt2.i] is not None

    sides += [schedule(heads, {"M": mla_stages(), "N": na_stages()}, may2), mla_norm(), na_norm()]

    def after_up():
        if ("v", 7) in B_ and ("k", 7) in B_ and not kv_done:
            kv_done.extend([(PE.sem, PE.n), B_["k", 7], B_["v", 7]])
            zero2.extend(memset(nav[i][:, 2, :], 0.0, kv_done) for i in (3, 4))
            na_sum.tok = list(kv_done)
            for i in (3, 4):
                nar.free[i] = list(kv_done)
            bt.free[0] = [kv_done, list(rotr.free.values())]
            tz.free[0] = [guard2, kv_done, B_["kpsq_used"]]
            B_["tz", 0] = bias_load(0)
            later(2, lambda: B_.update(kv=True))

    def main_moving(mat, kc):
        return {"in2": g_moving, "qup": cq_moving, "kvup": ck_moving}[mat](mat, kc)

    def main_width(mat, fb):
        return {"in2": in2_width(mat, fb), "qup": TQ, "kvup": TM}[mat]

    def main_done(mat, *a):
        {"in2": na_done, "qup": q_done, "kvup": k_done}[mat](mat, *a)

    def watched(gen):
        for x in gen:
            after_up()
            yield x

    ab = Banks([4, 5, 6, 7])
    run_with(watched(gemm(58, gbm, main_moving, main_width, main_done)), RATE)
    in2_pe.append((PE.sem, PE.n))
    drain()
    force(lambda: "mla" in B_)

    halves["out2"] = 8

    def mix_moving(mat, kc):
        return (mbh[:, kc - 8, :], mbl[:, kc - 8, :], B_["mix", kc]) if kc >= 8 else (mah[:, kc, :], mal[:, kc, :], B_["mix", kc])

    def out_first(mat, fb, b, bank, tok):
        t = tt(X[:, fb, 0:TQ], bank[:, 0:TQ], X[:, fb, 0:TQ], ALU.add, [tok, x_tok[fb]])
        give(b, t)
        x_tok[fb] = [t]

    run_with(gemm(16, gb, mix_moving, lambda m, f: TQ, out_first), RATE2)
    n = 0
    while sides:
        tick()
        step_sides()
        n += 1
        assert n < 500
    guard3 = [(V.sem, V.n), (A.sem, A.n), (PE.sem, PE.n), (G.sem, G.n)]
    for ring in (zr, ur, hr, cr):
        for k in ring.free:
            ring.free[k] = list(guard3)

    def out_second(mat, fb, b, bank, tok):
        t = tt(X[:, fb, 0:TQ], bank[:, 0:TQ], X[:, fb, 0:TQ], ALU.add, [tok, x_tok[fb]])
        give(b, t)
        x_tok[fb] = [t]

        def rest():
            s = v_("ffn_norm_g_2", fb)
            a = act(yh[:, fb, :], X[:, fb, 0:TQ], ACT.Copy, [t, guard3], scale=s)
            square_in(X[:, fb, 0:TQ], TQ, [t], fb == 0, True)

            def low():
                l = stt(yl[:, fb, :], X[:, fb, 0:TQ], s, f32(yh[:, fb, :]), ALU.mult, ALU.subtract, [t, guard3, a])
                y_tok[fb] = [a, l]
            later(1, low)
        later(1, rest)

    run_with(gemm(16, gb8, mix_moving, lambda m, f: TQ, out_second), 1.0)
    halves.clear()
    for i in range(2):
        zt = memset(zr.items[i][:, TQ - 1:TQ], 0.0, guard3)
        zr.free[i] = [guard3, zt]

    ab = Banks([6, 7])
    hid_free = [(PE.sem, PE.n), (A.sem, A.n)]

    def ffn2_norm():
        nonlocal r2_tok
        r2_tok = rms_of_sum(R2, TQ, [B_["r2_used"]])
        table("silu_and_others")

    after_first(gemm(176, gb6, y_moving, lambda m, f: TQ if m == "gate2" else T, glu_done(True)), 6, ffn2_norm)
    drain()

    oring2 = [ur.items[0], ur.items[1], hr.items[0], hr.items[1]]
    ofree = [ur.free[0], ur.free[1], hr.free[0], hr.free[1]]
    osem = [sem(f"out{i}") for i in range(4)]
    ocount = [0] * 4

    def last_done(mat, fb, b, bank, tok):
        k = fb % 4
        o, s = oring2[k], osem[k]
        t = tt(o[:, :], bank[:, 0:T], X[:, fb, 0:T], ALU.add, [tok, x_tok[fb], ofree[k]])
        give(b, t)
        SP.put(lambda q: q.dma_start(out[:, fb, :], o[:, :]).then_inc(s, 16), [t], signal=False)
        ocount[k] += 16
        ofree[k] = [(s, ocount[k])]

    for _ in gemm(88, gb, hid_moving, lambda m, f: T, last_done):
        pass
    assert not st["ready"] and st["done"] == len(plan)
    out_sems = [(osem[k], ocount[k]) for k in range(4)]

    with nc.Block() as block:
        @block.sync
        def _(e):
            SP.emit(e)
            for s, v in out_sems:
                e.wait_ge(s, v)

        @block.tensor
        def _(e):
            PE.emit(e)

        @block.vector
        def _(e):
            V.emit(e)

        @block.scalar
        def _(e):
            A.emit(e)

        @block.gpsimd
        def _(e):
            G.emit(e)


def layout(inputs):
    g = {k: np.asarray(v) for k, v in inputs.items()}

    def part(name, n=None):
        return np.asarray(g[name]).reshape(-1, P).T

    def rows(a):
        return a.T.reshape(KC, P, -1).transpose(1, 0, 2)

    n, r = 128, 64
    conv = g["conv_w_2"][0].reshape(3, FC, P).transpose(2, 0, 1).reshape(P, 3 * FC)
    mq, mk = g["mla_q_g_2"][0], g["mla_k_g_2"][0]
    vec = {"conv_w_2": conv, "mq_n": mq[:n, None], "mk_n": mk[:n, None],
           "mq_r": np.concatenate([mq[n:], mq[n:]])[:, None], "mk_r": np.concatenate([mk[n:], mk[n:]])[:, None]}
    vecs = np.concatenate([vec[k] if k in vec else part(k) for k, _ in VECS], axis=1)
    assert vecs.shape == (P, NVEC)

    w_in = g["w_in"][0]
    w_ada = g["w_ada"][0]
    w_in2 = g["w_in_2"][0]
    kpe = w_in2[:, 3840:3904]
    qup = g["w_q_up_2"][0].reshape(512, 8, 192)
    qcols = []
    for p in range(4):
        a, b = qup[:, 2 * p], qup[:, 2 * p + 1]
        qcols += [a[:, n:], b[:, n:], a[:, :n], b[:, :n]]
    mats = {"o": g["w_o"][0], "gate": g["w_gate"][0], "up": g["w_up"][0], "down": g["w_down"][0],
            "in2": np.concatenate([w_in2, kpe], axis=1), "qup": np.concatenate(qcols, axis=1), "kvup": g["w_kv_up_2"][0],
            "out2": g["w_out_2"][0], "gate2": g["w_gate_2"][0], "up2": g["w_up_2"][0], "down2": g["w_down_2"][0]}
    plan = tile_plan()
    wst = np.zeros((len(plan), P, TILE), np.float32)
    for t, what in enumerate(plan):
        if what[0] == "a":
            c, h = divmod(what[1], 2)
            wst[t] = w_ada[1024 * h:1024 * (h + 1), P * c:P * (c + 1)].T
        elif what[0] == "x":
            _, grp, kp = what
            d = wst[t].reshape(P, 2, 512)
            for i in range(2):
                at = 0
                for a, b in W_IN_GROUPS[grp]:
                    d[:, i, at:at + b - a] = w_in[(2 * kp + i) * P:(2 * kp + i + 1) * P, a:b]
                    at += b - a
        else:
            for i, (m, kc, fb) in enumerate(what[1]):
                wst[t, :, P * i:P * (i + 1)] = mats[m][kc * P:(kc + 1) * P, fb * P:(fb + 1) * P]

    meta = np.concatenate([g["meta_tokens_2"][15:], g["meta_tokens_2"][:15]])
    rpb = np.zeros((8, 15, RPB_ROW), np.float32)
    rpb[:, :, 64:95] = g["na_rpb_2"][0]
    mb = g["na_meta_bias_2"][0]
    mbias = np.concatenate([mb[:, 15:], mb[:, :15]], axis=1)

    ident = np.eye(P, dtype=np.float32)
    swap = np.zeros((P, P), np.float32)
    for hd in (0, 64):
        for j in range(32):
            swap[hd + 32 + j, hd + j] = -1.0
            swap[hd + j, hd + 32 + j] = 1.0
    q, k = np.arange(P)[:, None], np.arange(P)[None, :]
    causal = np.concatenate([np.zeros((P, P)), np.where(k <= q, 0.0, NEG)], axis=1)
    c = np.arange(P) % 64
    start = np.clip(c - 8, 0, 48)[:, None]
    kk = np.arange(64)[None, :]
    namask = np.where((kk >= start) & (kk < start + 16), 0.0, NEG)
    inv = np.power(np.float32(500000.0), -(np.arange(0, 32, 2, dtype=np.float32) / np.float32(32)))
    freq = np.broadcast_to(inv, (P, 16))
    consts = np.concatenate([ident, swap, causal, namask, freq], axis=1).astype(np.float32)
    inv2 = np.power(np.float32(10000.0), -np.arange(0, 64, 2, dtype=np.float32) / np.float32(64)).astype(np.float32)
    posn = np.concatenate([np.arange(16, 272), [15], np.arange(15)]).astype(np.float32)
    angle = (posn[None, :] * inv2[np.arange(P) % 32][:, None]).astype(np.float32)
    rope2 = np.stack([np.cos(angle), np.sin(angle)], axis=1).astype(np.float32)

    return {"wst": wst, "xT": rows(g["x"][0]), "metaT": rows(meta), "vecs": vecs, "consts": consts, "rope2": rope2, "rev": ident[::-1],
            "cvec": g["c"], "positions": g["positions"][0].reshape(2, P).T,
            "lambdas": np.concatenate([g["lambda_q1"], g["lambda_k1"], g["lambda_q2"], g["lambda_k2"]]),
            "rpb": rpb, "mbias": mbias}


def kernel(**inputs):
    import concourse.bacc as bacc
    from concourse.bass_utils import run_bass_kernel_spmd

    nc = bacc.Bacc("TRN2", target_bir_lowering=False, num_devices=1)
    arrays = {f"in_{k}": np.ascontiguousarray(a) for k, a in layout(inputs).items()}
    args = [nc.dram_tensor(k, a.shape, mybir.dt.from_np(a.dtype), kind="ExternalInput").ap() for k, a in arrays.items()]
    args.append(nc.dram_tensor("out_0", (P, KC, T), F32, kind="ExternalOutput").ap())
    build(nc, *args)
    r = run_bass_kernel_spmd(nc, [arrays], core_ids=[0])
    got = r.results[0]["out_0"]
    return np.ascontiguousarray(got.transpose(2, 1, 0).reshape(1, T, KC * P))
```
